# Optimizing a Trainium2 kernel written in Bass

```python
import math
import numpy as np
import jax, jax.numpy as jnp
from jax import lax

D_MODEL = 1024
BATCH = 1
SEQ = 256
DEPTH = 2

GRID_W = 64
MEM_LEN = 256
HEAD_DIM = 64
DA_HEADS = 4
DA_VDIM = 2 * HEAD_DIM
DA_QK = DA_HEADS * 2 * HEAD_DIM
DA_V = DA_HEADS * DA_VDIM
Q_BLOCK = 128
NA_HEADS = 8
NA_W = NA_HEADS * HEAD_DIM
NA_WIN_ROWS = 8
NA_WIN_COLS = 16
NA_QCOLS = 16
NA_KCOLS = 32
SC_W = 512
SC_K = 3
N_BRANCH = 3
BRANCH_W = 512
IN_SPLITS = (DA_QK, DA_QK, DA_V, NA_W, NA_W, NA_W, SC_W, SC_W, SC_W, N_BRANCH * D_MODEL)
IN_COLS = 7680
XA_HEADS = 4
XA_DIM = D_MODEL // XA_HEADS
D_FF = 2816
FFN_K = 3
ROPE_THETA = 10000.0
LN_EPS = 1e-5


def layer_norm(x, g, b):
    xf = x.astype(jnp.float32)
    mu = jnp.mean(xf, axis=-1, keepdims=True)
    var = jnp.mean(jnp.square(xf - mu), axis=-1, keepdims=True)
    y = (xf - mu) * lax.rsqrt(var + LN_EPS)
    return (y * g.astype(jnp.float32) + b.astype(jnp.float32)).astype(x.dtype)

def rms_norm(x, g):
    xf = x.astype(jnp.float32)
    y = xf * lax.rsqrt(jnp.mean(jnp.square(xf), axis=-1, keepdims=True) + LN_EPS)
    return (y * g.astype(jnp.float32)).astype(x.dtype)

def rope(x, pos):
    d = x.shape[-1]
    half = d // 2
    inv = ROPE_THETA ** (-jnp.arange(half, dtype=jnp.float32) * 2.0 / d)
    ang = pos.astype(jnp.float32)[:, None] * inv[None, :]
    cos = jnp.cos(ang).astype(x.dtype)
    sin = jnp.sin(ang).astype(x.dtype)
    x1, x2 = x[..., :half], x[..., half:]
    return jnp.concatenate([x1 * cos - x2 * sin, x2 * cos + x1 * sin], axis=-1)

def dwconv(x, w):
    k, c = w.shape
    return lax.conv_general_dilated(x, w[:, None, :], window_strides=(1,), padding=[(k // 2, k // 2)],
                                    dimension_numbers=('NWC', 'WIO', 'NWC'), feature_group_count=c)

def diff_attention(q, k, v, lam, pos):
    b, s = q.shape[0], q.shape[1]
    q = rope(q.transpose(0, 2, 3, 1, 4), pos) * (HEAD_DIM ** -0.5)
    k = rope(k.transpose(0, 2, 3, 1, 4), pos)
    vt = v.transpose(0, 2, 1, 3)
    nb = s // Q_BLOCK
    qb = q.reshape(b, DA_HEADS, 2, nb, Q_BLOCK, HEAD_DIM).transpose(3, 0, 1, 2, 4, 5)

    def block(qblk):
        sc = jnp.einsum('bhmqd,bhmkd->bhmqk', qblk, k, preferred_element_type=jnp.float32)
        p = jax.nn.softmax(sc, axis=-1)
        w = p[:, :, 0] - lam * p[:, :, 1]
        return jnp.einsum('bhqk,bhkv->bhqv', w.astype(vt.dtype), vt)

    o = lax.map(block, qb)
    return o.transpose(1, 2, 0, 3, 4).reshape(b, DA_HEADS, s, DA_VDIM)

def _na_static(rows):
    wr = min(NA_WIN_ROWS, rows)
    n_cb = GRID_W // NA_QCOLS
    c = np.arange(GRID_W).reshape(n_cb, NA_QCOLS)
    cs = np.clip(c - NA_WIN_COLS // 2, 0, GRID_W - NA_WIN_COLS)
    kstart = np.minimum(cs[:, 0], GRID_W - NA_KCOLS)
    kcol = kstart[:, None] + np.arange(NA_KCOLS)
    rel = kcol[:, None, :] - c[:, :, None]
    valid = (kcol[:, None, :] >= cs[:, :, None]) & (kcol[:, None, :] < cs[:, :, None] + NA_WIN_COLS)
    dc_idx = np.clip(rel + NA_WIN_COLS - 1, 0, 2 * NA_WIN_COLS - 2)
    return wr, n_cb, kcol.astype(np.int32), dc_idx.astype(np.int32), valid

def neighbourhood_attention(q, k, v, rpb):
    b, s = q.shape[0], q.shape[1]
    rows = s // GRID_W
    wr, n_cb, kcol, dc_idx, valid = _na_static(rows)

    def grid(t):
        return t.reshape(b, rows, GRID_W, NA_HEADS, HEAD_DIM).transpose(0, 3, 1, 2, 4)

    qg = grid(q) * (HEAD_DIM ** -0.5)
    kg = grid(k)
    vg = grid(v)
    qr = qg.reshape(b, NA_HEADS, rows, n_cb, NA_QCOLS, HEAD_DIM).transpose(2, 0, 1, 3, 4, 5)
    kcol_j = jnp.asarray(kcol)
    mask = jnp.asarray(valid)[:, :, None, :]
    bias_c = rpb[:, :, jnp.asarray(dc_idx)]

    def row_block(args):
        r, qblk = args
        rs = jnp.clip(r - wr // 2, 0, rows - wr)
        k_rows = lax.dynamic_slice_in_dim(kg, rs, wr, axis=2)
        v_rows = lax.dynamic_slice_in_dim(vg, rs, wr, axis=2)
        k_blk = jnp.take(k_rows, kcol_j, axis=3)
        v_blk = jnp.take(v_rows, kcol_j, axis=3)
        sc = jnp.einsum('bhjqd,bhrjkd->bhjqrk', qblk, k_blk, preferred_element_type=jnp.float32)
        dr_idx = rs + jnp.arange(wr) - r + (NA_WIN_ROWS - 1)
        bias = jnp.take(bias_c, dr_idx, axis=1).transpose(0, 2, 3, 1, 4)
        sc = jnp.where(mask, sc + bias[None].astype(jnp.float32), -jnp.inf)
        p = jax.nn.softmax(sc.reshape(sc.shape[:4] + (wr * NA_KCOLS,)), axis=-1).reshape(sc.shape)
        return jnp.einsum('bhjqrk,bhrjkd->bhjqd', p.astype(v_blk.dtype), v_blk)

    o = lax.map(row_block, (jnp.arange(rows, dtype=jnp.int32), qr))
    return o.transpose(1, 0, 3, 4, 2, 5).reshape(b, s, NA_W)

def hybrid_mixer(x, w_in, lam_q1, lam_k1, lam_q2, lam_k2, subln_g, rpb, sc_conv_w, w_branch, w_mix_out, lam_init, pos):
    b, s, _ = x.shape
    proj = x @ w_in
    qa, ka, va, qb, kb, vb, gb, gc, hc, gates = jnp.split(proj, np.cumsum(IN_SPLITS)[:-1].tolist(), axis=-1)
    lam = (jnp.exp(jnp.sum(lam_q1.astype(jnp.float32) * lam_k1.astype(jnp.float32)))
           - jnp.exp(jnp.sum(lam_q2.astype(jnp.float32) * lam_k2.astype(jnp.float32))) + lam_init)
    oa = diff_attention(qa.reshape(b, s, DA_HEADS, 2, HEAD_DIM), ka.reshape(b, s, DA_HEADS, 2, HEAD_DIM),
                        va.reshape(b, s, DA_HEADS, DA_VDIM), lam, pos)
    ya = (rms_norm(oa, subln_g) * (1.0 - lam_init)).transpose(0, 2, 1, 3).reshape(b, s, DA_V)
    yb = neighbourhood_attention(qb, kb, vb, rpb)
    yc = gb * dwconv(gc * hc, sc_conv_w)
    g = jax.nn.sigmoid(gates.reshape(b, s, N_BRANCH, D_MODEL))
    merged = (g[:, :, 0] * (ya @ w_branch[0]) + g[:, :, 1] * (yb @ w_branch[1])
              + g[:, :, 2] * (yc @ w_branch[2]))
    return merged @ w_mix_out

def memory_cross_attention(x, mem, xa_q, xa_kv, xa_o):
    b, s, _ = x.shape
    q = (x @ xa_q).reshape(b, s, XA_HEADS, XA_DIM) * (XA_DIM ** -0.5)
    k, v = jnp.split(mem @ xa_kv, 2, axis=-1)
    k = k.reshape(b, mem.shape[1], XA_HEADS, XA_DIM)
    v = v.reshape(b, mem.shape[1], XA_HEADS, XA_DIM)
    p = jax.nn.softmax(jnp.einsum('bqhd,bkhd->bhqk', q, k, preferred_element_type=jnp.float32), axis=-1)
    o = jnp.einsum('bhqk,bkhd->bqhd', p.astype(v.dtype), v).reshape(b, s, D_MODEL)
    return o @ xa_o

def conv_ffn(x, ffn_w_in, ffn_conv_w, ffn_conv_b, ffn_w_out):
    u, gt = jnp.split(x @ ffn_w_in, 2, axis=-1)
    a = dwconv(gt, ffn_conv_w) + ffn_conv_b
    return (jax.nn.silu(a) * u) @ ffn_w_out

def first_inputs(seed: int = 0) -> dict:
    key = jax.random.key(seed)
    ks = jax.random.split(key, 24)
    beta = (8.0 * DEPTH) ** -0.25

    def nrm(k, shape, scale):
        return jax.random.normal(k, shape, jnp.float32) * scale

    is_value = (False, False, True, False, False, True, False, False, True, False)
    col_scale = np.concatenate([np.full(n, beta if iv else 1.0, np.float32) for n, iv in zip(IN_SPLITS, is_value)])
    kv_scale = np.concatenate([np.ones(D_MODEL, np.float32), np.full(D_MODEL, beta, np.float32)])
    return {
        'x': nrm(ks[0], (BATCH, SEQ, D_MODEL), 1.0),
        'mem': nrm(ks[1], (BATCH, MEM_LEN, D_MODEL), 1.0),
        'emb_ln_g': 1.0 + nrm(ks[2], (D_MODEL,), 0.02),
        'emb_ln_b': nrm(ks[3], (D_MODEL,), 0.02),
        'w_in': nrm(ks[4], (DEPTH, D_MODEL, IN_COLS), D_MODEL ** -0.5) * jnp.asarray(col_scale),
        'lam_q1': nrm(ks[5], (DEPTH, HEAD_DIM), 0.1),
        'lam_k1': nrm(ks[6], (DEPTH, HEAD_DIM), 0.1),
        'lam_q2': nrm(ks[7], (DEPTH, HEAD_DIM), 0.1),
        'lam_k2': nrm(ks[8], (DEPTH, HEAD_DIM), 0.1),
        'subln_g': 1.0 + nrm(ks[9], (DEPTH, DA_VDIM), 0.02),
        'rpb': nrm(ks[10], (DEPTH, NA_HEADS, 2 * NA_WIN_ROWS - 1, 2 * NA_WIN_COLS - 1), 0.1),
        'sc_conv_w': nrm(ks[11], (DEPTH, SC_K, SC_W), SC_K ** -0.5),
        'w_branch': nrm(ks[12], (DEPTH, N_BRANCH, BRANCH_W, D_MODEL), BRANCH_W ** -0.5 * beta),
        'w_mix_out': nrm(ks[13], (DEPTH, D_MODEL, D_MODEL), D_MODEL ** -0.5 * beta),
        'xa_q': nrm(ks[14], (DEPTH, D_MODEL, D_MODEL), D_MODEL ** -0.5),
        'xa_kv': nrm(ks[15], (DEPTH, D_MODEL, 2 * D_MODEL), D_MODEL ** -0.5) * jnp.asarray(kv_scale),
        'xa_o': nrm(ks[16], (DEPTH, D_MODEL, D_MODEL), D_MODEL ** -0.5 * beta),
        'ffn_w_in': nrm(ks[17], (DEPTH, D_MODEL, 2 * D_FF), D_MODEL ** -0.5 * beta),
        'ffn_conv_w': nrm(ks[18], (DEPTH, FFN_K, D_FF), FFN_K ** -0.5),
        'ffn_conv_b': nrm(ks[19], (DEPTH, D_FF), 0.02),
        'ffn_w_out': nrm(ks[20], (DEPTH, D_FF, D_MODEL), D_FF ** -0.5 * beta),
        'ln_g': 1.0 + nrm(ks[21], (DEPTH, 3, D_MODEL), 0.02),
        'ln_b': nrm(ks[22], (DEPTH, 3, D_MODEL), 0.02),
    }

def first_block(x, mem, emb_ln_g, emb_ln_b, w_in, lam_q1, lam_k1, lam_q2, lam_k2, subln_g, rpb, sc_conv_w,
              w_branch, w_mix_out, xa_q, xa_kv, xa_o, ffn_w_in, ffn_conv_w, ffn_conv_b, ffn_w_out, ln_g, ln_b):
    alpha = (2.0 * DEPTH) ** 0.25
    pos = jnp.arange(x.shape[1], dtype=jnp.int32)
    x = layer_norm(x, emb_ln_g, emb_ln_b)
    for l in range(DEPTH):
        lam_init = 0.8 - 0.6 * math.exp(-0.3 * l)
        h = hybrid_mixer(x, w_in[l], lam_q1[l], lam_k1[l], lam_q2[l], lam_k2[l], subln_g[l], rpb[l],
                         sc_conv_w[l], w_branch[l], w_mix_out[l], lam_init, pos)
        x = layer_norm(alpha * x + h, ln_g[l, 0], ln_b[l, 0])
        h = memory_cross_attention(x, mem, xa_q[l], xa_kv[l], xa_o[l])
        x = layer_norm(alpha * x + h, ln_g[l, 1], ln_b[l, 1])
        h = conv_ffn(x, ffn_w_in[l], ffn_conv_w[l], ffn_conv_b[l], ffn_w_out[l])
        x = layer_norm(alpha * x + h, ln_g[l, 2], ln_b[l, 2])
    return x


D_MIX = D_MODEL
GLA_HEADS = 4
GLA_DK = 64
GLA_DV = 128
GLA_QK = GLA_HEADS * GLA_DK
GLA_WIDTH = GLA_HEADS * GLA_DV
GLA_LOWRANK = 16
GLA_TAU = 16.0
GLA_CHUNK = 64
SSD_HEADS = 8
SSD_HEADDIM = 64
SSD_WIDTH = SSD_HEADS * SSD_HEADDIM
SSD_GROUPS = 2
SSD_STATE = 64
SSD_BC = SSD_GROUPS * SSD_STATE
SSD_CONV = 4
SSD_CONV_DIM = SSD_WIDTH + 2 * SSD_BC
SSD_CHUNK = 128
D_FF_2 = 3584
N_EXPERTS = 8
TOP_K = 2
EPS = 1e-6

IN_SIZES = (GLA_QK, GLA_QK, GLA_WIDTH, GLA_WIDTH, GLA_LOWRANK,
            SSD_WIDTH, SSD_WIDTH, SSD_BC, SSD_BC, SSD_HEADS)
IN_SPLITS_2 = [int(s) for s in np.cumsum(IN_SIZES)[:-1]]
D_IN_PROJ = int(sum(IN_SIZES))


def rmsnorm(x, w):
    x32 = x.astype(jnp.float32)
    r = x32 * lax.rsqrt(jnp.mean(x32 * x32, axis=-1, keepdims=True) + EPS)
    return (r * w.astype(jnp.float32)).astype(x.dtype)

def inter_chunk_states(decay, contrib):
    d = jnp.moveaxis(decay, 1, 0)
    u = jnp.moveaxis(contrib, 1, 0)

    def step(s, inp):
        dn, un = inp
        return dn * s + un, s

    _, prev = lax.scan(step, jnp.zeros_like(u[0]), (d, u))
    return jnp.moveaxis(prev, 0, 1)

def gla_chunked(q, k, v, log_a):
    bsz, seq, nh, dk = q.shape
    dv = v.shape[-1]
    nc = seq // GLA_CHUNK
    shp = lambda t: t.astype(jnp.float32).reshape(bsz, nc, GLA_CHUNK, nh, t.shape[-1])
    q, k, v, log_a = shp(q) * (dk ** -0.5), shp(k), shp(v), shp(log_a)
    b = jnp.cumsum(log_a, axis=2)
    qe = q * jnp.exp(b)
    ke = k * jnp.exp(-b)
    causal = jnp.tril(jnp.ones((GLA_CHUNK, GLA_CHUNK), bool))
    att = jnp.einsum('bnihd,bnjhd->bnhij', qe, ke)
    att = jnp.where(causal, att, 0.0)
    o_intra = jnp.einsum('bnhij,bnjhv->bnihv', att, v)
    b_last = b[:, :, -1]
    k_tail = k * jnp.exp(b_last[:, :, None] - b)
    contrib = jnp.einsum('bnjhd,bnjhv->bnhdv', k_tail, v)
    s_prev = inter_chunk_states(jnp.exp(b_last)[..., None], contrib)
    o_inter = jnp.einsum('bnihd,bnhdv->bnihv', qe, s_prev)
    return (o_intra + o_inter).reshape(bsz, seq, nh, dv)

def ssd_chunked(xh, dt, a, bm, cm):
    bsz, seq, nh, p = xh.shape
    rep = nh // bm.shape[2]
    nc = seq // SSD_CHUNK
    f = lambda t: t.astype(jnp.float32).reshape((bsz, nc, SSD_CHUNK) + t.shape[2:])
    xh, dt = f(xh), f(dt)
    bh = f(jnp.repeat(bm, rep, axis=2))
    ch = f(jnp.repeat(cm, rep, axis=2))
    cum = jnp.cumsum(dt * a, axis=2)
    causal = jnp.tril(jnp.ones((SSD_CHUNK, SSD_CHUNK), bool))[:, :, None]
    seg = cum[:, :, :, None, :] - cum[:, :, None, :, :]
    decay = jnp.exp(jnp.where(causal, seg, -jnp.inf))
    xdt = xh * dt[..., None]
    scores = jnp.einsum('bnihs,bnjhs->bnijh', ch, bh) * decay
    y_intra = jnp.einsum('bnijh,bnjhp->bnihp', scores, xdt)
    cum_last = cum[:, :, -1]
    contrib = jnp.einsum('bnjhs,bnjhp->bnhps',
                         bh * jnp.exp(cum_last[:, :, None] - cum)[..., None], xdt)
    s_prev = inter_chunk_states(jnp.exp(cum_last)[..., None, None], contrib)
    y_inter = jnp.einsum('bnihs,bnhps->bnihp', ch * jnp.exp(cum)[..., None], s_prev)
    return (y_intra + y_inter).reshape(bsz, seq, nh, p)

def causal_depthwise_conv(u, w, b):
    kw, cdim = w.shape
    out = lax.conv_general_dilated(u, w.astype(u.dtype)[:, None, :], window_strides=(1,),
                                   padding=[(kw - 1, 0)],
                                   dimension_numbers=('NWC', 'WIO', 'NWC'),
                                   feature_group_count=cdim)
    return out + b.astype(u.dtype)

def hybrid_mixer_2(h, w_in, gla_a_w, gla_a_b, gla_norm_w, conv_w, conv_b,
                 dt_bias, a_log, d_skip, ssd_norm_w, w_out):
    bsz, seq, _ = h.shape
    proj = h @ w_in
    q, k, v, g, alr, z, xs, bm, cm, dt = jnp.split(proj, IN_SPLITS_2, axis=-1)
    log_a = jax.nn.log_sigmoid((alr @ gla_a_w + gla_a_b).astype(jnp.float32)) / GLA_TAU
    o = gla_chunked(q.reshape(bsz, seq, GLA_HEADS, GLA_DK),
                    k.reshape(bsz, seq, GLA_HEADS, GLA_DK),
                    v.reshape(bsz, seq, GLA_HEADS, GLA_DV),
                    log_a.reshape(bsz, seq, GLA_HEADS, GLA_DK))
    o = rmsnorm(o, gla_norm_w) * jax.nn.silu(g.astype(jnp.float32).reshape(bsz, seq, GLA_HEADS, GLA_DV))
    o = o.reshape(bsz, seq, GLA_WIDTH)
    xbc = jax.nn.silu(causal_depthwise_conv(jnp.concatenate([xs, bm, cm], axis=-1), conv_w, conv_b))
    xs, bm, cm = jnp.split(xbc, [SSD_WIDTH, SSD_WIDTH + SSD_BC], axis=-1)
    dt = jax.nn.softplus(dt.astype(jnp.float32) + dt_bias.astype(jnp.float32))
    a = -jnp.exp(a_log.astype(jnp.float32))
    xh = xs.reshape(bsz, seq, SSD_HEADS, SSD_HEADDIM)
    y = ssd_chunked(xh, dt, a,
                    bm.reshape(bsz, seq, SSD_GROUPS, SSD_STATE),
                    cm.reshape(bsz, seq, SSD_GROUPS, SSD_STATE))
    y = y + d_skip.astype(jnp.float32)[:, None] * xh.astype(jnp.float32)
    y = y.reshape(bsz, seq, SSD_WIDTH) * jax.nn.silu(z.astype(jnp.float32))
    y = rmsnorm(y, ssd_norm_w)
    merged = jnp.concatenate([o, y], axis=-1).astype(h.dtype)
    return merged @ w_out

def swiglu(t, w_gate, w_up, w_down):
    return (jax.nn.silu(t @ w_gate) * (t @ w_up)) @ w_down

def moe_swiglu(h, router_w, w_gate, w_up, w_down):
    bsz, seq, d = h.shape
    t = h.reshape(bsz * seq, d)
    logits = (t @ router_w).astype(jnp.float32)
    top_v, top_i = lax.top_k(logits, TOP_K)
    top_p = jax.nn.softmax(top_v, axis=-1)
    gates = jnp.sum(jax.nn.one_hot(top_i, N_EXPERTS, dtype=jnp.float32) * top_p[..., None], axis=1)
    gates = gates.astype(h.dtype)
    out = jnp.zeros_like(t)
    for e in range(N_EXPERTS):
        out = out + gates[:, e:e + 1] * swiglu(t, w_gate[e], w_up[e], w_down[e])
    return out.reshape(bsz, seq, d)

def second_inputs(seed: int = 0) -> dict:
    key = jax.random.key(seed)
    ks = iter(list(jax.random.split(key, 40)))
    f32 = jnp.float32
    nrm = lambda shape, scale: jax.random.normal(next(ks), shape, f32) * scale
    n_dense = (DEPTH + 1) // 2
    n_moe = DEPTH // 2
    d = D_MODEL
    x = nrm((BATCH, SEQ, d), 1.0)
    c = nrm((BATCH, d), 1.0)
    ada_w = nrm((DEPTH, d, 6 * d), 0.5 * d ** -0.5)
    ada_b = nrm((DEPTH, 6 * d), 0.02)
    norm1_w = 1.0 + nrm((DEPTH, d), 0.02)
    w_in = nrm((DEPTH, d, D_IN_PROJ), d ** -0.5)
    gla_a_w = nrm((DEPTH, GLA_LOWRANK, GLA_QK), GLA_LOWRANK ** -0.5)
    gla_a_b = nrm((DEPTH, GLA_QK), 0.1)
    gla_norm_w = 1.0 + nrm((DEPTH, GLA_DV), 0.02)
    conv_w = nrm((DEPTH, SSD_CONV, SSD_CONV_DIM), SSD_CONV ** -0.5)
    conv_b = nrm((DEPTH, SSD_CONV_DIM), 0.02)
    dt0 = jnp.exp(jax.random.uniform(next(ks), (DEPTH, SSD_HEADS), f32,
                                     np.log(1e-3).astype(np.float32), np.log(1e-1).astype(np.float32)))
    dt_bias = dt0 + jnp.log(-jnp.expm1(-dt0))
    a_log = jnp.log(jax.random.uniform(next(ks), (DEPTH, SSD_HEADS), f32, 1.0, 16.0))
    d_skip = 1.0 + nrm((DEPTH, SSD_HEADS), 0.1)
    ssd_norm_w = 1.0 + nrm((DEPTH, SSD_WIDTH), 0.02)
    w_out = nrm((DEPTH, D_MIX, d), D_MIX ** -0.5)
    norm2_w = 1.0 + nrm((DEPTH, d), 0.02)
    ffn_w_gate = nrm((n_dense, d, D_FF_2), d ** -0.5)
    ffn_w_up = nrm((n_dense, d, D_FF_2), d ** -0.5)
    ffn_w_down = nrm((n_dense, D_FF_2, d), D_FF_2 ** -0.5)
    router_w = nrm((n_moe, d, N_EXPERTS), d ** -0.5)
    moe_w_gate = nrm((n_moe, N_EXPERTS, d, D_FF_2), d ** -0.5)
    moe_w_up = nrm((n_moe, N_EXPERTS, d, D_FF_2), d ** -0.5)
    moe_w_down = nrm((n_moe, N_EXPERTS, D_FF_2, d), D_FF_2 ** -0.5)
    final_norm_w = 1.0 + nrm((d,), 0.02)
    return {"x": x, "c": c, "ada_w": ada_w, "ada_b": ada_b, "norm1_w": norm1_w,
            "w_in": w_in, "gla_a_w": gla_a_w, "gla_a_b": gla_a_b, "gla_norm_w": gla_norm_w,
            "conv_w": conv_w, "conv_b": conv_b, "dt_bias": dt_bias, "a_log": a_log,
            "d_skip": d_skip, "ssd_norm_w": ssd_norm_w, "w_out": w_out, "norm2_w": norm2_w,
            "ffn_w_gate": ffn_w_gate, "ffn_w_up": ffn_w_up, "ffn_w_down": ffn_w_down,
            "router_w": router_w, "moe_w_gate": moe_w_gate, "moe_w_up": moe_w_up,
            "moe_w_down": moe_w_down, "final_norm_w": final_norm_w}

def second_block(x, c, ada_w, ada_b, norm1_w, w_in, gla_a_w, gla_a_b, gla_norm_w,
              conv_w, conv_b, dt_bias, a_log, d_skip, ssd_norm_w, w_out, norm2_w,
              ffn_w_gate, ffn_w_up, ffn_w_down, router_w, moe_w_gate, moe_w_up,
              moe_w_down, final_norm_w):
    s = jax.nn.silu(c)
    for l in range(DEPTH):
        mod = s @ ada_w[l] + ada_b[l]
        sh1, sc1, g1, sh2, sc2, g2 = [m[:, None, :] for m in jnp.split(mod, 6, axis=-1)]
        h = rmsnorm(x, norm1_w[l]) * (1.0 + sc1) + sh1
        mix = hybrid_mixer_2(h, w_in[l], gla_a_w[l], gla_a_b[l], gla_norm_w[l], conv_w[l],
                           conv_b[l], dt_bias[l], a_log[l], d_skip[l], ssd_norm_w[l], w_out[l])
        x = x + g1 * mix
        h = rmsnorm(x, norm2_w[l]) * (1.0 + sc2) + sh2
        if l % 2 == 0:
            i = l // 2
            ff = swiglu(h, ffn_w_gate[i], ffn_w_up[i], ffn_w_down[i])
        else:
            i = l // 2
            ff = moe_swiglu(h, router_w[i], moe_w_gate[i], moe_w_up[i], moe_w_down[i])
        x = x + g2 * ff
    return rmsnorm(x, final_norm_w)


def setup_inputs(seed=0):
    out = dict(first_inputs(seed))
    for name, value in second_inputs(seed + 1).items():
        if name != "x":
            out[name + "_2"] = value
    return out


def reference(
    x, mem, emb_ln_g, emb_ln_b, w_in, lam_q1, lam_k1, lam_q2, lam_k2, subln_g, rpb, sc_conv_w,
    w_branch, w_mix_out, xa_q, xa_kv, xa_o, ffn_w_in, ffn_conv_w, ffn_conv_b, ffn_w_out, ln_g,
    ln_b, c_2, ada_w_2, ada_b_2, norm1_w_2, w_in_2, gla_a_w_2, gla_a_b_2, gla_norm_w_2,
    conv_w_2, conv_b_2, dt_bias_2, a_log_2, d_skip_2, ssd_norm_w_2, w_out_2, norm2_w_2,
    ffn_w_gate_2, ffn_w_up_2, ffn_w_down_2, router_w_2, moe_w_gate_2, moe_w_up_2, moe_w_down_2,
    final_norm_w_2,
):
    x = first_block(
        x, mem, emb_ln_g, emb_ln_b, w_in, lam_q1, lam_k1, lam_q2, lam_k2, subln_g, rpb,
        sc_conv_w, w_branch, w_mix_out, xa_q, xa_kv, xa_o, ffn_w_in, ffn_conv_w, ffn_conv_b,
        ffn_w_out, ln_g, ln_b,
    )
    return second_block(
        x, c_2, ada_w_2, ada_b_2, norm1_w_2, w_in_2, gla_a_w_2, gla_a_b_2, gla_norm_w_2,
        conv_w_2, conv_b_2, dt_bias_2, a_log_2, d_skip_2, ssd_norm_w_2, w_out_2, norm2_w_2,
        ffn_w_gate_2, ffn_w_up_2, ffn_w_down_2, router_w_2, moe_w_gate_2, moe_w_up_2,
        moe_w_down_2, final_norm_w_2,
    )


_drawn_inputs = setup_inputs


def setup_inputs(seed=0):
    import zlib

    import numpy as np

    out = dict(_drawn_inputs(seed))
    spreads = {}
    factors = {'lam_q1': 3.766,
     'lam_q2': 4.191,
     'lam_k2': 5.825,
     'subln_g': 8.0,
     'rpb': 8.0,
     'ffn_conv_b': 7.385,
     'norm1_w_2': 3.745,
     'gla_a_b_2': 5.076,
     'gla_norm_w_2': 8.0,
     'conv_b_2': 6.269,
     'ssd_norm_w_2': 26.762,
     'norm2_w_2': 3.473,
     'final_norm_w_2': 23.072,
     'd_skip_2': 30.057}
    for name, (base, spread) in spreads.items():
        noise = np.random.default_rng([zlib.crc32(name.encode()), seed]).standard_normal(out[name].shape)
        drawn = base * np.exp(spread * noise) if base else spread * noise
        out[name] = __import__('jax').numpy.asarray(drawn.astype(out[name].dtype))
    for name, factor in factors.items():
        out[name] = (out[name] * factor).astype(out[name].dtype)
    return out
```

```python
import math
from contextlib import ExitStack, contextmanager

import numpy as np

import concourse.bass as bass
from concourse import mybir

F32 = mybir.dt.float32
ALU = mybir.AluOpType
ACT = mybir.ActivationFunctionType
AX = mybir.AxisListType

P = 128
TOK = 256
D = 1024
KD = D // P
DEPTH = 2
ALPHA = (2.0 * DEPTH) ** 0.25
SLOTS = 9
CH = 2048
CW = CH // KD
FF1, FF2 = 2816, 3584
EXPERTS = 8
NEG = -1.0e30


class Follow:

    def __init__(self, eng, own, given=()):
        self.eng, self.own, self.last = eng, own, own
        self.base, self.here, self.followed = {}, {s.name: 1 for s in given}, set()

    def now(self, sem):
        return self.base.get(sem.name, 0) + self.here.get(sem.name, 0)

    def bump(self, sem, by=1):
        self.followed.add(sem.name)
        self.here[sem.name] = self.here.get(sem.name, 0) + by

    def next(self, sem, by=1):
        self.bump(sem, by)
        return self.now(sem)

    def count(self, sem):
        self.last = sem if sem is not None else self.own
        self.bump(self.last)
        return self.last

    @contextmanager
    def trips(self, n, per):
        with self.eng.Fori(0, n) as i:
            base, here = self.base, self.here
            names = set(per) | set(base) | set(here)
            start = {s: base.get(s, 0) + here.get(s, 0) for s in names}
            self.base = {s: start[s] + i * per[s] if per.get(s) else start[s] for s in names}
            self.here = {}
            yield i
            wrong = {s: self.here.get(s, 0) for s in set(self.here) | set(per)
                     if s in self.followed and per.get(s, 0) != self.here.get(s, 0)}
            if wrong:
                BAD.append((per, wrong))
        self.base, self.here = base, {s: here.get(s, 0) + n * per.get(s, 0) for s in set(per) | set(here)}


C_ID, C_ROT, C_COS, C_SIN, C_TRI, C_BAN, C_DIAG, C_WIN, C_HALF, C_EPS1, C_EPS2, C_ONE, C_IOTA = (
    0, 128, 256, 512, 768, 896, 1024, 1152, 1216, 1218, 1219, 1220, 1221)
C_ALL = C_IOTA + P
A_LNG, A_LNB, A_SUB, A_SCW, A_FF, A_LAM0, A_LAM1, A_LAMV = 0, 24, 48, 49, 61, 149, 150, 151
A_ALL = A_LAMV + 256
B_N1, B_N2, B_ADA, B_AB, B_GN, B_CW, B_CB, B_DTB, B_ALOG, B_DS, B_SN = 0, 8, 16, 64, 66, 67, 91, 97, 105, 113, 117
B_ALL = B_SN + 4

LAYER1 = {
    "act_ready0": 6, "act_ready1": 5, "bank_free0": 24, "bank_free1": 24, "bank_free2": 31, "bank_free3": 31,
    "bank_free4": 11, "bank_free5": 11, "bank_free6": 6, "bank_free7": 6, "bank_full0": 24, "bank_full1": 24,
    "bank_full2": 31, "bank_full3": 31, "bank_full4": 11, "bank_full5": 11, "bank_full6": 6, "bank_full7": 6,
    "bias_in": 256, "centred": 3, "conv_ready0": 6, "conv_ready1": 5, "exp_ready": 20, "ffn_summed": 1, "gate_full0": 6,
    "gate_full1": 5, "gates_ready": 1, "heads_ready": 1, "lam_dot": 1, "lam_exp": 1, "mean_ready": 3, "merged_ready": 1,
    "mixer_in": 1, "par_in": 16, "peak_ready": 20, "probs_ready": 20, "silu_ready0": 6, "silu_ready1": 5,
    "squares_ready": 3, "std_ready": 3, "sub_squares": 1, "sub_std": 1, "up_full0": 6, "up_full1": 5, "var_ready": 3,
    "vector_step": 157, "w_loaded0": 256, "w_loaded1": 256, "w_loaded2": 256, "w_loaded3": 240, "w_loaded4": 240,
    "w_loaded5": 224, "w_loaded6": 144, "w_loaded7": 144, "w_loaded8": 144, "w_used0": 16, "w_used1": 16, "w_used2": 16,
    "w_used3": 15, "w_used4": 15, "w_used5": 14, "w_used6": 9, "w_used7": 9, "w_used8": 9, "x_ready": 3, "y_ready": 1,}
FFN1_TRIP = {
    "act_ready0": 1, "act_ready1": 1, "conv_ready0": 1, "conv_ready1": 1, "gate_full0": 1, "gate_full1": 1,
    "silu_ready0": 1, "silu_ready1": 1, "up_full0": 1, "up_full1": 1, "vector_step": 12, "w_loaded0": 16, "w_loaded1": 16,
    "w_loaded2": 16, "w_loaded3": 16, "w_loaded4": 16, "w_loaded5": 16, "w_used0": 1, "w_used1": 1, "w_used2": 1,
    "w_used3": 1, "w_used4": 1, "w_used5": 1,}
FFN2_TRIP = {
    "act_ready0": 1, "act_ready1": 1, "gate_full0": 1, "gate_full1": 1, "silu_ready0": 1, "silu_ready1": 1, "up_full0": 1,
    "up_full1": 1, "w_loaded0": 16, "w_loaded1": 16, "w_loaded2": 16, "w_loaded3": 16, "w_loaded4": 16, "w_loaded5": 16,
    "w_used0": 1, "w_used1": 1, "w_used2": 1, "w_used3": 1, "w_used4": 1, "w_used5": 1,}
FFN3_TRIP = {
    "act_ready0": 1, "act_ready1": 1, "gate_full0": 1, "gate_full1": 1, "silu_ready0": 1, "silu_ready1": 1, "up_full0": 1,
    "up_full1": 1, "w_loaded0": 16, "w_loaded1": 16, "w_loaded2": 16, "w_loaded3": 16, "w_loaded4": 16, "w_loaded5": 16,
    "w_used0": 1, "w_used1": 1, "w_used2": 1, "w_used3": 1, "w_used4": 1, "w_used5": 1,}
EXPERT = {
    "act_ready0": 7, "act_ready1": 7, "back_free": 1, "back_full": 1, "bank_free4": 1, "bank_free5": 1, "bank_free6": 1,
    "bank_free7": 1, "bank_full4": 1, "bank_full5": 1, "bank_full6": 1, "bank_full7": 1, "gate_full0": 7, "gate_full1": 7,
    "result_free": 4, "result_full": 4, "select_ready": 1, "silu_ready0": 7, "silu_ready1": 7, "up_full0": 7,
    "up_full1": 7, "vector_step": 8, "w_loaded0": 112, "w_loaded1": 112, "w_loaded2": 112, "w_loaded3": 112,
    "w_loaded4": 112, "w_loaded5": 112, "w_used0": 7, "w_used1": 7, "w_used2": 7, "w_used3": 7, "w_used4": 7, "w_used5": 7,}
BAD = []


def program(nc, io):
    w_in, w_branch, w_mix, xa_q, xa_kv, xa_o, ffn_in, ffn_out = (
        io[n] for n in ("w_in", "w_branch", "w_mix_out", "xa_q", "xa_kv", "xa_o", "ffn_w_in", "ffn_w_out"))

    with ExitStack() as ctx:
        def sb(name, *shape, dt=F32):
            return ctx.enter_context(nc.sbuf_tensor(name, [P, *shape], dt))

        def sem(name):
            return ctx.enter_context(nc.semaphore(name))

        def tiles(ap, k):
            return ap.rearrange("p (k t) -> p k t", k=k)

        def spread(ap, k):
            return ap.rearrange("p (o t) -> p o t", o=1).broadcast_to([P, k, ap.shape[1]])

        ring = sb("ring", SLOTS, CH)
        xT = sb("xT", KD, TOK)
        work = sb("work", 2 * CH)
        yT = tiles(work[:, 0:CH], KD)
        merged = tiles(work[:, CH:2 * CH], KD)
        bias = work[:, 0:3072].rearrange("p (h j c) -> p h j c", h=8, j=6)
        memT = sb("memT", KD, TOK)
        qa, ka, qb, kb, gb, gc, hc = (sb(n, 4, TOK) for n in ("qa", "ka", "qb", "kb", "gb", "gc", "hc"))
        va, vb = (sb(n, 2, 512) for n in ("va", "vb"))
        qhalf = [[sb(f"qhalf{a}{m}", 4, TOK) for m in range(2)] for a in range(2)]
        gates = sb("gates", 24, TOK)
        flat = gates[:, :, :].rearrange("p n t -> p (n t)")
        squares = tiles(flat[:, 0:CH], KD)
        conva, silu, act = (flat[:, i * 1024:(i + 1) * 1024].rearrange("p (b j t) -> p b j t", b=2, j=2) for i in range(3))
        scores = sb("scores", 2, 512)
        probs = sb("probs", 2, 512)
        probsT = sb("probsT", 2, 2, 2, TOK)
        const = sb("const", C_ALL)
        ones = sb("ones", P)
        zeros = sb("zeros", 512, dt=mybir.dt.bfloat16)
        par = sb("par", A_ALL)
        par2 = [par[:, l * B_ALL:(l + 1) * B_ALL] for l in range(DEPTH)]
        std = sb("std", TOK)
        peak = sb("peak", 2, 2)
        total = sb("total", 2, 2)
        lam = sb("lam", 8)
        ffp = sb("ffp", 8)
        eln = sb("eln", 24)
        cond = sb("cond", KD)
        mod = sb("mod", 48)
        mods = sb("mods", DEPTH, 48)
        gain = sb("gain", KD)
        small = sb("small", 64)
        dta, route, second = (sb(n, 2, 8) for n in ("dta", "route", "second"))
        cumt = sb("cumt", 24)
        flag = sb("flag", SLOTS + 9)
        place = sb("place", 16, dt=mybir.dt.uint32)
        chosen = sb("chosen", 2, 8)
        picks = sb("picks", EXPERTS + 1, 4)
        pick = sb("pick", 2, 4)
        crowd = sb("crowd", 8)
        crowded = sb("crowded", 1, dt=mybir.dt.int32)
        ident = const[:, C_ID:C_ID + P]
        rot = const[:, C_ROT:C_ROT + P]
        tri = const[:, C_TRI:C_TRI + P]
        half = [const[:, C_HALF + m:C_HALF + m + 1] for m in range(2)]
        eps1, eps2, one = (const[:, c:c + 1] for c in (C_EPS1, C_EPS2, C_ONE))
        bank = [ctx.enter_context(nc.psum_tensor(f"bank{b}", [P, 512], F32)) for b in range(8)]


        alr = scores[:, 1, 0:TOK]
        half_kv = probsT[:, :, :, :, :].rearrange("p a b c t -> p (a b c t)")
        qe = [tiles(half_kv[:, 512 * m:512 * m + 512], 2) for m in range(2)]
        ke, ktail = (tiles(half_kv[:, c:c + 512], 2) for c in (1024, 1536))
        ktok = [hc[:, 2 * m:2 * m + 2, :] for m in range(2)]
        att = flat[:, 4096:5120].rearrange("p (a h t) -> p a h t", a=2, h=4)
        states = work[:, 0:768].rearrange("p (n j v) -> p n j v", n=3, j=2)
        cmg, btok, state = tiles(work[:, 768:1280], 2), work[:, 1280:1408], work[:, 1408:1920]
        osq = memT[:, 4:8, :]
        cme = memT[:, 0:4, :].rearrange("p k t -> p (k t)").rearrange("p (h t) -> p h t", h=8)
        cumr, ecum = flat[:, 0:CH], flat[:, 5120:6144]
        seg = flat[:, CH:2 * CH].rearrange("p (c h t) -> p c h t", c=2, h=8)
        xw = kb[:, 0:2, :].rearrange("p k t -> p (k t)")
        dtraw, dtabs, dt, aexp, wtail = (small[:, c:c + n] for c, n in ((0, 16), (16, 16), (32, 16), (48, 8), (56, 8)))
        logit, best, placef, pair = small[:, 0:16], small[:, 16:32], small[:, 32:48], small[:, 48:56]

        htok = work[:, CH:2 * CH].rearrange("p (t d) -> p t d", t=2)
        xe = memT[:, 0:4, :].rearrange("p k t -> p (k t)").rearrange("p (k s) -> p k s", k=KD)
        ye = memT[:, 4:8, :].rearrange("p k t -> p (k t)")
        select, weigh = (tiles(hc[:, i, :], 2) for i in range(2))
        back = hc[:, 2, :]
        slots = const[:, C_IOTA:C_IOTA + P]

        w_loaded = [sem(f"w_loaded{s}") for s in range(SLOTS)]
        w_used = [sem(f"w_used{s}") for s in range(SLOTS)]
        bank_full = [sem(f"bank_full{b}") for b in range(8)]
        bank_free = [sem(f"bank_free{b}") for b in range(8)]
        tensor_step, vector_step, scalar_step, pool_step = (sem(n + "_step") for n in ("tensor", "vector", "scalar", "pool"))
        inputs_in, par_in, bias_in, par2_in = sem("inputs_in"), sem("par_in"), sem("bias_in"), sem("par2_in")
        windows_out = sem("windows_out")
        x_ready, y_ready, mean_ready, centred = sem("x_ready"), sem("y_ready"), sem("mean_ready"), sem("centred")
        squares_ready, var_ready, std_ready = sem("squares_ready"), sem("var_ready"), sem("std_ready")
        mixer_in, peak_ready, exp_ready, probs_ready = (
            sem("mixer_in"), sem("peak_ready"), sem("exp_ready"), sem("probs_ready"))
        heads_ready, merged_ready, lam_dot, lam_exp = sem("heads_ready"), sem("merged_ready"), sem("lam_dot"), sem("lam_exp")
        sub_raw, sub_squares, sub_std, gates_ready = sem("sub_raw"), sem("sub_squares"), sem("sub_std"), sem("gates_ready")
        cond_ready = sem("cond_ready")
        gate_full, up_full, conv_ready, silu_ready, act_ready = (
            [sem(f"{n}{i}") for i in range(2)] for n in ("gate_full", "up_full", "conv_ready", "silu_ready", "act_ready"))
        ffn_summed, out_done = sem("ffn_summed"), sem("out_done")
        alr_ready, decay_in, decay_exp, decay_ln, cum_ready, cum_exp, gla_in = (sem(n) for n in (
            "alr_ready", "decay_in", "decay_exp", "decay_ln", "cum_ready", "cum_exp", "gla_in"))
        tails_ready, att_ready, states_ready, raw_ready, normed_sq, normed_std = (sem(n) for n in (
            "tails_ready", "att_ready", "states_ready", "raw_ready", "normed_sq", "normed_std"))
        conv_in, conv_silu, dt_abs, dt_ln, dta_ready, seg_ready, seg_exp, ssd_in, state_in = (sem(n) for n in (
            "conv_in", "conv_silu", "dt_abs", "dt_ln", "dta_ready", "seg_ready", "seg_exp", "ssd_in", "state_in"))
        back_full, back_free, result_full, result_free = (sem(n) for n in ("back_full", "back_free", "result_full", "result_free"))
        proj_ready, pair_exp, pair_ready, route_in, chosen_ready, crowd_ready, select_ready, final_step = (sem(n) for n in (
            "proj_ready", "pair_exp", "pair_ready", "route_in", "chosen_ready", "crowd_ready", "select_ready", "final_step"))

        free = w_used + bank_free + [result_free]

        block = ctx.enter_context(nc.Block())

        def kpn(w):
            return w.rearrange("(k p) n -> p k n", p=P)

        cuts = [[(0, 256)], [(256, 256)], [(512, 256)], [(768, 256)], [(1024, 256)], [(1280, 256)], [(1552, 256)],
                [(1808, 256)], [(2064, 256)], [(2320, 256)], [(2576, 256)], [(1536, 16), (2832, 8)]]

        def ffn_steps(up, down, n, engine, per, f):
            up(0, 0)
            with f.trips((n - 1) // 2, per) as i:
                up(1, 2 * i + 1)
                down(0, 2 * i)
                up(0, 2 * i + 2)
                down(1, 2 * i + 1)
            if n % 2 == 0:
                up(1, n - 1)
                down(0, n - 2)
            down((n - 1) % 2, n - 1)

        @block.sync
        def _(sp):
            f = Follow(sp, tensor_step, free)
            turn = [0]

            def load(pieces, slot=None):
                s = turn[0] % SLOTS if slot is None else slot
                turn[0] += 1
                sp.wait_ge(w_used[s], f.now(w_used[s]))
                f.bump(w_used[s])
                pieces = pieces if isinstance(pieces, list) else [pieces]
                k, n = pieces[0].shape[1], sum(piece.shape[2] for piece in pieces)
                dst = tiles(ring[:, s, 0:k * n], k)
                at = 0
                for piece in pieces:
                    sp.dma_start(dst[:, :, at:at + piece.shape[2]], piece).then_inc(w_loaded[s], 16)
                    at += piece.shape[2]

            def ffn(gate, up_w, down_w, n, per):
                def up(p, i):
                    load(up_w(i), 3 * p + 1)
                    load(gate(i), 3 * p)

                def down(p, i):
                    load(down_w(i), 3 * p + 2)

                ffn_steps(up, down, n, sp, per, f)

            with f.trips(DEPTH, LAYER1) as l:
                turn[0] = 0
                for c in range(18):
                    load(kpn(w_in[l])[:, :, c * CW:(c + 1) * CW])
                for u in range(16):
                    if u < 12:
                        load(kpn(w_in[l])[:, :, (18 + u) * CW:(19 + u) * CW])
                    load(kpn(io["ada_w_2"][l])[:, :, u * CW:(u + 1) * CW])
                for n in range(4):
                    for b in range(3):
                        load(kpn(w_branch[l, b])[:, :, n * CW:(n + 1) * CW])
                for n in range(4):
                    load(kpn(w_mix[l])[:, :, n * CW:(n + 1) * CW])
                for n in range(8):
                    load(kpn(xa_kv[l])[:, :, n * CW:(n + 1) * CW])
                for n in range(4):
                    load(kpn(xa_q[l])[:, :, n * CW:(n + 1) * CW])
                for u in range(8):
                    load(kpn(io["ada_w_2"][l])[:, :, (16 + u) * CW:(17 + u) * CW])
                for n in range(4):
                    load(kpn(xa_o[l])[:, :, n * CW:(n + 1) * CW])
                ffn(lambda i: kpn(ffn_in[l])[:, :, bass.ds(i * CW + FF1, CW)],
                    lambda i: kpn(ffn_in[l])[:, :, bass.ds(i * CW, CW)],
                    lambda i: kpn(ffn_out[l, bass.ds(i * CW, CW), :]), FF1 // CW, FFN1_TRIP)
            for l in range(DEPTH):
                turn[0] = 0
                for cut in cuts:
                    load([kpn(io["w_in_2"][l])[:, :, c:c + n] for c, n in cut])
                for n in range(4):
                    load(kpn(io["w_out_2"][l])[:, :, n * CW:(n + 1) * CW])
                names = [("ffn_w_gate_2", "ffn_w_up_2", "ffn_w_down_2"), ("moe_w_gate_2", "moe_w_up_2", "moe_w_down_2")][l]
                wg, wu, wd = (io[n] for n in names)
                if l == 0:
                    ffn(lambda i: kpn(wg[0])[:, :, bass.ds(i * CW, CW)], lambda i: kpn(wu[0])[:, :, bass.ds(i * CW, CW)],
                        lambda i: kpn(wd[0, bass.ds(i * CW, CW), :]), FF2 // CW, FFN2_TRIP)
                else:
                    load(kpn(io["router_w_2"][0]))
                    def experts():
                        with f.trips(EXPERTS, EXPERT) as e:
                            ffn(lambda i: kpn(wg[0, e])[:, :, bass.ds(i * CW, CW)],
                                lambda i: kpn(wu[0, e])[:, :, bass.ds(i * CW, CW)],
                                lambda i: kpn(wd[0, e, bass.ds(i * CW, CW), :]), FF2 // CW, FFN3_TRIP)

                    experts()
                    sp.wait_ge(crowd_ready, f.next(crowd_ready))
                    with sp.If(sp.value_load(crowded[0:1, 0:1], min_val=0, max_val=1) > 0):
                        experts()

        @block.gpsimd
        def _(pool):
            f = Follow(pool, pool_step)
            for i, s in enumerate(free):
                pool.memset(flag[0:1, i:i + 1], 0.0).then_inc(s, 1)
            pool.memset(ones[:, :], 1.0 / D)
            pool.memset(zeros[:, :], 0.0).then_inc(f.count(pool_step), 1)
            for dst, src in ((const[:, :], io["const"]), (eln[:, :], io["eln"]),
                             (yT, kpn(io["xT"])), (memT[:, :, :], kpn(io["memT"]))):
                pool.dma_start(dst, src).then_inc(inputs_in, 16)
            for l in range(DEPTH):
                src = io["rpb"][l].rearrange("h j i -> (h j i)")
                pool.dma_start(io["windows"][l].rearrange("c h j i -> c (h j i)"),
                               bass.AP(src.tensor, src.offset, [[0, 64], [1, 8 * 7 * 127]])).then_inc(windows_out, 16)
            pool.wait_ge(windows_out, 16 * DEPTH)
            with f.trips(DEPTH, LAYER1) as l:
                pool.wait_ge(x_ready, f.now(x_ready) + 1)
                f.bump(x_ready, 3)
                pool.dma_start(par[:, :], io["par1"][l]).then_inc(par_in, 16)
                for side in range(2):
                    for h in range(8):
                        at = io["windows"][l, :, h, 1 - side:7 - side, 63:127]
                        src = bass.AP(at.tensor, at.offset, [[8 * 7 * 127 - 1, 64], [127, 6], [1, 64]])
                        pool.dma_start(bias[64 * side:64 * side + 64, h], src).then_inc(bias_in, 16)
            pool.wait_ge(x_ready, f.now(x_ready) + 1)
            f.bump(x_ready)
            for l in range(DEPTH):
                pool.dma_start(par2[l], io["par2"][l]).then_inc(par2_in, 16)
                pool.dma_start(kb[0:16, 2 + l, :], io["gla_a_w_2"][l]).then_inc(par2_in, 16)
            f.bump(x_ready, 2 * DEPTH)
            pool.dma_start(eln[:, 0:8], io["fin"]).then_inc(par2_in, 16)
            pool.wait_ge(y_ready, 2 + 2 * DEPTH + 1)
            pool.dma_start(kpn(io["out"]), yT).then_inc(out_done, 16)
            pool.wait_ge(out_done, 16)

        @block.tensor
        def _(pe):
            f = Follow(pe, tensor_step, free)
            turn, spent = [0], []

            def mm(out, lhsT, rhs, start, stop, done=None, **kw):
                ins = nc.tensor.matmul(out, lhsT, rhs, start=start, stop=stop, **kw)
                if done is not None:
                    ins.then_inc(f.count(done), 1)
                elif spent:
                    ins.then_inc(f.count(w_used[spent.pop()]), 1)

            def chunk(k=KD, n=CW, slot=None, pieces=1):
                s = turn[0] % SLOTS if slot is None else slot
                turn[0] += 1
                pe.wait_ge(w_loaded[s], f.next(w_loaded[s], 16 * pieces))
                return tiles(ring[:, s, 0:k * n], k), s

            def open_bank(b):
                pe.wait_ge(bank_free[b], f.now(bank_free[b]))
                f.bump(bank_free[b])

            def by_features(b, x, w, k, done):
                for j in range(2):
                    for t in range(k):
                        mm(bank[b][:, j * TOK:(j + 1) * TOK], w[:, t, j * P:(j + 1) * P], x[:, t, :],
                           t == 0, t == k - 1, done if (j, t) == (1, k - 1) else None)

            def features(b, x, k=KD):
                w, s = chunk(k)
                open_bank(b)
                by_features(b, x, w, k, bank_full[b])
                spent.append(s)

            def tokens(b, x):
                w, s = chunk()
                open_bank(b)
                for j in range(2):
                    for t in range(KD):
                        mm(bank[b][:, j * CW:(j + 1) * CW], x[:, t, j * P:(j + 1) * P], w[:, t, :],
                           t == 0, t == KD - 1, bank_full[b] if (j, t) == (1, KD - 1) else None)
                spent.append(s)

            def modulation(b):
                w, s = chunk()
                open_bank(b)
                for j in range(2):
                    for t in range(KD):
                        mm(bank[b][:, j:j + 1], w[:, t, j * P:(j + 1) * P], cond[:, t:t + 1],
                           t == 0, t == KD - 1, bank_full[b] if (j, t) == (1, KD - 1) else None)
                spent.append(s)

            def taken(b):
                pe.wait_ge(bank_free[b], f.now(bank_free[b]))

            def norm_mean():
                for t in range(KD):
                    mm(bank[5][:, 0:TOK], ones[:, :], yT[:, t, :], t == 0, t == KD - 1,
                       mean_ready if t == KD - 1 else None)

            def norm_var():
                pe.wait_ge(squares_ready, f.next(squares_ready))
                for t in range(KD):
                    mm(bank[4][:, 0:TOK], ones[:, :], squares[:, t, :], t == 0, t == KD - 1,
                       var_ready if t == KD - 1 else None)

            def turn_probs(u, n):
                pe.wait_ge(probs_ready, f.next(probs_ready))
                b = 4 + u % 2
                open_bank(b)
                for i in range(n):
                    ins = nc.tensor.transpose(bank[b][:, i * P:(i + 1) * P], probs[:, u % 2, i * P:(i + 1) * P], ident)
                ins.then_inc(f.count(bank_full[b]), 1)

            def probs_turned(u):
                pe.wait_ge(bank_free[4 + u % 2], f.now(bank_free[4 + u % 2]))

            def ffn(x, n, per):
                def up(p, i):
                    for o, full in ((0, gate_full[p]), (1, up_full[p])):
                        w, s = chunk(slot=3 * p + o)
                        by_features(2 * p + o, x, w, KD, full)
                        spent.append(s)
                    if isinstance(i, int) and i == 0:
                        mm(bank[4][:, 0:1], zeros[0:1, 0:P], zeros[0:1, 0:1], False, False, skip_group_check=True)

                def down(p, i):
                    w, s = chunk(2, D, 3 * p + 2)
                    pe.wait_ge(act_ready[p], f.next(act_ready[p]))
                    for t in range(2):
                        for n in range(KD):
                            mm(bank[4 + n // 2][:, (n % 2) * TOK:(n % 2 + 1) * TOK], w[:, t, n * P:(n + 1) * P],
                               act[:, p, t, :], False, False, w_used[s] if (t, n) == (1, KD - 1) else None,
                               skip_group_check=True)

                ffn_steps(up, down, n, pe, per, f)

            def open_sums():
                for b in range(4, 8):
                    mm(bank[b][:, :], zeros[0:1, 0:P], zeros[0:1, :], True, False, skip_group_check=True)

            def close_sums():
                for b in range(4, 8):
                    mm(bank[b][:, :], zeros[0:1, 0:P], zeros[0:1, :], False, True, ffn_summed if b == 7 else None,
                       skip_group_check=True)

            pe.wait_ge(inputs_in, f.next(inputs_in, 64))
            pe.wait_ge(pool_step, f.next(pool_step))
            norm_mean()
            norm_var()
            pe.wait_ge(cond_ready, f.next(cond_ready))
            pe.wait_ge(x_ready, f.next(x_ready))
            with f.trips(DEPTH, LAYER1) as l:
                turn[0] = 0
                for c in range(18):
                    (tokens if c in (4, 5, 10, 11) else features)(c % 4, xT)
                    if c == 7:
                        for j in range(4):
                            open_bank(j)
                            mm(bank[j][:, :], rot, (qa, ka)[j // 2][:, 2 * (j % 2):2 * (j % 2) + 2, :], True, True, bank_full[j])
                pe.wait_ge(mixer_in, f.next(mixer_in))
                for u in range(18):
                    if u < 16:
                        b = u % 2
                        open_bank(b)
                        a, t, qt = u // 8, u // 2 % 4, u % 2
                        for m in range(2):
                            mm(bank[b][:, m * TOK:(m + 1) * TOK], qhalf[a][m][:, t, qt * P:(qt + 1) * P], (ka, kb)[a][:, t, :],
                               True, True, bank_full[b] if m else None)
                    if u < 12:
                        features(6 + u % 2, xT)
                    if u < 16:
                        modulation(2 + u % 2)
                    if 1 <= u <= 16:
                        turn_probs(u - 1, 2 if u - 1 < 8 else 4)
                    if u == 10:
                        pe.wait_ge(sub_squares, f.next(sub_squares))
                        for h in range(4):
                            b = 4 + h // 2
                            if h % 2 == 0:
                                open_bank(b)
                            mm(bank[b][:, (h % 2) * TOK:(h % 2 + 1) * TOK], ones[:, :], ka[:, h, :], True, True,
                               bank_full[b] if h % 2 else None)
                    if u >= 3 and u % 2 == 1:
                        n = (u - 3) // 2
                        probs_turned(u - 2)
                        b = 2 + n % 2
                        open_bank(b)
                        for m in range(1 if n < 4 else 2):
                            for t in range(2):
                                if n < 4:
                                    v, out = va[:, t, n * P:(n + 1) * P], bank[b][:, 0:TOK]
                                else:
                                    h = 2 * (n - 4) + m
                                    v, out = vb[:, t, 64 * h:64 * h + 64], bank[b][64 * m:64 * m + 64, 0:TOK]
                                mm(out, v, probsT[:, n % 2, m, t, :], t == 0, t == 1,
                                   bank_full[b] if t and (n < 4 or m) else None)
                pe.wait_ge(heads_ready, f.next(heads_ready))
                for n in range(4):
                    for br, src in enumerate((qa, qb, hc)):
                        features((3 * n + br) % 4, src, 4)
                pe.wait_ge(merged_ready, f.next(merged_ready))
                for n in range(4):
                    features(n, merged)
                for n in range(4):
                    features(n, memT)
                taken(3)
                norm_mean()
                for n in range(2):
                    tokens(n, memT)
                norm_var()
                for n in range(2):
                    tokens(2 + n, memT)
                pe.wait_ge(x_ready, f.next(x_ready))
                for n in range(4):
                    features(n, xT)
                taken(3)
                for u in range(6):
                    if u < 4:
                        b = u % 2
                        open_bank(b)
                        for m in range(2):
                            h, qt = 2 * (u // 2) + m, u % 2
                            for t in range(2):
                                mm(bank[b][:, m * TOK:(m + 1) * TOK],
                                   (qa, ka)[h // 2][:, 2 * (h % 2) + t, qt * P:(qt + 1) * P],
                                   (qb, kb)[h // 2][:, 2 * (h % 2) + t, :], t == 0, t == 1, bank_full[b] if m and t else None)
                        modulation(2)
                        modulation(3)
                    if 1 <= u <= 4:
                        turn_probs(u - 1, 4)
                    if u >= 3 and u % 2 == 1:
                        n = (u - 3) // 2
                        probs_turned(u - 2)
                        for m in range(2):
                            h, b = 2 * n + m, 2 + m
                            open_bank(b)
                            for j in range(2):
                                for t in range(2):
                                    mm(bank[b][:, j * TOK:(j + 1) * TOK],
                                       (va, vb)[n][:, t, m * TOK + j * P:m * TOK + (j + 1) * P],
                                       probsT[:, n % 2, m, t, :], t == 0, t == 1, bank_full[b] if j and t else None)
                taken(3)
                for n in range(4):
                    features(n, merged)
                taken(3)
                norm_mean()
                norm_var()
                pe.wait_ge(x_ready, f.next(x_ready))
                open_sums()
                ffn(xT, FF1 // CW, FFN1_TRIP)
                close_sums()
                pe.wait_ge(y_ready, f.next(y_ready))
                norm_mean()
                norm_var()
                pe.wait_ge(x_ready, f.next(x_ready))

            for l in range(DEPTH):
                turn[0] = 0
                norm_var()
                pe.wait_ge(y_ready, f.next(y_ready))
                for c in range(11):
                    (tokens if c in (2, 3) else features)(c % 4, yT)
                w, s = chunk(KD, 24, pieces=2)
                open_bank(3)
                for t in range(KD):
                    mm(bank[3][0:16, 0:TOK], w[:, t, 0:16], yT[:, t, :], t == 0, t == KD - 1)
                for j in range(2):
                    for t in range(KD):
                        mm(bank[3][:, TOK + 8 * j:TOK + 8 * j + 8], yT[:, t, j * P:(j + 1) * P], w[:, t, 16:24],
                           t == 0, t == KD - 1, bank_full[3] if (j, t) == (1, KD - 1) else None)
                spent.append(s)
                taken(3)
                open_bank(0)
                for j in range(2):
                    mm(bank[0][:, j * TOK:(j + 1) * TOK], kb[0:16, 2 + l, j * P:(j + 1) * P], alr[0:16, :], True, True,
                       bank_full[0] if j else None)
                pe.wait_ge(conv_silu, f.next(conv_silu))
                for t in range(2):
                    open_bank(2 + t)
                    for j in range(4):
                        ins = nc.tensor.transpose(bank[2 + t][:, j * P:(j + 1) * P], qb[:, j, t * P:(t + 1) * P], ident)
                    ins.then_inc(f.count(bank_full[2 + t]), 1)
                open_bank(1)
                nc.tensor.transpose(bank[1][:, 0:P], ka[:, 0, 0:P], ident).then_inc(f.count(bank_full[1]), 1)
                pe.wait_ge(gla_in, f.next(gla_in))
                open_bank(1)
                for t in range(2):
                    for j in range(2):
                        ins = nc.tensor.transpose(bank[1][:, (2 * t + j) * P:(2 * t + j + 1) * P], ktail[:, j, t * P:(t + 1) * P], ident)
                ins.then_inc(f.count(bank_full[1]), 1)
                for a in range(2):
                    open_bank(2 + a)
                    for h in range(4):
                        mm(bank[2 + a][:, h * P:(h + 1) * P], ke[:, h // 2, a * P:(a + 1) * P],
                           qe[h % 2][:, h // 2, a * P:(a + 1) * P], True, True, bank_full[2 + a] if h == 3 else None)
                taken(1)
                for j in range(2):
                    open_bank(j)
                    for n in range(3):
                        for m in range(2):
                            h = 2 * j + m
                            mm(bank[j][64 * m:64 * m + 64, n * P:(n + 1) * P], ktok[n % 2][:, n // 2, h * 64:h * 64 + 64],
                               va[:, n // 2, h * P:(h + 1) * P], True, True, bank_full[j] if (n, m) == (2, 1) else None)
                for j in range(2):
                    open_bank(j)
                    for m in range(2):
                        h = 2 * j + m
                        for a in range(2):
                            at = m * TOK + a * P
                            mm(bank[j][:, at:at + P], va[:, a, h * P:(h + 1) * P], att[:, a, h, :], True, False,
                               skip_group_check=True)
                            for n in range(max(1, 2 * a), 2 * a + 2):
                                at = m * TOK + n * 64
                                mm(bank[j][:, at:at + 64], states[:, n - 1, j, :], qe[m][:, j, n * 64:n * 64 + 64],
                                   False, n == 2 * a + 1, bank_full[j] if (m, n) == (1, 3) else None, skip_group_check=True)
                pe.wait_ge(normed_sq, f.next(normed_sq))
                for j in range(2):
                    open_bank(4 + j)
                    for m in range(2):
                        mm(bank[4 + j][:, m * TOK:(m + 1) * TOK], ones[:, :], osq[:, 2 * j + m, :], True, True,
                           bank_full[4 + j] if m else None)
                pe.wait_ge(dta_ready, f.next(dta_ready))
                for q in range(4):
                    open_bank(q)
                    for i in range(4):
                        c, h = q // 2, 4 * (q % 2) + i
                        mm(bank[q][:, i * P:(i + 1) * P], dta[:, c, h:h + 1].to_broadcast([P, P]), tri, True, True,
                           bank_full[q] if i == 3 else None)
                open_bank(0)
                for c in range(2):
                    mm(bank[0][:, 8 * c:8 * c + 8], tri, dta[:, c, :], True, True)
                mm(bank[0][:, 16:24], ones[:, :], dta[:, 0, :], True, True, bank_full[0])
                pe.wait_ge(ssd_in, f.next(ssd_in))
                open_bank(1)
                for c in range(2):
                    for g in range(2):
                        mm(bank[1][:, (2 * c + g) * P:(2 * c + g + 1) * P], ka[:, 0, c * P:(c + 1) * P], cmg[:, g, c * P:(c + 1) * P],
                           True, True, bank_full[1] if (c, g) == (1, 1) else None)
                pe.wait_ge(state_in, f.next(state_in))
                open_bank(2)
                mm(bank[2][:, :], btok, xw, True, True, bank_full[2])
                pe.wait_ge(pair_ready, f.next(pair_ready))
                for j in range(2):
                    open_bank(j)
                    for i in range(2):
                        for m in range(2):
                            h = 4 * j + 2 * i + m
                            for c in range(2):
                                out = bank[j][64 * m:64 * m + 64, i * TOK + c * P:i * TOK + (c + 1) * P]
                                mm(out, vb[:, c, h * 64:h * 64 + 64], seg[:, c, h, :], True, c == 0, skip_group_check=True)
                            mm(out, state[:, h * 64:h * 64 + 64], cme[:, h, :], False, True,
                               bank_full[j] if (i, m) == (1, 1) else None, skip_group_check=True)
                pe.wait_ge(normed_sq, f.next(normed_sq))
                open_bank(4)
                for j in range(4):
                    mm(bank[4][:, 0:TOK], ones[:, :], osq[:, j, :], j == 0, j == 3, bank_full[4] if j == 3 else None)
                pe.wait_ge(merged_ready, f.next(merged_ready))
                for n in range(4):
                    features(n, merged)
                pe.wait_ge(x_ready, f.next(x_ready))
                norm_var()
                pe.wait_ge(y_ready, f.next(y_ready))
                if l == 0:
                    open_sums()
                    ffn(yT, FF2 // CW, FFN2_TRIP)
                else:
                    w, s = chunk(KD, 8)
                    open_bank(0)
                    for j in range(2):
                        for t in range(KD):
                            mm(bank[0][:, 8 * j:8 * j + 8], yT[:, t, j * P:(j + 1) * P], w[:, t, :], t == 0, t == KD - 1,
                               bank_full[0] if (j, t) == (1, KD - 1) else None)
                    spent.append(s)
                    for q in range(4):
                        open_bank(4 + q)
                        for i in range(4):
                            ins = nc.tensor.transpose(bank[4 + q][:, i * P:(i + 1) * P],
                                                      yT[:, 4 * (q % 2) + i, (q // 2) * P:(q // 2 + 1) * P], ident)
                        ins.then_inc(f.count(bank_full[4 + q]), 1)
                    pe.wait_ge(chosen_ready, f.next(chosen_ready))
                    open_bank(0)
                    every = one.to_broadcast([P, P])
                    mm(bank[0][:, 0:8], tri, chosen[:, 0, :], True, True)
                    mm(bank[0][:, 8:16], tri, chosen[:, 1, :], True, False)
                    mm(bank[0][:, 8:16], every, chosen[:, 0, :], False, True)
                    mm(bank[0][:, 16:24], every, chosen[:, 0, :], True, False)
                    mm(bank[0][:, 16:24], every, chosen[:, 1, :], False, True, bank_full[0])

                    def gather():
                        for q in range(2):
                            open_bank(6 + q)
                            for i in range(4):
                                for t in range(2):
                                    k = 4 * q + i
                                    mm(bank[6 + q][:, i * P:(i + 1) * P], htok[:, t, k * P:(k + 1) * P], select[:, t, :],
                                       t == 0, t == 1, bank_full[6 + q] if (i, t) == (3, 1) else None)

                    def up(p, i):
                        for o, full in ((0, gate_full[p]), (1, up_full[p])):
                            w, s = chunk(slot=3 * p + o)
                            for j in range(2):
                                for t in range(KD):
                                    mm(bank[2 * p + o][:, j * P:(j + 1) * P], w[:, t, j * P:(j + 1) * P], xe[:, t, :],
                                       t == 0, t == KD - 1, full if (j, t) == (1, KD - 1) else None)
                            spent.append(s)
                        if isinstance(i, int) and i == 0:
                            pe.wait_ge(result_free, f.now(result_free))
                            for n in range(2):
                                open_bank(4 + n)
                                mm(bank[4 + n][:, :], zeros[0:1, 0:P], zeros[0:1, :], True, False, skip_group_check=True)

                    def down(p, i):
                        w, s = chunk(2, D, 3 * p + 2)
                        pe.wait_ge(act_ready[p], f.next(act_ready[p]))
                        for t in range(2):
                            for n in range(2):
                                mm(bank[4 + n][:, :], act[:, p, t, 0:P], w[:, t, n * 512:(n + 1) * 512], False, False,
                                   w_used[s] if (t, n) == (1, 1) else None, skip_group_check=True)
                        if isinstance(i, int) and i == FF2 // CW - 2:
                            pe.wait_ge(select_ready, f.next(select_ready))
                            for t in range(2):
                                ins = nc.tensor.transpose(bank[0][:, t * P:(t + 1) * P], weigh[:, t, :], ident)
                            ins.then_inc(f.count(back_full), 1)

                    def experts():
                        pe.wait_ge(select_ready, f.next(select_ready))
                        taken(7)
                        pe.wait_ge(result_free, f.now(result_free))
                        gather()
                        taken(0)
                        taken(6)
                        taken(7)
                        with f.trips(EXPERTS, EXPERT):
                            ffn_steps(up, down, FF2 // CW, pe, FFN3_TRIP, f)
                            for n in range(2):
                                mm(bank[4 + n][:, :], zeros[0:1, 0:P], zeros[0:1, :], False, True, bank_full[4 + n],
                                   skip_group_check=True)
                            gather()
                            pe.wait_ge(back_free, f.next(back_free))
                            taken(4)
                            taken(5)
                            for q, b in enumerate((2, 3, 6, 7)):
                                if b > 5:
                                    taken(b)
                                for j in range(2):
                                    k = 2 * q + j
                                    mm(bank[b][:, j * TOK:(j + 1) * TOK], ye[:, k * P:(k + 1) * P], back, True, True,
                                       result_full if j else None)
                            f.bump(result_free, 4)

                    experts()
                    pe.wait_ge(crowd_ready, f.next(crowd_ready))
                    with pe.If(pe.value_load(crowded[0:1, 0:1], min_val=0, max_val=1) > 0):
                        experts()
                if l == 0:
                    close_sums()
                pe.wait_ge(x_ready, f.next(x_ready))
            norm_var()

        @block.vector
        def _(dve):
            f = Follow(dve, vector_step, free)
            v = nc.vector
            cos2, sin2 = (spread(const[:, c:c + TOK], 2) for c in (C_COS, C_SIN))

            def pairs(b):
                return tiles(bank[b][:, :], 2)

            def take(b, dst, src=None):
                dve.wait_ge(bank_full[b], f.next(bank_full[b]))
                v.tensor_copy(dst, pairs(b) if src is None else src).then_inc(f.count(bank_free[b]), 1)

            def norm_centre():
                dve.wait_ge(mean_ready, f.next(mean_ready))
                v.tensor_tensor(yT, yT, spread(bank[5][:, 0:TOK], KD), ALU.subtract).then_inc(f.count(centred), 1)

            def scaled_by_std(dst, src):
                dve.wait_ge(std_ready, f.next(std_ready))
                v.reciprocal(std[:, :], std[:, :]).then_inc(f.count(vector_step), 1)
                dve.wait_ge(f.last, f.now(f.last))
                v.tensor_tensor(dst, src, spread(std[:, :], KD), ALU.mult).then_inc(f.count(vector_step), 1)
                dve.wait_ge(f.last, f.now(f.last))

            def norm_finish(gains, biases):
                scaled_by_std(yT, yT)
                for k in range(KD):
                    ins = v.tensor_scalar(xT[:, k, :], yT[:, k, :], gains[:, k:k + 1], biases[:, k:k + 1], ALU.mult, ALU.add)
                ins.then_inc(f.count(x_ready), 1)

            def residual(n, b, done):
                v.scalar_tensor_tensor(yT[:, 2 * n:2 * n + 2, :], xT[:, 2 * n:2 * n + 2, :], ALPHA, pairs(b),
                                       ALU.mult, ALU.add).then_inc(f.count(done), 1)

            def peaks(u, scale, add=None):
                b = u % 2
                dve.wait_ge(bank_full[b], f.next(bank_full[b]))
                s = tiles(scores[:, b, :], 2)
                if add is None:
                    v.tensor_scalar(s, pairs(b), -scale, None, ALU.mult).then_inc(f.count(bank_free[b]), 1)
                else:
                    v.scalar_tensor_tensor(s, pairs(b), -scale, add, ALU.mult, ALU.subtract).then_inc(f.count(bank_free[b]), 1)
                dve.wait_ge(f.last, f.now(f.last))
                v.tensor_reduce(peak[:, b, :], s, AX.X, ALU.min).then_inc(f.count(peak_ready), 1)

            def normalise(u, difference):
                b = u % 2
                dve.wait_ge(exp_ready, f.next(exp_ready))
                v.reciprocal(total[:, b, :], total[:, b, :]).then_inc(f.count(vector_step), 1)
                dve.wait_ge(f.last, f.now(f.last))
                p = tiles(probs[:, b, :], 2)
                if difference:
                    v.tensor_tensor(total[:, b, 1:2], total[:, b, 1:2], lam[:, 4:5], ALU.mult).then_inc(f.count(vector_step), 1)
                    dve.wait_ge(f.last, f.now(f.last))
                    v.tensor_scalar(p[:, 1, :], p[:, 1, :], total[:, b, 1:2], None, ALU.mult).then_inc(f.count(vector_step), 1)
                    dve.wait_ge(f.last, f.now(f.last))
                    v.scalar_tensor_tensor(p[:, 0, :], p[:, 0, :], total[:, b, 0:1], p[:, 1, :], ALU.mult, ALU.add).then_inc(f.count(probs_ready), 1)
                else:
                    r = total[:, b, :].rearrange("p (m o) -> p m o", o=1).broadcast_to([P, 2, TOK])
                    v.tensor_tensor(p, p, r, ALU.mult).then_inc(f.count(probs_ready), 1)

            dve.wait_ge(inputs_in, f.next(inputs_in, 64))
            norm_centre()
            norm_finish(eln[:, 0:8], eln[:, 8:16])
            with f.trips(DEPTH, LAYER1) as l:
                dve.wait_ge(par_in, f.next(par_in, 16))
                lv = par[:, A_LAMV:A_LAMV + 256].rearrange("p (a b d) -> p a b d", a=2, b=2)
                v.tensor_tensor(tiles(scores[:, 0, 0:128], 2), lv[:, :, 0, :], lv[:, :, 1, :], ALU.mult).then_inc(f.count(vector_step), 1)
                v.tensor_tensor(lam[:, 5:6], par[:, A_SUB:A_SUB + 1], par[:, A_LAM1:A_LAM1 + 1], ALU.mult).then_inc(f.count(vector_step), 1)
                dve.wait_ge(f.last, f.now(f.last))
                v.tensor_reduce(lam[:, 0:2], tiles(scores[:, 0, 0:128], 2), AX.X, ALU.add).then_inc(f.count(lam_dot), 1)
                dve.wait_ge(lam_exp, f.next(lam_exp))
                v.scalar_tensor_tensor(lam[:, 4:5], lam[:, 3:4], lam[:, 2:3], par[:, A_LAM0:A_LAM0 + 1],
                                       ALU.subtract, ALU.subtract).then_inc(f.count(vector_step), 1)
                for c in range(18):
                    b, i = c % 4, c % 2
                    if c in (6, 7):
                        dve.wait_ge(bank_full[b], f.next(bank_full[b]))
                        for m in range(2):
                            v.tensor_scalar(qhalf[1][m][:, 2 * i:2 * i + 2, :], pairs(b), half[m], None, ALU.mult).then_inc(f.count(bank_free[b] if m else vector_step), 1)
                    elif c in (4, 5, 10, 11):
                        take(b, (va if c < 6 else vb)[:, :, i * CW:(i + 1) * CW])
                    else:
                        take(b, (qa, ka, None, None, kb, None, gb, gc, hc)[c // 2][:, 2 * i:2 * i + 2, :])
                    if c == 7:
                        for j in range(4):
                            src, tmp = (qa, ka)[j // 2][:, 2 * (j % 2):2 * (j % 2) + 2, :], tiles(scores[:, 0, :], 2)
                            dve.wait_ge(bank_full[j], f.next(bank_full[j]))
                            v.tensor_tensor(tmp, pairs(j), sin2, ALU.mult).then_inc(f.count(bank_free[j]), 1)
                            v.tensor_tensor(src, src, cos2, ALU.mult).then_inc(f.count(vector_step), 1)
                            dve.wait_ge(f.last, f.now(f.last))
                            v.tensor_tensor(src, src, tmp, ALU.add).then_inc(f.count(vector_step), 1)
                            dve.wait_ge(f.last, f.now(f.last))
                            if j < 2:
                                for m in range(2):
                                    v.tensor_scalar(qhalf[0][m][:, 2 * j:2 * j + 2, :], src, half[m], None, ALU.mult).then_inc(f.count(vector_step), 1)
                dve.wait_ge(bias_in, f.next(bias_in, 256))
                wide = bias.rearrange("p h j c -> p (h j) c")
                v.tensor_tensor(wide, wide, spread(const[:, C_WIN:C_WIN + 64], 48), ALU.add).then_inc(f.count(vector_step), 1)
                dve.wait_ge(f.last, f.now(f.last))
                v.tensor_tensor(gc[:, :, :], gc[:, :, :], hc[:, :, :], ALU.mult).then_inc(f.count(mixer_in), 1)
                for u in range(18):
                    if u < 8:
                        peaks(u, 0.125)
                    elif u < 16:
                        hp, at = u // 2 - 4, 2 - 2 * (u % 2)
                        peaks(u, 0.125, bias[:, 2 * hp:2 * hp + 2, at:at + 4, :].rearrange("p h j c -> p h (j c)"))
                    if 1 <= u <= 16:
                        normalise(u - 1, u - 1 < 8)
                    if u < 16:
                        b = 2 + u % 2
                        take(b, mod[:, 2 * u:2 * u + 2], bank[b][:, 0:2])
                    if 2 <= u < 6:
                        t = u - 2
                        w = [par[:, A_SCW + 4 * k + t:A_SCW + 4 * k + t + 1] for k in range(3)]
                        dve.wait_ge(f.last, f.now(f.last))
                        v.tensor_scalar(hc[:, t, :], gc[:, t, :], w[1], None, ALU.mult).then_inc(f.count(vector_step), 1)
                        dve.wait_ge(f.last, f.now(f.last))
                        v.scalar_tensor_tensor(hc[:, t, 1:TOK], gc[:, t, 0:TOK - 1], w[0], hc[:, t, 1:TOK], ALU.mult, ALU.add).then_inc(f.count(vector_step), 1)
                        dve.wait_ge(f.last, f.now(f.last))
                        v.scalar_tensor_tensor(hc[:, t, 0:TOK - 1], gc[:, t, 1:TOK], w[2], hc[:, t, 0:TOK - 1], ALU.mult, ALU.add).then_inc(f.count(vector_step), 1)
                        dve.wait_ge(f.last, f.now(f.last))
                        v.tensor_tensor(hc[:, t, :], hc[:, t, :], gb[:, t, :], ALU.mult).then_inc(f.count(vector_step), 1)
                    if u >= 3 and u % 2 == 1:
                        n = (u - 3) // 2
                        b = 2 + n % 2
                        take(b, (qa[:, n, :] if n < 4 else qb[:, n - 4, :]), bank[b][:, 0:TOK])
                        if n < 4:
                            dve.wait_ge(f.last, f.now(f.last))
                            v.tensor_tensor(ka[:, n, :], qa[:, n, :], qa[:, n, :], ALU.mult).then_inc(f.count(sub_squares if n == 3 else vector_step), 1)
                    if u == 14:
                        dve.wait_ge(sub_std, f.next(sub_std))
                        v.reciprocal(ka[:, :, :], ka[:, :, :]).then_inc(f.count(vector_step), 1)
                dve.wait_ge(f.last, f.now(f.last))
                v.scalar_tensor_tensor(qa[:, :, :], qa[:, :, :], lam[:, 5:6], ka[:, :, :], ALU.mult, ALU.mult).then_inc(f.count(heads_ready), 1)
                dve.wait_ge(gates_ready, f.next(gates_ready))
                for n in range(4):
                    for br in range(3):
                        c = 3 * n + br
                        b = c % 4
                        dve.wait_ge(bank_full[b], f.next(bank_full[b]))
                        g = gates[:, 8 * br + 2 * n:8 * br + 2 * n + 2, :]
                        dst = merged[:, 2 * n:2 * n + 2, :] if br == 0 else tiles(scores[:, c % 2, :], 2)
                        dve.wait_ge(f.last, f.now(f.last))
                        v.tensor_tensor(dst, pairs(b), g, ALU.mult).then_inc(f.count(bank_free[b]), 1)
                        if br:
                            dve.wait_ge(f.last, f.now(f.last))
                            m = merged[:, 2 * n:2 * n + 2, :]
                            v.tensor_tensor(m, m, dst, ALU.add).then_inc(f.count(merged_ready if (n, br) == (3, 2) else vector_step), 1)
                for n in range(4):
                    dve.wait_ge(bank_full[n], f.next(bank_full[n]))
                    residual(n, n, bank_free[n])
                for n in range(4):
                    take(n, (qb, kb)[n // 2][:, 2 * (n % 2):2 * (n % 2) + 2, :])
                norm_centre()
                for n in range(2):
                    take(n, va[:, :, n * CW:(n + 1) * CW])
                norm_finish(par[:, A_LNG:A_LNG + 8], par[:, A_LNB:A_LNB + 8])
                for n in range(2):
                    take(2 + n, vb[:, :, n * CW:(n + 1) * CW])
                for n in range(4):
                    take(n, (qa, ka)[n // 2][:, 2 * (n % 2):2 * (n % 2) + 2, :])
                for u in range(6):
                    if u < 4:
                        peaks(u, 1.0 / 16)
                    if 1 <= u <= 4:
                        normalise(u - 1, False)
                    if u < 4:
                        for i in range(2):
                            c = 16 + 2 * u + i
                            take(2 + i, mod[:, 2 * c:2 * c + 2], bank[2 + i][:, 0:2])
                    if u >= 3 and u % 2 == 1:
                        for m in range(2):
                            h = 2 * ((u - 3) // 2) + m
                            take(2 + m, merged[:, 2 * h:2 * h + 2, :])
                v.tensor_copy(mods[:, bass.ds(l, 1), :], mod[:, :].rearrange("p (o c) -> p o c", o=1)).then_inc(f.count(vector_step), 1)
                for n in range(4):
                    dve.wait_ge(bank_full[n], f.next(bank_full[n]))
                    residual(n, n, bank_free[n])
                norm_centre()
                norm_finish(par[:, A_LNG + 8:A_LNG + 16], par[:, A_LNB + 8:A_LNB + 16])

                def up(p, i):
                    v.tensor_copy(ffp[:, :], par[:, bass.ds(i * 8 + A_FF, 8)]).then_inc(f.count(vector_step), 1)
                    dve.wait_ge(f.last, f.now(f.last))
                    dve.wait_ge(gate_full[p], f.next(gate_full[p]))
                    g, b = pairs(2 * p), 2 * p
                    for j in range(2):
                        v.tensor_scalar(conva[:, p, j, :], g[:, j, :], ffp[:, 4 * j + 1:4 * j + 2], ffp[:, 4 * j + 3:4 * j + 4],
                                        ALU.mult, ALU.add).then_inc(f.count(vector_step), 1)
                    dve.wait_ge(f.last, f.now(f.last))
                    for j in range(2):
                        v.scalar_tensor_tensor(conva[:, p, j, 1:TOK], g[:, j, 0:TOK - 1], ffp[:, 4 * j:4 * j + 1],
                                               conva[:, p, j, 1:TOK], ALU.mult, ALU.add).then_inc(f.count(vector_step), 1)
                    dve.wait_ge(f.last, f.now(f.last))
                    for j in range(2):
                        v.scalar_tensor_tensor(conva[:, p, j, 0:TOK - 1], g[:, j, 1:TOK], ffp[:, 4 * j + 2:4 * j + 3],
                                               conva[:, p, j, 0:TOK - 1], ALU.mult, ALU.add).then_inc(f.count(conv_ready[p] if j else vector_step), 1)
                    dve.wait_ge(up_full[p], f.next(up_full[p]))
                    dve.wait_ge(silu_ready[p], f.next(silu_ready[p]))
                    v.tensor_tensor(act[:, p, :, :], silu[:, p, :, :], pairs(b + 1), ALU.mult).then_inc(f.count(act_ready[p]), 1)

                ffn_steps(up, lambda p, i: None, FF1 // CW, dve, FFN1_TRIP, f)
                dve.wait_ge(ffn_summed, f.next(ffn_summed))
                for n in range(4):
                    residual(n, 4 + n, y_ready if n == 3 else None)
                norm_centre()
                norm_finish(par[:, A_LNG + 16:A_LNG + 24], par[:, A_LNB + 16:A_LNB + 24])

            def rms_finish(l, which):
                scaled_by_std(yT, xT[:, :, :])
                for k in range(KD):
                    ins = v.tensor_scalar(yT[:, k, :], yT[:, k, :], gain[:, k:k + 1],
                                          mods[:, l, 24 * which + k:24 * which + k + 1], ALU.mult, ALU.add)
                ins.then_inc(f.count(y_ready), 1)

            def rms_gain(l, which, done=None):
                v.scalar_tensor_tensor(gain[:, :], mods[:, l, 24 * which + 8:24 * which + 16], 1.0,
                                       par2[l][:, 8 * which:8 * which + 8], ALU.add, ALU.mult).then_inc(f.count(done), 1)

            def add_gated(l, which, n, b, done):
                for i in range(2):
                    k = 2 * n + i
                    v.scalar_tensor_tensor(xT[:, k, :], pairs(b)[:, i, :], mods[:, l, 24 * which + 16 + k:24 * which + 17 + k],
                                           xT[:, k, :], ALU.mult, ALU.add).then_inc(f.count(done if i else vector_step), 1)

            dve.wait_ge(par2_in, f.next(par2_in, 80))
            for l in range(DEPTH):
                v.tensor_tensor(mods[:, l, :], mods[:, l, :], par2[l][:, B_ADA:B_ADA + 48], ALU.add).then_inc(f.count(vector_step), 1)
            for l in range(DEPTH):
                p2 = par2[l]
                dve.wait_ge(f.last, f.now(f.last))
                rms_gain(l, 0)
                rms_finish(l, 0)
                dsts = [qa[:, 0:2, :], qa[:, 2:4, :], va[:, :, 0:CW], va[:, :, CW:2 * CW], gb[:, 0:2, :], gb[:, 2:4, :],
                        gc[:, 0:2, :], gc[:, 2:4, :], hc[:, 0:2, :], hc[:, 2:4, :], kb[:, 0:2, :]]
                for c, dst in enumerate(dsts):
                    take(c % 4, dst)
                dve.wait_ge(bank_full[3], f.next(bank_full[3]))
                v.tensor_tensor(tiles(dtraw, 2), tiles(bank[3][:, TOK:TOK + 16], 2), spread(p2[:, B_DTB:B_DTB + 8], 2), ALU.add).then_inc(f.count(vector_step), 1)
                dve.wait_ge(f.last, f.now(f.last))
                v.scalar_tensor_tensor(dtabs, dtraw, -1.0, dtraw, ALU.mult, ALU.max).then_inc(f.count(proj_ready), 1)
                v.tensor_copy(alr[0:16, :], bank[3][0:16, 0:TOK]).then_inc(f.count(bank_free[3]), 1)
                dve.wait_ge(f.last, f.now(f.last))
                raw = [hc[:, j, :] for j in range(4)] + [kb[:, j, :] for j in range(2)]
                dst = [qb[:, j, :] for j in range(4)] + [ka[:, j, :] for j in range(2)]
                for tap in (3, 2, 1, 0):
                    s = 3 - tap
                    for j in range(6):
                        w = p2[:, B_CW + 6 * tap + j:B_CW + 6 * tap + j + 1]
                        if s == 0:
                            ins = v.tensor_scalar(dst[j], raw[j], w, p2[:, B_CB + j:B_CB + j + 1], ALU.mult, ALU.add)
                        else:
                            ins = v.scalar_tensor_tensor(dst[j][:, s:TOK], raw[j][:, 0:TOK - s], w, dst[j][:, s:TOK], ALU.mult, ALU.add)
                    ins.then_inc(f.count(conv_in if tap == 0 else vector_step), 1)
                    dve.wait_ge(f.last, f.now(f.last))
                dve.wait_ge(bank_full[0], f.next(bank_full[0]))
                z = ka[:, 2:4, :]
                for j in range(2):
                    v.tensor_scalar(z[:, j, :], pairs(0)[:, j, :], p2[:, B_AB + j:B_AB + j + 1], None, ALU.add).then_inc(f.count(bank_free[0] if j else vector_step), 1)
                dve.wait_ge(f.last, f.now(f.last))
                v.scalar_tensor_tensor(tiles(scores[:, 0, :], 2), z, -1.0, z, ALU.mult, ALU.max).then_inc(f.count(decay_in), 1)
                dve.wait_ge(dt_ln, f.next(dt_ln))
                v.scalar_tensor_tensor(dt, dtraw, 0.0, dtabs, ALU.max, ALU.add).then_inc(f.count(vector_step), 1)
                dve.wait_ge(f.last, f.now(f.last))
                v.scalar_tensor_tensor(dta[:, :, :], tiles(dt, 2), -1.0, spread(aexp, 2), ALU.mult, ALU.mult).then_inc(f.count(dta_ready), 1)
                dve.wait_ge(decay_ln, f.next(decay_ln))
                v.scalar_tensor_tensor(z, z, 0.0, tiles(scores[:, 0, :], 2), ALU.min, ALU.subtract).then_inc(f.count(vector_step), 1)
                dve.wait_ge(f.last, f.now(f.last))
                v.tensor_scalar(z, z, 1.0 / 16, None, ALU.mult).then_inc(f.count(vector_step), 1)
                dve.wait_ge(f.last, f.now(f.last))
                run = probs[:, 0, :].rearrange("p (n c) -> p n c", c=64)
                zc = z.rearrange("p j (n c) -> p (j n) c", c=64)
                for n in range(8):
                    ins = v.tensor_tensor_scan(run[:, n, :], one.to_broadcast([P, 64]), zc[:, n, :], 0.0, ALU.mult, ALU.add)
                ins.then_inc(f.count(vector_step), 1)
                dve.wait_ge(f.last, f.now(f.last))
                v.tensor_tensor(scores[:, 1, :].rearrange("p (n c) -> p n c", c=64), run[:, :, 63:64].broadcast_to([P, 8, 64]), run,
                                ALU.subtract).then_inc(f.count(cum_ready), 1)
                dve.wait_ge(cum_exp, f.next(cum_exp))
                grow2, shrink, tail = tiles(probs[:, 1, :], 2), tiles(scores[:, 0, :], 2), tiles(scores[:, 1, :], 2)
                qs = tiles(probs[:, 0, :], 2)
                v.scalar_tensor_tensor(qs, qa[:, 0:2, :], 0.125, grow2, ALU.mult, ALU.mult).then_inc(f.count(vector_step), 1)
                v.tensor_tensor(ke, qa[:, 2:4, :], shrink, ALU.mult).then_inc(f.count(vector_step), 1)
                dve.wait_ge(f.last, f.now(f.last))
                for m in range(2):
                    v.tensor_scalar(qe[m], qs, half[m], None, ALU.mult).then_inc(f.count(vector_step), 1)
                v.tensor_tensor(ktail, qa[:, 2:4, :], tail, ALU.mult).then_inc(f.count(gla_in), 1)
                v.memset(att, 0.0).then_inc(f.count(vector_step), 1)
                for t in range(2):
                    dve.wait_ge(bank_full[2 + t], f.next(bank_full[2 + t]))
                    v.tensor_tensor(tiles(vb[:, t, :], 8), tiles(bank[2 + t][:, :], 8),
                                    dt[:, 8 * t:8 * t + 8].rearrange("p (h o) -> p h o", o=1).broadcast_to([P, 8, 64]), ALU.mult).then_inc(f.count(bank_free[2 + t]), 1)
                take(1, btok, bank[1][:, 0:P])
                dve.wait_ge(bank_full[1], f.next(bank_full[1]))
                for m in range(2):
                    v.tensor_scalar(ktok[m], pairs(1), half[m], None, ALU.mult).then_inc(f.count(bank_free[1] if m else vector_step), 1)
                allow = const[:, C_DIAG:C_DIAG + P].bitcast(mybir.dt.uint32)
                for a in range(2):
                    dve.wait_ge(bank_full[2 + a], f.next(bank_full[2 + a]))
                    v.copy_predicated(att[:, a, :, :], spread(allow, 4), tiles(bank[2 + a][:, :], 4)).then_inc(f.count(bank_free[2 + a]), 1)
                for j in range(2):
                    dve.wait_ge(bank_full[j], f.next(bank_full[j]))
                    for n in range(3):
                        new = bank[j][:, n * P:(n + 1) * P]
                        if n == 0:
                            ins = v.tensor_copy(states[:, 0, j, :], new)
                        else:
                            at = j * TOK + n * 64 + 63
                            ins = v.scalar_tensor_tensor(states[:, n, j, :], states[:, n - 1, j, :], probs[:, 1, at:at + 1], new, ALU.mult, ALU.add)
                        ins.then_inc(f.count(bank_free[j] if n == 2 else vector_step), 1)
                        dve.wait_ge(f.last, f.now(f.last))
                for j in range(2):
                    take(j, merged[:, 2 * j:2 * j + 2, :])
                dve.wait_ge(f.last, f.now(f.last))
                v.tensor_tensor(osq, merged[:, 0:4, :], merged[:, 0:4, :], ALU.mult).then_inc(f.count(normed_sq), 1)
                for q in range(4):
                    take(q, cumr[:, q * 512:(q + 1) * 512], bank[q][:, :])
                take(0, cumt[:, :], bank[0][:, 0:24])
                dve.wait_ge(f.last, f.now(f.last))
                for c in range(2):
                    for h in range(8):
                        at = (8 * c + h) * P
                        v.scalar_tensor_tensor(seg[:, c, h, :], cumr[:, at:at + P], cumt[:, 8 * c + h:8 * c + h + 1],
                                               const[:, C_BAN:C_BAN + P], ALU.subtract, ALU.add).then_inc(f.count(vector_step), 1)
                v.scalar_tensor_tensor(wtail, cumt[:, 16:24], float(D), cumt[:, 0:8], ALU.mult, ALU.subtract).then_inc(f.count(seg_ready), 1)
                for g in range(2):
                    v.tensor_scalar(cmg[:, g, :], ka[:, 1, :], half[g], None, ALU.mult).then_inc(f.count(ssd_in if g else vector_step), 1)
                dve.wait_ge(normed_std, f.next(normed_std))
                v.reciprocal(osq, osq).then_inc(f.count(vector_step), 1)
                dve.wait_ge(f.last, f.now(f.last))
                v.scalar_tensor_tensor(merged[:, 0:4, :], merged[:, 0:4, :], p2[:, B_GN:B_GN + 1], osq, ALU.mult, ALU.mult).then_inc(f.count(vector_step), 1)
                dve.wait_ge(f.last, f.now(f.last))
                v.tensor_tensor(merged[:, 0:4, :], merged[:, 0:4, :], gb[:, :, :], ALU.mult).then_inc(f.count(vector_step), 1)
                dve.wait_ge(seg_exp, f.next(seg_exp))
                v.tensor_tensor(tiles(xw, 8), tiles(vb[:, 0, :], 8), wtail.rearrange("p (h o) -> p h o", o=1).broadcast_to([P, 8, 64]),
                                ALU.mult).then_inc(f.count(state_in), 1)
                dve.wait_ge(bank_full[1], f.next(bank_full[1]))
                for c in range(2):
                    for g in range(2):
                        s = seg[:, c, 4 * g:4 * g + 4, :]
                        v.tensor_tensor(s, s, spread(bank[1][:, (2 * c + g) * P:(2 * c + g + 1) * P], 4), ALU.mult).then_inc(f.count(bank_free[1] if (c, g) == (1, 1) else vector_step), 1)
                take(2, state, bank[2][:, :])
                for g in range(2):
                    v.tensor_tensor(cme[:, 4 * g:4 * g + 4, :], tiles(ecum, 8)[:, 4 * g:4 * g + 4, :], spread(cmg[:, g, P:TOK], 4),
                                    ALU.mult).then_inc(f.count(pair_ready if g else vector_step), 1)
                for j in range(2):
                    dve.wait_ge(bank_full[j], f.next(bank_full[j]))
                    for i in range(2):
                        t = 2 * j + i
                        v.scalar_tensor_tensor(merged[:, 4 + t, :], qb[:, t, :], p2[:, B_DS + t:B_DS + t + 1], pairs(j)[:, i, :],
                                               ALU.mult, ALU.add).then_inc(f.count(bank_free[j] if i else vector_step), 1)
                dve.wait_ge(f.last, f.now(f.last))
                v.tensor_tensor(merged[:, 4:8, :], merged[:, 4:8, :], gc[:, :, :], ALU.mult).then_inc(f.count(vector_step), 1)
                dve.wait_ge(f.last, f.now(f.last))
                v.tensor_tensor(osq, merged[:, 4:8, :], merged[:, 4:8, :], ALU.mult).then_inc(f.count(normed_sq), 1)
                dve.wait_ge(normed_std, f.next(normed_std))
                v.reciprocal(std[:, :], std[:, :]).then_inc(f.count(vector_step), 1)
                dve.wait_ge(f.last, f.now(f.last))
                for j in range(4):
                    ins = v.scalar_tensor_tensor(merged[:, 4 + j, :], merged[:, 4 + j, :], p2[:, B_SN + j:B_SN + j + 1], std[:, :],
                                                 ALU.mult, ALU.mult)
                ins.then_inc(f.count(merged_ready), 1)
                for n in range(4):
                    dve.wait_ge(bank_full[n], f.next(bank_full[n]))
                    add_gated(l, 0, n, n, bank_free[n])
                rms_gain(l, 1, x_ready)
                rms_finish(l, 1)
                if l == 0:
                    def up(p, i):
                        f.bump(gate_full[p])
                        dve.wait_ge(up_full[p], f.next(up_full[p]))
                        dve.wait_ge(silu_ready[p], f.next(silu_ready[p]))
                        v.tensor_tensor(act[:, p, :, :], silu[:, p, :, :], pairs(2 * p + 1), ALU.mult).then_inc(f.count(act_ready[p]), 1)

                    ffn_steps(up, lambda p, i: None, FF2 // CW, dve, FFN2_TRIP, f)
                else:
                    take(0, tiles(logit, 2), tiles(bank[0][:, 0:16], 2))
                    dve.wait_ge(f.last, f.now(f.last))
                    for t in range(2):
                        v.max(best[:, 8 * t:8 * t + 8], logit[:, 8 * t:8 * t + 8]).then_inc(f.count(vector_step), 1)
                    dve.wait_ge(f.last, f.now(f.last))
                    for t in range(2):
                        v.max_index(place[:, 8 * t:8 * t + 8], best[:, 8 * t:8 * t + 8], logit[:, 8 * t:8 * t + 8]).then_inc(f.count(vector_step), 1)
                    b2 = tiles(best, 2)
                    v.tensor_tensor(pair[:, 0:2], b2[:, :, 1], b2[:, :, 0], ALU.subtract).then_inc(f.count(route_in), 1)
                    dve.wait_ge(f.last, f.now(f.last))
                    v.tensor_copy(placef, place[:, :]).then_inc(f.count(vector_step), 1)
                    v.memset(picks[:, EXPERTS:EXPERTS + 1, :], 0.0).then_inc(f.count(vector_step), 1)
                    dve.wait_ge(f.last, f.now(f.last))
                    v.tensor_scalar(placef, placef, 1.0, None, ALU.add).then_inc(f.count(vector_step), 1)
                    dve.wait_ge(f.last, f.now(f.last))
                    number = slots[:, 0:EXPERTS]
                    for t in range(2):
                        v.tensor_scalar(chosen[:, t, :], number, placef[:, 8 * t:8 * t + 1], None, ALU.is_equal).then_inc(f.count(vector_step), 1)
                    dve.wait_ge(f.last, f.now(f.last))
                    for t in range(2):
                        v.scalar_tensor_tensor(chosen[:, t, :], number, placef[:, 8 * t + 1:8 * t + 2], chosen[:, t, :],
                                               ALU.is_equal, ALU.add).then_inc(f.count(chosen_ready if t else vector_step), 1)
                    dve.wait_ge(pair_exp, f.next(pair_exp))
                    v.tensor_scalar(pair[:, 2:4], pair[:, 0:2], 1.0, None, ALU.add).then_inc(f.count(vector_step), 1)
                    dve.wait_ge(f.last, f.now(f.last))
                    v.reciprocal(pair[:, 2:4], pair[:, 2:4]).then_inc(f.count(vector_step), 1)
                    dve.wait_ge(f.last, f.now(f.last))
                    v.tensor_tensor(pair[:, 4:6], pair[:, 0:2], pair[:, 2:4], ALU.mult).then_inc(f.count(vector_step), 1)
                    dve.wait_ge(f.last, f.now(f.last))
                    for t in range(2):
                        v.tensor_scalar(route[:, t, :], number, placef[:, 8 * t:8 * t + 1], pair[:, 2 + t:3 + t], ALU.is_equal, ALU.mult).then_inc(f.count(vector_step), 1)
                        v.tensor_scalar(second[:, t, :], number, placef[:, 8 * t + 1:8 * t + 2], pair[:, 4 + t:5 + t], ALU.is_equal, ALU.mult).then_inc(f.count(vector_step), 1)
                    dve.wait_ge(f.last, f.now(f.last))
                    v.tensor_tensor(picks[:, 0:EXPERTS, 2:4].rearrange("p e t -> p t e"), route[:, :, :], second[:, :, :], ALU.add).then_inc(f.count(vector_step), 1)
                    dve.wait_ge(bank_full[0], f.next(bank_full[0]))
                    v.tensor_tensor(picks[:, 0:EXPERTS, 0:2].rearrange("p e t -> p t e"), tiles(bank[0][:, 0:16], 2), chosen[:, :, :],
                                    ALU.mult).then_inc(f.count(vector_step), 1)
                    v.tensor_reduce(crowd[:, 0:1], bank[0][:, 16:24], AX.X, ALU.max).then_inc(f.count(bank_free[0]), 1)
                    dve.wait_ge(f.last, f.now(f.last))
                    v.tensor_scalar(crowded[:, :], crowd[:, 0:1], float(P), None, ALU.is_gt).then_inc(f.count(crowd_ready), 1)

                    def up(p, i):
                        f.bump(gate_full[p])
                        dve.wait_ge(up_full[p], f.next(up_full[p]))
                        dve.wait_ge(silu_ready[p], f.next(silu_ready[p]))
                        v.tensor_tensor(act[:, p, :, 0:P], silu[:, p, :, 0:P], tiles(bank[2 * p + 1][:, 0:2 * P], 2), ALU.mult).then_inc(f.count(act_ready[p]), 1)
                        if isinstance(i, int) and i == 0:
                            for t in range(2):
                                v.tensor_scalar(weigh[:, t, :], slots, pick[:, 0, t:t + 1], pick[:, 0, 2 + t:3 + t], ALU.is_equal, ALU.mult).then_inc(f.count(vector_step), 1)
                            for t in range(2):
                                v.tensor_scalar(select[:, t, :], slots, pick[:, 1, t:t + 1], None, ALU.is_equal).then_inc(f.count(select_ready if t else vector_step), 1)

                    def experts():
                        for t in range(2):
                            v.tensor_scalar(select[:, t, :], slots, picks[:, 0, t:t + 1], None, ALU.is_equal).then_inc(f.count(select_ready if t else vector_step), 1)
                        with f.trips(EXPERTS, EXPERT) as e:
                            dve.wait_ge(f.last, f.now(f.last))
                            v.tensor_copy(pick[:, :, :], picks[:, bass.ds(e, 2), :]).then_inc(f.count(vector_step), 1)
                            dve.wait_ge(f.last, f.now(f.last))
                            ffn_steps(up, lambda p, i: None, FF2 // CW, dve, FFN3_TRIP, f)
                            for n, b in enumerate((2, 3, 6, 7)):
                                dve.wait_ge(result_full, f.next(result_full))
                                add_gated(l, 1, n, b, result_free)
                        dve.wait_ge(f.last, f.now(f.last))

                    experts()
                    with dve.If(dve.value_load(crowded[0:1, 0:1], min_val=0, max_val=1) > 0):
                        v.tensor_scalar(picks[:, :, 0:2], picks[:, :, 0:2], -float(P), None, ALU.add).then_inc(f.count(vector_step), 1)
                        dve.wait_ge(f.last, f.now(f.last))
                        experts()
                    v.tensor_copy(gain[:, :], eln[:, 0:8]).then_inc(x_ready, 1)
                if l == 0:
                    dve.wait_ge(ffn_summed, f.next(ffn_summed))
                    for n in range(4):
                        add_gated(l, 1, n, 4 + n, x_ready if n == 3 else None)
            dve.wait_ge(std_ready, f.next(std_ready))
            v.reciprocal(std[:, :], std[:, :]).then_inc(final_step, 1)
            dve.wait_ge(final_step, 1)
            v.tensor_tensor(yT, xT[:, :, :], spread(std[:, :], KD), ALU.mult).then_inc(final_step, 1)
            dve.wait_ge(final_step, 2)
            for k in range(KD):
                ins = v.tensor_scalar(yT[:, k, :], yT[:, k, :], gain[:, k:k + 1], None, ALU.mult)
            ins.then_inc(f.count(y_ready), 1)

        @block.scalar
        def _(eng):
            f = Follow(eng, scalar_step, free)
            a = nc.scalar

            def take(b, dst, src=None):
                eng.wait_ge(bank_full[b], f.next(bank_full[b]))
                a.copy(dst, tiles(bank[b][:, :], 2) if src is None else src).then_inc(f.count(bank_free[b]), 1)

            def norm(eps, src, before):
                eng.wait_ge(before, f.next(before))
                a.activation(squares, src, ACT.Square).then_inc(f.count(squares_ready), 1)
                eng.wait_ge(var_ready, f.next(var_ready))
                a.activation(std[:, :], bank[4][:, 0:TOK], ACT.Sqrt, bias=eps).then_inc(f.count(std_ready), 1)

            def exps(u):
                b = u % 2
                eng.wait_ge(peak_ready, f.next(peak_ready))
                for m in range(2):
                    ins = a.activation(probs[:, b, m * TOK:(m + 1) * TOK], scores[:, b, m * TOK:(m + 1) * TOK], ACT.Exp,
                                       bias=peak[:, b, m:m + 1], scale=-1.0, accum_out=total[:, b, m:m + 1])
                ins.then_inc(f.count(exp_ready), 1)

            def probs_out(u, n, whole):
                b, qt = 4 + u % 2, u % 2
                dst = probsT[:, n % 2, :, :, qt * P:(qt + 1) * P]
                if whole:
                    take(b, dst.rearrange("p m t q -> p (m t) q"), tiles(bank[b][:, :], 4))
                else:
                    take(b, dst[:, 0, :, :], tiles(bank[b][:, 0:2 * P], 2))

            eng.wait_ge(inputs_in, f.next(inputs_in, 64))
            a.activation(cond[:, :], eln[:, 16:24], ACT.Silu).then_inc(f.count(cond_ready), 1)
            norm(eps1, yT, centred)
            f.bump(x_ready)
            with f.trips(DEPTH, LAYER1):
                eng.wait_ge(lam_dot, f.next(lam_dot))
                a.activation(lam[:, 2:4], lam[:, 0:2], ACT.Exp).then_inc(f.count(lam_exp), 1)
                for u in range(18):
                    if u < 16:
                        exps(u)
                    if u < 12:
                        take(6 + u % 2, gates[:, 2 * u:2 * u + 2, :])
                    if 1 <= u <= 16:
                        probs_out(u - 1, (u - 1) // 2, u - 1 >= 8)
                    if u == 10:
                        for j in range(2):
                            take(4 + j, ka[:, 2 * j:2 * j + 2, :])
                        eng.wait_ge(f.last, f.now(f.last))
                        a.activation(ka[:, :, :], ka[:, :, :], ACT.Sqrt, bias=eps1, scale=float(D // P)).then_inc(f.count(sub_std), 1)
                eng.wait_ge(f.last, f.now(f.last))
                a.activation(flat, flat, ACT.Sigmoid).then_inc(f.count(gates_ready), 1)
                norm(eps1, yT, centred)
                for u in range(6):
                    if u < 4:
                        exps(u)
                    if 1 <= u <= 4:
                        probs_out(u - 1, (u - 1) // 2, True)
                norm(eps1, yT, centred)

                def up(p, i):
                    eng.wait_ge(conv_ready[p], f.next(conv_ready[p]))
                    a.activation(silu[:, p, :, :], conva[:, p, :, :], ACT.Silu).then_inc(f.count(silu_ready[p]), 1)

                ffn_steps(up, lambda p, i: None, FF1 // CW, eng, FFN1_TRIP, f)
                norm(eps1, yT, centred)
                f.bump(x_ready, 3)

            def up(p, i):
                eng.wait_ge(gate_full[p], f.next(gate_full[p]))
                a.activation(silu[:, p, :, :], tiles(bank[2 * p][:, :], 2), ACT.Silu).then_inc(f.count(silu_ready[p]), 1)

            eng.wait_ge(x_ready, f.now(x_ready))
            for l in range(DEPTH):
                if l == 0:
                    a.activation(squares, xT[:, :, :], ACT.Square).then_inc(f.count(squares_ready), 1)
                    eng.wait_ge(var_ready, f.next(var_ready))
                    a.activation(std[:, :], bank[4][:, 0:TOK], ACT.Sqrt, bias=eps2).then_inc(f.count(std_ready), 1)
                else:
                    norm(eps2, xT[:, :, :], x_ready)
                eng.wait_ge(proj_ready, f.next(proj_ready))
                a.activation(gb[:, :, :], gb[:, :, :], ACT.Silu).then_inc(f.count(scalar_step), 1)
                a.activation(gc[:, :, :], gc[:, :, :], ACT.Silu).then_inc(f.count(scalar_step), 1)
                eng.wait_ge(conv_in, f.next(conv_in))
                a.activation(qb[:, :, :], qb[:, :, :], ACT.Silu).then_inc(f.count(scalar_step), 1)
                a.activation(ka[:, 0:2, :], ka[:, 0:2, :], ACT.Silu).then_inc(f.count(conv_silu), 1)
                a.activation(aexp, par2[l][:, B_ALOG:B_ALOG + 8], ACT.Exp).then_inc(f.count(scalar_step), 1)
                a.activation(dtabs, dtabs, ACT.Exp, scale=-1.0).then_inc(f.count(scalar_step), 1)
                eng.wait_ge(decay_in, f.next(decay_in))
                a.activation(scores[:, 0, :], scores[:, 0, :], ACT.Exp, scale=-1.0).then_inc(f.count(scalar_step), 1)
                eng.wait_ge(f.last, f.now(f.last))
                a.activation(dtabs, dtabs, ACT.Ln, bias=one).then_inc(f.count(dt_ln), 1)
                a.activation(scores[:, 0, :], scores[:, 0, :], ACT.Ln, bias=one).then_inc(f.count(decay_ln), 1)
                eng.wait_ge(cum_ready, f.next(cum_ready))
                a.activation(probs[:, 1, :], probs[:, 0, :], ACT.Exp).then_inc(f.count(scalar_step), 1)
                a.activation(scores[:, 0, :], probs[:, 0, :], ACT.Exp, scale=-1.0).then_inc(f.count(scalar_step), 1)
                a.activation(scores[:, 1, :], scores[:, 1, :], ACT.Exp).then_inc(f.count(cum_exp), 1)
                for j in range(2):
                    take(4 + j, osq[:, 2 * j:2 * j + 2, :])
                eng.wait_ge(f.last, f.now(f.last))
                a.activation(osq, osq, ACT.Sqrt, bias=eps2, scale=float(D // P)).then_inc(f.count(normed_std), 1)
                eng.wait_ge(seg_ready, f.next(seg_ready))
                a.activation(flat[:, CH:2 * CH], flat[:, CH:2 * CH], ACT.Exp).then_inc(f.count(scalar_step), 1)
                a.activation(ecum, cumr[:, 1024:2048], ACT.Exp).then_inc(f.count(scalar_step), 1)
                a.activation(wtail, wtail, ACT.Exp).then_inc(f.count(seg_exp), 1)
                take(4, std[:, :], bank[4][:, 0:TOK])
                eng.wait_ge(f.last, f.now(f.last))
                a.activation(std[:, :], std[:, :], ACT.Sqrt, bias=eps2, scale=2.0).then_inc(f.count(normed_std), 1)
                norm(eps2, xT[:, :, :], x_ready)
                if l == 0:
                    ffn_steps(up, lambda p, i: None, FF2 // CW, eng, FFN2_TRIP, f)
                else:
                    eng.wait_ge(route_in, f.next(route_in))
                    a.activation(pair[:, 0:2], pair[:, 0:2], ACT.Exp).then_inc(f.count(pair_exp), 1)
                    for q in range(4):
                        take(4 + q, htok[:, q // 2, 512 * (q % 2):512 * (q % 2) + 512], bank[4 + q][:, :])

                    def up_slots(p, i):
                        eng.wait_ge(gate_full[p], f.next(gate_full[p]))
                        a.activation(silu[:, p, :, 0:P], tiles(bank[2 * p][:, 0:2 * P], 2), ACT.Silu).then_inc(f.count(silu_ready[p]), 1)

                    def experts():
                        for q in range(2):
                            take(6 + q, xe[:, 4 * q:4 * q + 4, :], tiles(bank[6 + q][:, :], 4))
                        with f.trips(EXPERTS, EXPERT):
                            ffn_steps(up_slots, lambda p, i: None, FF2 // CW, eng, FFN3_TRIP, f)
                            eng.wait_ge(back_full, f.next(back_full))
                            a.copy(back, bank[0][:, 0:TOK]).then_inc(f.count(back_free), 1)
                            for n in range(2):
                                take(4 + n, ye[:, n * 512:(n + 1) * 512], bank[4 + n][:, :])
                            for q in range(2):
                                take(6 + q, xe[:, 4 * q:4 * q + 4, :], tiles(bank[6 + q][:, :], 4))

                    experts()
                    eng.wait_ge(crowd_ready, f.next(crowd_ready))
                    with eng.If(eng.value_load(crowded[0:1, 0:1], min_val=0, max_val=1) > 0):
                        experts()
            norm(eps2, xT[:, :, :], x_ready)
    if BAD:
        raise AssertionError("counts per trip differ from the tables")


def constants():
    c = np.zeros((P, C_ALL), np.float32)
    c[:, C_ID:C_ID + P] = np.eye(P)
    for m in range(P):
        if m % 64 < 32:
            c[m + 32, C_ROT + m] = -1.0
        else:
            c[m - 32, C_ROT + m] = 1.0
    inv = np.float32(10000.0) ** (-np.arange(32, dtype=np.float32) * np.float32(2.0) / np.float32(64))
    angle = np.arange(TOK, dtype=np.float32)[None, :] * inv.astype(np.float32)[:, None]
    c[:, C_COS:C_COS + TOK] = np.tile(np.cos(angle), (4, 1))
    c[:, C_SIN:C_SIN + TOK] = np.tile(np.sin(angle), (4, 1))
    j, i = np.arange(P)[:, None], np.arange(P)[None, :]
    c[:, C_TRI:C_TRI + P] = j <= i
    c[:, C_BAN:C_BAN + P] = np.where(j <= i, 0.0, NEG)
    c[:, C_DIAG:C_DIAG + P] = (j <= i) & (j // 64 == i // 64)
    q, k = np.arange(64)[:, None], np.arange(64)[None, :]
    start = np.clip(q - 8, 0, 48)
    c[:, C_WIN:C_WIN + 64] = np.tile(np.where((k >= start) & (k < start + 16), 0.0, NEG), (2, 1))
    for m in range(2):
        c[64 * m:64 * m + 64, C_HALF + m] = 1.0
    c[:, C_EPS1], c[:, C_EPS2], c[:, C_ONE] = 1e-5, 1e-6, 1.0
    c[:, C_IOTA:C_IOTA + P] = np.arange(1, P + 1)
    return c


def columns(vector):
    v = np.asarray(vector)
    return np.moveaxis(v.reshape(-1, P), 0, 1)


def rows(vector):
    return np.broadcast_to(np.asarray(vector).reshape(1, -1), (P, np.asarray(vector).size))


BIG = ["w_in", "w_branch", "w_mix_out", "xa_q", "xa_kv", "xa_o", "ffn_w_in", "ffn_w_out", "ada_w_2", "w_in_2", "gla_a_w_2",
       "w_out_2", "ffn_w_gate_2", "ffn_w_up_2", "ffn_w_down_2", "router_w_2", "moe_w_gate_2", "moe_w_up_2", "moe_w_down_2"]


def layout(i):
    arrays = {n: np.ascontiguousarray(i[n]) for n in BIG}
    arrays["xT"] = np.ascontiguousarray(np.asarray(i["x"])[0].T)
    arrays["memT"] = np.ascontiguousarray(np.asarray(i["mem"])[0].T)
    arrays["const"] = constants()
    arrays["eln"] = np.concatenate([columns(i["emb_ln_g"]), columns(i["emb_ln_b"]), columns(i["c_2"])], axis=1)
    arrays["fin"] = np.ascontiguousarray(columns(i["final_norm_w_2"]))
    par1 = np.zeros((DEPTH, P, A_ALL), np.float32)
    par2 = np.zeros((DEPTH, P, B_ALL), np.float32)
    for l in range(DEPTH):
        init = 0.8 - 0.6 * math.exp(-0.3 * l)
        taps = np.concatenate([np.asarray(i["ffn_conv_w"])[l], np.asarray(i["ffn_conv_b"])[l][None]], axis=0)
        par1[l, :, A_LNG:A_LNG + 24] = columns(np.asarray(i["ln_g"])[l])
        par1[l, :, A_LNB:A_LNB + 24] = columns(np.asarray(i["ln_b"])[l])
        par1[l, :, A_SUB:A_SUB + 1] = columns(np.asarray(i["subln_g"])[l])
        par1[l, :, A_SCW:A_SCW + 12] = columns(np.asarray(i["sc_conv_w"])[l])
        par1[l, :, A_FF:A_FF + 88] = np.moveaxis(taps.reshape(4, FF1 // P, P), (0, 1, 2), (2, 1, 0)).reshape(P, 88)
        par1[l, :, A_LAM0] = init
        par1[l, :, A_LAM1] = 1.0 - init
        for k, n in enumerate(("lam_q1", "lam_k1", "lam_q2", "lam_k2")):
            par1[l, :, A_LAMV + 64 * k:A_LAMV + 64 * k + 64] = rows(np.asarray(i[n])[l])
        for at, value in ((B_N1, columns(np.asarray(i["norm1_w_2"])[l])), (B_N2, columns(np.asarray(i["norm2_w_2"])[l])),
                          (B_ADA, columns(np.asarray(i["ada_b_2"])[l])), (B_AB, columns(np.asarray(i["gla_a_b_2"])[l])),
                          (B_GN, columns(np.asarray(i["gla_norm_w_2"])[l])), (B_CW, columns(np.asarray(i["conv_w_2"])[l])),
                          (B_CB, columns(np.asarray(i["conv_b_2"])[l])), (B_DTB, rows(np.asarray(i["dt_bias_2"])[l])),
                          (B_ALOG, rows(np.asarray(i["a_log_2"])[l])),
                          (B_DS, columns(np.repeat(np.asarray(i["d_skip_2"])[l], 64))),
                          (B_SN, columns(np.asarray(i["ssd_norm_w_2"])[l]))):
            par2[l, :, at:at + value.shape[1]] = value
    arrays["par1"], arrays["par2"] = par1, par2
    rpb = np.zeros((DEPTH, 8, 7, 127), np.float32)
    rpb[..., 48:79] = np.asarray(i["rpb"])[:, :, 4:11, :]
    arrays["rpb"] = rpb
    return {n: np.ascontiguousarray(a) for n, a in arrays.items()}


def kernel(**inputs):
    import concourse.bacc as bacc
    from concourse.bass_utils import run_bass_kernel_spmd as run

    nc = bacc.Bacc("TRN2", target_bir_lowering=False, num_devices=1)
    arrays = layout(inputs)
    io = {n: nc.dram_tensor(f"in_{n}", a.shape, F32, kind="ExternalInput").ap() for n, a in arrays.items()}
    io["out"] = nc.dram_tensor("outT", (D, TOK), F32, kind="ExternalOutput").ap()
    io["windows"] = nc.dram_tensor("windows", (DEPTH, 64, 8, 7, 127), F32, kind="Internal").ap()
    program(nc, io)
    r = run(nc, [{f"in_{n}": a for n, a in arrays.items()}], core_ids=[0])
    return np.ascontiguousarray(r.results[0]["outT"].T)[None]
```

```python
import math
from contextlib import ExitStack, contextmanager

import numpy as np

import concourse.bass as bass
from concourse import mybir

F32 = mybir.dt.float32
F32R = mybir.dt.float32r
ALU = mybir.AluOpType
ACT = mybir.ActivationFunctionType
AX = mybir.AxisListType

P = 128
TOK = 256
D = 1024
KD = D // P
DEPTH = 2
ALPHA = (2.0 * DEPTH) ** 0.25
SLOTS = 9
CH = 2048
CW = CH // KD
FF1, FF2 = 2816, 3584
EXPERTS = 8
NEG = -1.0e30


class Follow:

    def __init__(self, eng, own, given=()):
        self.eng, self.own, self.last = eng, own, own
        self.base, self.here, self.followed = {}, {s.name: 1 for s in given}, set()

    def now(self, sem):
        return self.base.get(sem.name, 0) + self.here.get(sem.name, 0)

    def bump(self, sem, by=1):
        self.followed.add(sem.name)
        self.here[sem.name] = self.here.get(sem.name, 0) + by

    def next(self, sem, by=1):
        self.bump(sem, by)
        return self.now(sem)

    def count(self, sem):
        self.last = sem if sem is not None else self.own
        self.bump(self.last)
        return self.last

    @contextmanager
    def trips(self, n, per):
        with self.eng.Fori(0, n) as i:
            base, here = self.base, self.here
            names = set(per) | set(base) | set(here)
            start = {s: base.get(s, 0) + here.get(s, 0) for s in names}
            self.base = {s: start[s] + i * per[s] if per.get(s) else start[s] for s in names}
            self.here = {}
            yield i
            wrong = {s: self.here.get(s, 0) for s in set(self.here) | set(per)
                     if s in self.followed and per.get(s, 0) != self.here.get(s, 0)}
            if wrong:
                BAD.append((per, wrong))
        self.base, self.here = base, {s: here.get(s, 0) + n * per.get(s, 0) for s in set(per) | set(here)}


C_ID, C_ROT, C_COS, C_SIN, C_TRI, C_BAN, C_DIAG, C_WIN, C_HALF, C_EPS1, C_EPS2, C_ONE, C_IOTA = (
    0, 128, 256, 512, 768, 896, 1024, 1152, 1216, 1218, 1219, 1220, 1221)
C_ALL = C_IOTA + P
A_LNG, A_LNB, A_SUB, A_SCW, A_FF, A_LAM0, A_LAM1, A_LAMV = 0, 24, 48, 49, 61, 149, 150, 151
A_ALL = A_LAMV + 256
B_N1, B_N2, B_ADA, B_AB, B_GN, B_CW, B_CB, B_DTB, B_ALOG, B_DS, B_SN = 0, 8, 16, 64, 66, 67, 91, 97, 105, 113, 117
B_ALL = B_SN + 4

LAYER1 = {
    "act_hi_ready0": 6, "act_hi_ready1": 5, "act_ready0": 6, "act_ready1": 5, "bank_free0": 24, "bank_free1": 24,
    "bank_free2": 31, "bank_free3": 31, "bank_free4": 11, "bank_free5": 11, "bank_free6": 6, "bank_free7": 6,
    "bank_full0": 24, "bank_full1": 24, "bank_full2": 31, "bank_full3": 31, "bank_full4": 11, "bank_full5": 11,
    "bank_full6": 6, "bank_full7": 6, "bias_in": 256, "centred": 3, "conv_ready0": 6, "conv_ready1": 5, "down_done": 11,
    "exp_ready": 20, "ffn_loaded0": 96, "ffn_loaded1": 96, "ffn_loaded2": 96, "ffn_loaded3": 80, "ffn_loaded4": 80,
    "ffn_loaded5": 80, "ffn_summed": 1, "gate_full0": 6, "gate_full1": 5, "gates_ready": 1, "heads_ready": 1,
    "hi_ready0": 17, "hi_ready1": 16, "lam_dot": 1, "lam_exp": 1, "lo_ready0": 17, "lo_ready1": 16, "mean_ready": 3,
    "merged_ready": 1, "mixer_in": 1, "par_in": 16, "peak_ready": 20, "probs_ready": 20, "product_ready0": 6,
    "product_ready1": 5, "silu_ready0": 6, "silu_ready1": 5, "squares_ready": 3, "std_ready": 3, "sub_squares": 1,
    "sub_std": 1, "up_full0": 6, "up_full1": 5, "var_ready": 3, "vector_step": 158, "w_loaded0": 160, "w_loaded1": 160,
    "w_loaded2": 160, "w_loaded3": 160, "w_loaded4": 160, "w_loaded5": 144, "w_loaded6": 144, "w_loaded7": 144,
    "w_loaded8": 144, "w_used0": 16, "w_used1": 16, "w_used2": 16, "w_used3": 15, "w_used4": 15, "w_used5": 14,
    "w_used6": 9, "w_used7": 9, "w_used8": 9, "x_hi_ready": 2, "x_lo_ready": 1, "x_ready": 3, "y_ready": 1,}
FFN1_TRIP = {
    "act_hi_ready0": 1, "act_hi_ready1": 1, "act_ready0": 1, "act_ready1": 1, "conv_ready0": 1, "conv_ready1": 1,
    "down_done": 2, "ffn_loaded0": 16, "ffn_loaded1": 16, "ffn_loaded2": 16, "ffn_loaded3": 16, "ffn_loaded4": 16,
    "ffn_loaded5": 16, "gate_full0": 1, "gate_full1": 1, "hi_ready0": 3, "hi_ready1": 3, "lo_ready0": 3, "lo_ready1": 3,
    "product_ready0": 1, "product_ready1": 1, "silu_ready0": 1, "silu_ready1": 1, "up_full0": 1, "up_full1": 1,
    "vector_step": 12, "w_used0": 1, "w_used1": 1, "w_used2": 1, "w_used3": 1, "w_used4": 1, "w_used5": 1,}
FFN2_TRIP = {
    "act_hi_ready0": 1, "act_hi_ready1": 1, "act_ready0": 1, "act_ready1": 1, "down_done": 2, "ffn_loaded0": 16,
    "ffn_loaded1": 16, "ffn_loaded2": 16, "ffn_loaded3": 16, "ffn_loaded4": 16, "ffn_loaded5": 16, "gate_full0": 1,
    "gate_full1": 1, "hi_ready0": 3, "hi_ready1": 3, "lo_ready0": 3, "lo_ready1": 3, "product_ready0": 1,
    "product_ready1": 1, "silu_ready0": 1, "silu_ready1": 1, "up_full0": 1, "up_full1": 1, "w_used0": 1, "w_used1": 1,
    "w_used2": 1, "w_used3": 1, "w_used4": 1, "w_used5": 1,}
FFN3_TRIP = {
    "act_hi_ready0": 1, "act_hi_ready1": 1, "act_ready0": 1, "act_ready1": 1, "down_done": 2, "ffn_loaded0": 16,
    "ffn_loaded1": 16, "ffn_loaded2": 16, "ffn_loaded3": 16, "ffn_loaded4": 16, "ffn_loaded5": 16, "gate_full0": 1,
    "gate_full1": 1, "hi_ready0": 2, "hi_ready1": 2, "hi_ready2": 2, "lo_ready0": 2, "lo_ready1": 2, "lo_ready2": 2,
    "silu_ready0": 1, "silu_ready1": 1, "turn_ready0": 1, "turn_ready1": 1, "turned0": 1, "turned1": 1, "up_full0": 1,
    "up_full1": 1, "w_used0": 1, "w_used1": 1, "w_used2": 1, "w_used3": 1, "w_used4": 1, "w_used5": 1,}
EXPERT = {
    "act_hi_ready0": 7, "act_hi_ready1": 7, "act_ready0": 7, "act_ready1": 7, "back_free": 1, "back_full": 1,
    "bank_free4": 1, "bank_free5": 1, "bank_full4": 1, "bank_full5": 1, "down_done": 14, "ffn_loaded0": 112,
    "ffn_loaded1": 112, "ffn_loaded2": 112, "ffn_loaded3": 112, "ffn_loaded4": 112, "ffn_loaded5": 112, "gate_full0": 7,
    "gate_full1": 7, "gather_free": 2, "gather_full": 2, "gather_hi": 2, "hi_ready0": 14, "hi_ready1": 14, "hi_ready2": 14,
    "lo_ready0": 14, "lo_ready1": 14, "lo_ready2": 14, "result_free": 4, "result_full": 4, "select_ready": 1,
    "silu_ready0": 7, "silu_ready1": 7, "turn_ready0": 7, "turn_ready1": 7, "turned0": 7, "turned1": 7, "up_full0": 7,
    "up_full1": 7, "vector_step": 8, "w_used0": 7, "w_used1": 7, "w_used2": 7, "w_used3": 7, "w_used4": 7, "w_used5": 7,}
BAD = []


def program(nc, io):
    w_in, w_branch, w_mix, xa_q, xa_kv, xa_o, ffn_in, ffn_out = (
        io[n] for n in ("w_in", "w_branch", "w_mix_out", "xa_q", "xa_kv", "xa_o", "ffn_w_in", "ffn_w_out"))

    with ExitStack() as ctx:
        def sb(name, *shape, dt=F32):
            return ctx.enter_context(nc.sbuf_tensor(name, [P, *shape], dt))

        def sem(name):
            return ctx.enter_context(nc.semaphore(name))

        def tiles(ap, k):
            return ap.rearrange("p (k t) -> p k t", k=k)

        def spread(ap, k):
            return ap.rearrange("p (o t) -> p o t", o=1).broadcast_to([P, k, ap.shape[1]])

        ring_head = sb("ring_head", 6, CH)
        xT = sb("xT", KD, TOK)
        work = sb("work", 2 * CH)
        yT = tiles(work[:, 0:CH], KD)
        merged = tiles(work[:, CH:2 * CH], KD)
        bias = work[:, 0:3072].rearrange("p (h j c) -> p h j c", h=8, j=6)
        memT = sb("memT", KD, TOK)
        kb = sb("kb", 4, TOK)
        gates = sb("gates", 24, TOK)
        flat = gates[:, :, :].rearrange("p n t -> p (n t)")
        squares = tiles(flat[:, 0:CH], KD)
        conva, silu, act = (flat[:, i * 1024:(i + 1) * 1024].rearrange("p (b j t) -> p b j t", b=2, j=2) for i in range(3))
        scores = sb("scores", 2, 512)
        probs = sb("probs", 2, 512)
        const = sb("const", C_ALL)
        ones = sb("ones", P)
        zeros = sb("zeros", 512, dt=mybir.dt.bfloat16)
        par = sb("par", A_ALL)
        par2 = [par[:, l * B_ALL:(l + 1) * B_ALL] for l in range(DEPTH)]
        std = sb("std", TOK)
        peak = sb("peak", 2, 2)
        total = sb("total", 2, 2)
        lam = sb("lam", 8)
        ffp = sb("ffp", 8)
        eln = sb("eln", 24)
        cond = sb("cond", KD)
        mod = sb("mod", 48)
        mods = sb("mods", DEPTH, 48)
        gain = sb("gain", KD)
        small = sb("small", 64)
        dta, route, second = (sb(n, 2, 8) for n in ("dta", "route", "second"))
        cumt = sb("cumt", 24)
        flag = sb("flag", SLOTS + 10)
        place = sb("place", 16, dt=mybir.dt.uint32)
        chosen = sb("chosen", 2, 8)
        picks = sb("picks", EXPERTS + 1, 4)
        pick = sb("pick", 2, 4)
        crowd = sb("crowd", 8)
        crowded = sb("crowded", 1, dt=mybir.dt.int32)
        def in_scope(scope, name, *shape, dt=F32):
            return scope.enter_context(nc.sbuf_tensor(name, [P, *shape], dt))

        with ExitStack() as loads:
            ring_tail = in_scope(loads, "ring_tail", SLOTS - 6, CH)
            with ExitStack() as mixer:
                qa, ka, qb, gb, gc, hc = (in_scope(mixer, n, 4, TOK) for n in ("qa", "ka", "qb", "gb", "gc", "hc"))
                va, vb = (in_scope(mixer, n, 2, 512) for n in ("va", "vb"))
                qhalf = [[in_scope(mixer, f"qhalf{a}{m}", 4, TOK) for m in range(2)] for a in range(2)]
                probsT = in_scope(mixer, "probsT", 2, 2, 2, TOK)
            with ExitStack() as ffns:
                w_hi, w_lo = (in_scope(ffns, n, 2, CH, dt=F32R) for n in ("w_hi", "w_lo"))
                x_hi, x_lo = (in_scope(ffns, n, KD, TOK, dt=F32R) for n in ("x_hi", "x_lo"))
                act_hi, act_lo = (in_scope(ffns, n, 2, 2, TOK, dt=F32R) for n in ("act_hi", "act_lo"))
        ew_hi, ew_lo = (sb(n, 3, CH, dt=F32R) for n in ("ew_hi", "ew_lo"))
        xe_hi, xe_lo = (sb(n, KD, P, dt=F32R) for n in ("xe_hi", "xe_lo"))
        eact_hi, eact_lo = (sb(n, 2, 2, P, dt=F32R) for n in ("eact_hi", "eact_lo"))

        def ring(s):
            return ring_head[:, s, :] if s < 6 else ring_tail[:, s - 6, :]

        ident = const[:, C_ID:C_ID + P]
        rot = const[:, C_ROT:C_ROT + P]
        tri = const[:, C_TRI:C_TRI + P]
        half = [const[:, C_HALF + m:C_HALF + m + 1] for m in range(2)]
        eps1, eps2, one = (const[:, c:c + 1] for c in (C_EPS1, C_EPS2, C_ONE))
        bank = [ctx.enter_context(nc.psum_tensor(f"bank{b}", [P, 512], F32)) for b in range(8)]


        alr = scores[:, 1, 0:TOK]
        half_kv = probsT[:, :, :, :, :].rearrange("p a b c t -> p (a b c t)")
        qe = [tiles(half_kv[:, 512 * m:512 * m + 512], 2) for m in range(2)]
        ke, ktail = (tiles(half_kv[:, c:c + 512], 2) for c in (1024, 1536))
        ktok = [hc[:, 2 * m:2 * m + 2, :] for m in range(2)]
        att = flat[:, 4096:5120].rearrange("p (a h t) -> p a h t", a=2, h=4)
        states = work[:, 0:768].rearrange("p (n j v) -> p n j v", n=3, j=2)
        cmg, btok, state = tiles(work[:, 768:1280], 2), work[:, 1280:1408], work[:, 1408:1920]
        osq = memT[:, 4:8, :]
        cme = memT[:, 0:4, :].rearrange("p k t -> p (k t)").rearrange("p (h t) -> p h t", h=8)
        cumr, ecum = flat[:, 0:CH], flat[:, 5120:6144]
        seg = flat[:, CH:2 * CH].rearrange("p (c h t) -> p c h t", c=2, h=8)
        xw = kb[:, 0:2, :].rearrange("p k t -> p (k t)")
        dtraw, dtabs, dt, aexp, wtail = (small[:, c:c + n] for c, n in ((0, 16), (16, 16), (32, 16), (48, 8), (56, 8)))
        logit, best, placef, pair = small[:, 0:16], small[:, 16:32], small[:, 32:48], small[:, 48:56]

        htok = work[:, CH:2 * CH].rearrange("p (t d) -> p t d", t=2)
        ye = memT[:, 4:8, :].rearrange("p k t -> p (k t)")
        select, weigh = (tiles(kb[:, i, :], 2) for i in range(2))
        back = kb[:, 2, :]
        slots = const[:, C_IOTA:C_IOTA + P]

        w_loaded = [sem(f"w_loaded{s}") for s in range(SLOTS)]
        w_used = [sem(f"w_used{s}") for s in range(SLOTS)]
        bank_full = [sem(f"bank_full{b}") for b in range(8)]
        bank_free = [sem(f"bank_free{b}") for b in range(8)]
        tensor_step, vector_step, scalar_step, pool_step = (sem(n + "_step") for n in ("tensor", "vector", "scalar", "pool"))
        inputs_in, par_in, bias_in, par2_in = sem("inputs_in"), sem("par_in"), sem("bias_in"), sem("par2_in")
        windows_out = sem("windows_out")
        x_ready, y_ready, mean_ready, centred = sem("x_ready"), sem("y_ready"), sem("mean_ready"), sem("centred")
        squares_ready, var_ready, std_ready = sem("squares_ready"), sem("var_ready"), sem("std_ready")
        mixer_in, peak_ready, exp_ready, probs_ready = (
            sem("mixer_in"), sem("peak_ready"), sem("exp_ready"), sem("probs_ready"))
        heads_ready, merged_ready, lam_dot, lam_exp = sem("heads_ready"), sem("merged_ready"), sem("lam_dot"), sem("lam_exp")
        sub_raw, sub_squares, sub_std, gates_ready = sem("sub_raw"), sem("sub_squares"), sem("sub_std"), sem("gates_ready")
        cond_ready = sem("cond_ready")
        gate_full, up_full, conv_ready, silu_ready, act_ready = (
            [sem(f"{n}{i}") for i in range(2)] for n in ("gate_full", "up_full", "conv_ready", "silu_ready", "act_ready"))
        ffn_loaded = [sem(f"ffn_loaded{s}") for s in range(6)]
        hi_ready, lo_ready = ([sem(f"{n}{i}") for i in range(3)] for n in ("hi_ready", "lo_ready"))
        down_done, x_hi_ready, x_lo_ready = sem("down_done"), sem("x_hi_ready"), sem("x_lo_ready")
        product_ready, act_hi_ready, turn_ready, turned = (
            [sem(f"{n}{i}") for i in range(2)] for n in ("product_ready", "act_hi_ready", "turn_ready", "turned"))
        gather_full, gather_hi, gather_free = sem("gather_full"), sem("gather_hi"), sem("gather_free")
        ffn_summed, out_done = sem("ffn_summed"), sem("out_done")
        alr_ready, decay_in, decay_exp, decay_ln, cum_ready, cum_exp, gla_in = (sem(n) for n in (
            "alr_ready", "decay_in", "decay_exp", "decay_ln", "cum_ready", "cum_exp", "gla_in"))
        tails_ready, att_ready, states_ready, raw_ready, normed_sq, normed_std = (sem(n) for n in (
            "tails_ready", "att_ready", "states_ready", "raw_ready", "normed_sq", "normed_std"))
        conv_in, conv_silu, dt_abs, dt_ln, dta_ready, seg_ready, seg_exp, ssd_in, state_in = (sem(n) for n in (
            "conv_in", "conv_silu", "dt_abs", "dt_ln", "dta_ready", "seg_ready", "seg_exp", "ssd_in", "state_in"))
        back_full, back_free, result_full, result_free = (sem(n) for n in ("back_full", "back_free", "result_full", "result_free"))
        proj_ready, pair_exp, pair_ready, route_in, chosen_ready, crowd_ready, select_ready, final_step = (sem(n) for n in (
            "proj_ready", "pair_exp", "pair_ready", "route_in", "chosen_ready", "crowd_ready", "select_ready", "final_step"))

        free = w_used + bank_free + [result_free, down_done]

        block = ctx.enter_context(nc.Block())

        def kpn(w):
            return w.rearrange("(k p) n -> p k n", p=P)

        cuts = [[(0, 256)], [(256, 256)], [(512, 256)], [(768, 256)], [(1024, 256)], [(1280, 256)], [(1552, 256)],
                [(1808, 256)], [(2064, 256)], [(2320, 256)], [(2576, 256)], [(1536, 16), (2832, 8)]]

        def ffn_steps(up, down, n, engine, per, f):
            up(0, 0)
            with f.trips((n - 1) // 2, per) as i:
                up(1, 2 * i + 1)
                down(0, 2 * i)
                up(0, 2 * i + 2)
                down(1, 2 * i + 1)
            if n % 2 == 0:
                up(1, n - 1)
                down(0, n - 2)
            down((n - 1) % 2, n - 1)

        def dense_steps(split, form, finish, n, engine, per, f):
            with f.trips((n - 1) // 2, per) as i:
                form(0, 2 * i)
                split(3, 0, 1)
                finish(0)
                split(4, 1, 5)
                split(2, 0, 3)
                form(1, 2 * i + 1)
                split(0, 1, 4)
                finish(1)
                split(1, 0, 2)
                split(5, 1, 0)
            form(0, n - 2 + n % 2)
            if n % 2 == 0:
                split(3, 0, 1)
                finish(0)
                split(4, 1, 5)
                split(2, 0, 3)
                form(1, n - 1)
                finish(1)
                split(5, 1, 4)
            else:
                finish(0)
                split(2, 0, 1)

        def expert_steps(split, form, finish, engine, f):
            split(0, 0)
            split(1, 1)
            with f.trips((FF2 // CW - 1) // 2, FFN3_TRIP):
                split(3, 2, 0)
                form(0)
                split(4, 0, 1)
                split(2, 1, 5)
                finish(0)
                split(0, 2, 3)
                form(1)
                split(1, 0, 4)
                split(5, 1, 2)
                finish(1)
            split(3, 2, 0)
            form(0)
            split(4, 0, 1)
            split(2, 1, 5)
            finish(0)

        @block.sync
        def _(sp):
            f = Follow(sp, tensor_step, free)
            turn = [0]

            def load(pieces, slot=None, ffn=False):
                s = turn[0] % SLOTS if slot is None else slot
                turn[0] += 1
                sp.wait_ge(w_used[s], f.now(w_used[s]))
                f.bump(w_used[s])
                pieces = pieces if isinstance(pieces, list) else [pieces]
                k, n = pieces[0].shape[1], sum(piece.shape[2] for piece in pieces)
                dst = tiles(ring(s)[:, 0:k * n], k)
                at = 0
                for piece in pieces:
                    sp.dma_start(dst[:, :, at:at + piece.shape[2]], piece).then_inc(ffn_loaded[s] if ffn else w_loaded[s], 16)
                    at += piece.shape[2]

            def ffn(gate, up_w, down_w, n, per):
                def up(p, i):
                    load(up_w(i), 3 * p + 1, True)
                    load(gate(i), 3 * p, True)

                def down(p, i):
                    load(down_w(i), 3 * p + 2, True)

                ffn_steps(up, down, n, sp, per, f)

            with f.trips(DEPTH, LAYER1) as l:
                turn[0] = 0
                for c in range(18):
                    load(kpn(w_in[l])[:, :, c * CW:(c + 1) * CW])
                for u in range(16):
                    if u < 12:
                        load(kpn(w_in[l])[:, :, (18 + u) * CW:(19 + u) * CW])
                    load(kpn(io["ada_w_2"][l])[:, :, u * CW:(u + 1) * CW])
                for n in range(4):
                    for b in range(3):
                        load(kpn(w_branch[l, b])[:, :, n * CW:(n + 1) * CW])
                for n in range(4):
                    load(kpn(w_mix[l])[:, :, n * CW:(n + 1) * CW])
                for n in range(8):
                    load(kpn(xa_kv[l])[:, :, n * CW:(n + 1) * CW])
                for n in range(4):
                    load(kpn(xa_q[l])[:, :, n * CW:(n + 1) * CW])
                for u in range(8):
                    load(kpn(io["ada_w_2"][l])[:, :, (16 + u) * CW:(17 + u) * CW])
                for n in range(4):
                    load(kpn(xa_o[l])[:, :, n * CW:(n + 1) * CW])
                ffn(lambda i: kpn(ffn_in[l])[:, :, bass.ds(i * CW + FF1, CW)],
                    lambda i: kpn(ffn_in[l])[:, :, bass.ds(i * CW, CW)],
                    lambda i: kpn(ffn_out[l, bass.ds(i * CW, CW), :]), FF1 // CW, FFN1_TRIP)
            for l in range(DEPTH):
                turn[0] = 0
                for cut in cuts:
                    load([kpn(io["w_in_2"][l])[:, :, c:c + n] for c, n in cut])
                for n in range(4):
                    load(kpn(io["w_out_2"][l])[:, :, n * CW:(n + 1) * CW])
                names = [("ffn_w_gate_2", "ffn_w_up_2", "ffn_w_down_2"), ("moe_w_gate_2", "moe_w_up_2", "moe_w_down_2")][l]
                wg, wu, wd = (io[n] for n in names)
                if l == 0:
                    ffn(lambda i: kpn(wg[0])[:, :, bass.ds(i * CW, CW)], lambda i: kpn(wu[0])[:, :, bass.ds(i * CW, CW)],
                        lambda i: kpn(wd[0, bass.ds(i * CW, CW), :]), FF2 // CW, FFN2_TRIP)
                else:
                    load(kpn(io["router_w_2"][0]))
                    def experts():
                        with f.trips(EXPERTS, EXPERT) as e:
                            ffn(lambda i: kpn(wg[0, e])[:, :, bass.ds(i * CW, CW)],
                                lambda i: kpn(wu[0, e])[:, :, bass.ds(i * CW, CW)],
                                lambda i: kpn(wd[0, e, bass.ds(i * CW, CW), :]), FF2 // CW, FFN3_TRIP)

                    experts()
                    sp.wait_ge(crowd_ready, f.next(crowd_ready))
                    with sp.If(sp.value_load(crowded[0:1, 0:1], min_val=0, max_val=1) > 0):
                        experts()

        @block.gpsimd
        def _(pool):
            f = Follow(pool, pool_step)
            for i, s in enumerate(free):
                pool.memset(flag[0:1, i:i + 1], 0.0).then_inc(s, 1)
            pool.memset(ones[:, :], 1.0 / D)
            pool.memset(zeros[:, :], 0.0).then_inc(f.count(pool_step), 1)
            for dst, src in ((const[:, :], io["const"]), (eln[:, :], io["eln"]),
                             (yT, kpn(io["xT"])), (memT[:, :, :], kpn(io["memT"]))):
                pool.dma_start(dst, src).then_inc(inputs_in, 16)
            for l in range(DEPTH):
                src = io["rpb"][l].rearrange("h j i -> (h j i)")
                pool.dma_start(io["windows"][l].rearrange("c h j i -> c (h j i)"),
                               bass.AP(src.tensor, src.offset, [[0, 64], [1, 8 * 7 * 127]])).then_inc(windows_out, 16)
            pool.wait_ge(windows_out, 16 * DEPTH)
            with f.trips(DEPTH, LAYER1) as l:
                pool.wait_ge(x_ready, f.now(x_ready) + 1)
                f.bump(x_ready, 3)
                pool.dma_start(par[:, :], io["par1"][l]).then_inc(par_in, 16)
                for side in range(2):
                    for h in range(8):
                        at = io["windows"][l, :, h, 1 - side:7 - side, 63:127]
                        src = bass.AP(at.tensor, at.offset, [[8 * 7 * 127 - 1, 64], [127, 6], [1, 64]])
                        pool.dma_start(bias[64 * side:64 * side + 64, h], src).then_inc(bias_in, 16)
            pool.wait_ge(x_ready, f.now(x_ready) + 1)
            f.bump(x_ready)
            for l in range(DEPTH):
                pool.dma_start(par2[l], io["par2"][l]).then_inc(par2_in, 16)
                pool.dma_start(kb[0:16, 2 + l, :], io["gla_a_w_2"][l]).then_inc(par2_in, 16)
            f.bump(x_ready, 2 * DEPTH)
            pool.dma_start(eln[:, 0:8], io["fin"]).then_inc(par2_in, 16)
            pool.wait_ge(y_ready, 2 + 2 * DEPTH + 1)
            pool.dma_start(kpn(io["out"]), yT).then_inc(out_done, 16)
            pool.wait_ge(out_done, 16)

        @block.tensor
        def _(pe):
            f = Follow(pe, tensor_step, free)
            turn, spent = [0], []

            def mm(out, lhsT, rhs, start, stop, done=None, **kw):
                ins = nc.tensor.matmul(out, lhsT, rhs, start=start, stop=stop, **kw)
                if done is not None:
                    ins.then_inc(f.count(done), 1)
                elif spent:
                    ins.then_inc(f.count(w_used[spent.pop()]), 1)

            def chunk(k=KD, n=CW, slot=None, pieces=1):
                s = turn[0] % SLOTS if slot is None else slot
                turn[0] += 1
                pe.wait_ge(w_loaded[s], f.next(w_loaded[s], 16 * pieces))
                return tiles(ring(s)[:, 0:k * n], k), s

            def open_bank(b):
                pe.wait_ge(bank_free[b], f.now(bank_free[b]))
                f.bump(bank_free[b])

            def by_features(b, x, w, k, done):
                for j in range(2):
                    for t in range(k):
                        mm(bank[b][:, j * TOK:(j + 1) * TOK], w[:, t, j * P:(j + 1) * P], x[:, t, :],
                           t == 0, t == k - 1, done if (j, t) == (1, k - 1) else None)

            def features(b, x, k=KD):
                w, s = chunk(k)
                open_bank(b)
                by_features(b, x, w, k, bank_full[b])
                spent.append(s)

            def tokens(b, x):
                w, s = chunk()
                open_bank(b)
                for j in range(2):
                    for t in range(KD):
                        mm(bank[b][:, j * CW:(j + 1) * CW], x[:, t, j * P:(j + 1) * P], w[:, t, :],
                           t == 0, t == KD - 1, bank_full[b] if (j, t) == (1, KD - 1) else None)
                spent.append(s)

            def modulation(b):
                w, s = chunk()
                open_bank(b)
                for j in range(2):
                    for t in range(KD):
                        mm(bank[b][:, j:j + 1], w[:, t, j * P:(j + 1) * P], cond[:, t:t + 1],
                           t == 0, t == KD - 1, bank_full[b] if (j, t) == (1, KD - 1) else None)
                spent.append(s)

            def taken(b):
                pe.wait_ge(bank_free[b], f.now(bank_free[b]))

            def norm_mean():
                for t in range(KD):
                    mm(bank[5][:, 0:TOK], ones[:, :], yT[:, t, :], t == 0, t == KD - 1,
                       mean_ready if t == KD - 1 else None)

            def norm_var():
                pe.wait_ge(squares_ready, f.next(squares_ready))
                for t in range(KD):
                    mm(bank[4][:, 0:TOK], ones[:, :], squares[:, t, :], t == 0, t == KD - 1,
                       var_ready if t == KD - 1 else None)

            def turn_probs(u, n):
                pe.wait_ge(probs_ready, f.next(probs_ready))
                b = 4 + u % 2
                open_bank(b)
                for i in range(n):
                    ins = nc.tensor.transpose(bank[b][:, i * P:(i + 1) * P], probs[:, u % 2, i * P:(i + 1) * P], ident)
                ins.then_inc(f.count(bank_full[b]), 1)

            def probs_turned(u):
                pe.wait_ge(bank_free[4 + u % 2], f.now(bank_free[4 + u % 2]))

            def ffn(n, per):
                seq = [0]
                pe.wait_ge(x_lo_ready, f.next(x_lo_ready))
                open_sums()

                def halves(k, n):
                    h = seq[0] % 2
                    seq[0] += 1
                    pe.wait_ge(lo_ready[h], f.next(lo_ready[h]))
                    return [tiles(t[:, h, 0:k * n], k) for t in (w_hi, w_lo)]

                def up(p, i):
                    for o, full in ((0, gate_full[p]), (1, up_full[p])):
                        hi, lo = halves(KD, CW)
                        for j in range(2):
                            for t in range(KD):
                                cols, out = slice(j * P, (j + 1) * P), bank[2 * p + o][:, j * TOK:(j + 1) * TOK]
                                mm(out, hi[:, t, cols], x_hi[:, t, :], t == 0, False)
                                mm(out, hi[:, t, cols], x_lo[:, t, :], False, False)
                                mm(out, lo[:, t, cols], x_hi[:, t, :], False, t == KD - 1, full if (j, t) == (1, KD - 1) else None)
                        spent.append(3 * p + o)
                    if isinstance(i, int) and i == 0:
                        hand_back()

                def hand_back():
                    mm(bank[4][:, 0:1], zeros[0:1, 0:P], zeros[0:1, 0:1], False, False, skip_group_check=True)

                def down(p, i):
                    hi, lo = halves(2, D)
                    pe.wait_ge(act_ready[p], f.next(act_ready[p]))
                    for t in range(2):
                        for n in range(KD):
                            cols, out = slice(n * P, (n + 1) * P), bank[4 + n // 2][:, (n % 2) * TOK:(n % 2 + 1) * TOK]
                            mm(out, hi[:, t, cols], act_hi[:, p, t, :], False, False, skip_group_check=True)
                            mm(out, hi[:, t, cols], act_lo[:, p, t, :], False, False, skip_group_check=True)
                            mm(out, lo[:, t, cols], act_hi[:, p, t, :], False, False,
                               down_done if (t, n) == (1, KD - 1) else None, skip_group_check=True)
                    spent.append(3 * p + 2)
                    hand_back()

                ffn_steps(up, down, n, pe, per, f)

            def open_sums():
                for b in range(4, 8):
                    mm(bank[b][:, :], zeros[0:1, 0:P], zeros[0:1, :], True, False, skip_group_check=True)

            def close_sums():
                for b in range(4, 8):
                    mm(bank[b][:, :], zeros[0:1, 0:P], zeros[0:1, :], False, True, ffn_summed if b == 7 else None,
                       skip_group_check=True)

            pe.wait_ge(inputs_in, f.next(inputs_in, 64))
            pe.wait_ge(pool_step, f.next(pool_step))
            norm_mean()
            norm_var()
            pe.wait_ge(cond_ready, f.next(cond_ready))
            pe.wait_ge(x_ready, f.next(x_ready))
            with f.trips(DEPTH, LAYER1) as l:
                turn[0] = 0
                for c in range(18):
                    (tokens if c in (4, 5, 10, 11) else features)(c % 4, xT)
                    if c == 7:
                        for j in range(4):
                            open_bank(j)
                            mm(bank[j][:, :], rot, (qa, ka)[j // 2][:, 2 * (j % 2):2 * (j % 2) + 2, :], True, True, bank_full[j])
                pe.wait_ge(mixer_in, f.next(mixer_in))
                for u in range(18):
                    if u < 16:
                        b = u % 2
                        open_bank(b)
                        a, t, qt = u // 8, u // 2 % 4, u % 2
                        for m in range(2):
                            mm(bank[b][:, m * TOK:(m + 1) * TOK], qhalf[a][m][:, t, qt * P:(qt + 1) * P], (ka, kb)[a][:, t, :],
                               True, True, bank_full[b] if m else None)
                    if u < 12:
                        features(6 + u % 2, xT)
                    if u < 16:
                        modulation(2 + u % 2)
                    if 1 <= u <= 16:
                        turn_probs(u - 1, 2 if u - 1 < 8 else 4)
                    if u == 10:
                        pe.wait_ge(sub_squares, f.next(sub_squares))
                        for h in range(4):
                            b = 4 + h // 2
                            if h % 2 == 0:
                                open_bank(b)
                            mm(bank[b][:, (h % 2) * TOK:(h % 2 + 1) * TOK], ones[:, :], ka[:, h, :], True, True,
                               bank_full[b] if h % 2 else None)
                    if u >= 3 and u % 2 == 1:
                        n = (u - 3) // 2
                        probs_turned(u - 2)
                        b = 2 + n % 2
                        open_bank(b)
                        for m in range(1 if n < 4 else 2):
                            for t in range(2):
                                if n < 4:
                                    v, out = va[:, t, n * P:(n + 1) * P], bank[b][:, 0:TOK]
                                else:
                                    h = 2 * (n - 4) + m
                                    v, out = vb[:, t, 64 * h:64 * h + 64], bank[b][64 * m:64 * m + 64, 0:TOK]
                                mm(out, v, probsT[:, n % 2, m, t, :], t == 0, t == 1,
                                   bank_full[b] if t and (n < 4 or m) else None)
                pe.wait_ge(heads_ready, f.next(heads_ready))
                for n in range(4):
                    for br, src in enumerate((qa, qb, hc)):
                        features((3 * n + br) % 4, src, 4)
                pe.wait_ge(merged_ready, f.next(merged_ready))
                for n in range(4):
                    features(n, merged)
                for n in range(4):
                    features(n, memT)
                taken(3)
                norm_mean()
                for n in range(2):
                    tokens(n, memT)
                norm_var()
                for n in range(2):
                    tokens(2 + n, memT)
                pe.wait_ge(x_ready, f.next(x_ready))
                for n in range(4):
                    features(n, xT)
                taken(3)
                for u in range(6):
                    if u < 4:
                        b = u % 2
                        open_bank(b)
                        for m in range(2):
                            h, qt = 2 * (u // 2) + m, u % 2
                            for t in range(2):
                                mm(bank[b][:, m * TOK:(m + 1) * TOK],
                                   (qa, ka)[h // 2][:, 2 * (h % 2) + t, qt * P:(qt + 1) * P],
                                   (qb, kb)[h // 2][:, 2 * (h % 2) + t, :], t == 0, t == 1, bank_full[b] if m and t else None)
                        modulation(2)
                        modulation(3)
                    if 1 <= u <= 4:
                        turn_probs(u - 1, 4)
                    if u >= 3 and u % 2 == 1:
                        n = (u - 3) // 2
                        probs_turned(u - 2)
                        for m in range(2):
                            h, b = 2 * n + m, 2 + m
                            open_bank(b)
                            for j in range(2):
                                for t in range(2):
                                    mm(bank[b][:, j * TOK:(j + 1) * TOK],
                                       (va, vb)[n][:, t, m * TOK + j * P:m * TOK + (j + 1) * P],
                                       probsT[:, n % 2, m, t, :], t == 0, t == 1, bank_full[b] if j and t else None)
                taken(3)
                for n in range(4):
                    features(n, merged)
                taken(3)
                norm_mean()
                norm_var()
                f.bump(x_ready)
                ffn(FF1 // CW, FFN1_TRIP)
                close_sums()
                pe.wait_ge(y_ready, f.next(y_ready))
                norm_mean()
                norm_var()
                pe.wait_ge(x_ready, f.next(x_ready))

            for l in range(DEPTH):
                turn[0] = 0
                norm_var()
                pe.wait_ge(y_ready, f.next(y_ready))
                for c in range(11):
                    (tokens if c in (2, 3) else features)(c % 4, yT)
                w, s = chunk(KD, 24, pieces=2)
                open_bank(3)
                for t in range(KD):
                    mm(bank[3][0:16, 0:TOK], w[:, t, 0:16], yT[:, t, :], t == 0, t == KD - 1)
                for j in range(2):
                    for t in range(KD):
                        mm(bank[3][:, TOK + 8 * j:TOK + 8 * j + 8], yT[:, t, j * P:(j + 1) * P], w[:, t, 16:24],
                           t == 0, t == KD - 1, bank_full[3] if (j, t) == (1, KD - 1) else None)
                spent.append(s)
                taken(3)
                open_bank(0)
                for j in range(2):
                    mm(bank[0][:, j * TOK:(j + 1) * TOK], kb[0:16, 2 + l, j * P:(j + 1) * P], alr[0:16, :], True, True,
                       bank_full[0] if j else None)
                pe.wait_ge(conv_silu, f.next(conv_silu))
                for t in range(2):
                    open_bank(2 + t)
                    for j in range(4):
                        ins = nc.tensor.transpose(bank[2 + t][:, j * P:(j + 1) * P], qb[:, j, t * P:(t + 1) * P], ident)
                    ins.then_inc(f.count(bank_full[2 + t]), 1)
                open_bank(1)
                nc.tensor.transpose(bank[1][:, 0:P], ka[:, 0, 0:P], ident).then_inc(f.count(bank_full[1]), 1)
                pe.wait_ge(gla_in, f.next(gla_in))
                open_bank(1)
                for t in range(2):
                    for j in range(2):
                        ins = nc.tensor.transpose(bank[1][:, (2 * t + j) * P:(2 * t + j + 1) * P], ktail[:, j, t * P:(t + 1) * P], ident)
                ins.then_inc(f.count(bank_full[1]), 1)
                for a in range(2):
                    open_bank(2 + a)
                    for h in range(4):
                        mm(bank[2 + a][:, h * P:(h + 1) * P], ke[:, h // 2, a * P:(a + 1) * P],
                           qe[h % 2][:, h // 2, a * P:(a + 1) * P], True, True, bank_full[2 + a] if h == 3 else None)
                taken(1)
                for j in range(2):
                    open_bank(j)
                    for n in range(3):
                        for m in range(2):
                            h = 2 * j + m
                            mm(bank[j][64 * m:64 * m + 64, n * P:(n + 1) * P], ktok[n % 2][:, n // 2, h * 64:h * 64 + 64],
                               va[:, n // 2, h * P:(h + 1) * P], True, True, bank_full[j] if (n, m) == (2, 1) else None)
                for j in range(2):
                    open_bank(j)
                    for m in range(2):
                        h = 2 * j + m
                        for a in range(2):
                            at = m * TOK + a * P
                            mm(bank[j][:, at:at + P], va[:, a, h * P:(h + 1) * P], att[:, a, h, :], True, False,
                               skip_group_check=True)
                            for n in range(max(1, 2 * a), 2 * a + 2):
                                at = m * TOK + n * 64
                                mm(bank[j][:, at:at + 64], states[:, n - 1, j, :], qe[m][:, j, n * 64:n * 64 + 64],
                                   False, n == 2 * a + 1, bank_full[j] if (m, n) == (1, 3) else None, skip_group_check=True)
                pe.wait_ge(normed_sq, f.next(normed_sq))
                for j in range(2):
                    open_bank(4 + j)
                    for m in range(2):
                        mm(bank[4 + j][:, m * TOK:(m + 1) * TOK], ones[:, :], osq[:, 2 * j + m, :], True, True,
                           bank_full[4 + j] if m else None)
                pe.wait_ge(dta_ready, f.next(dta_ready))
                for q in range(4):
                    open_bank(q)
                    for i in range(4):
                        c, h = q // 2, 4 * (q % 2) + i
                        mm(bank[q][:, i * P:(i + 1) * P], dta[:, c, h:h + 1].to_broadcast([P, P]), tri, True, True,
                           bank_full[q] if i == 3 else None)
                open_bank(0)
                for c in range(2):
                    mm(bank[0][:, 8 * c:8 * c + 8], tri, dta[:, c, :], True, True)
                mm(bank[0][:, 16:24], ones[:, :], dta[:, 0, :], True, True, bank_full[0])
                pe.wait_ge(ssd_in, f.next(ssd_in))
                open_bank(1)
                for c in range(2):
                    for g in range(2):
                        mm(bank[1][:, (2 * c + g) * P:(2 * c + g + 1) * P], ka[:, 0, c * P:(c + 1) * P], cmg[:, g, c * P:(c + 1) * P],
                           True, True, bank_full[1] if (c, g) == (1, 1) else None)
                pe.wait_ge(state_in, f.next(state_in))
                open_bank(2)
                mm(bank[2][:, :], btok, xw, True, True, bank_full[2])
                pe.wait_ge(pair_ready, f.next(pair_ready))
                for j in range(2):
                    open_bank(j)
                    for i in range(2):
                        for m in range(2):
                            h = 4 * j + 2 * i + m
                            for c in range(2):
                                out = bank[j][64 * m:64 * m + 64, i * TOK + c * P:i * TOK + (c + 1) * P]
                                mm(out, vb[:, c, h * 64:h * 64 + 64], seg[:, c, h, :], True, c == 0, skip_group_check=True)
                            mm(out, state[:, h * 64:h * 64 + 64], cme[:, h, :], False, True,
                               bank_full[j] if (i, m) == (1, 1) else None, skip_group_check=True)
                pe.wait_ge(normed_sq, f.next(normed_sq))
                open_bank(4)
                for j in range(4):
                    mm(bank[4][:, 0:TOK], ones[:, :], osq[:, j, :], j == 0, j == 3, bank_full[4] if j == 3 else None)
                pe.wait_ge(merged_ready, f.next(merged_ready))
                for n in range(4):
                    features(n, merged)
                pe.wait_ge(x_ready, f.next(x_ready))
                norm_var()
                pe.wait_ge(y_ready, f.next(y_ready))
                if l == 0:
                    ffn(FF2 // CW, FFN2_TRIP)
                else:
                    w, s = chunk(KD, 8)
                    open_bank(0)
                    for j in range(2):
                        for t in range(KD):
                            mm(bank[0][:, 8 * j:8 * j + 8], yT[:, t, j * P:(j + 1) * P], w[:, t, :], t == 0, t == KD - 1,
                               bank_full[0] if (j, t) == (1, KD - 1) else None)
                    spent.append(s)
                    for q in range(4):
                        open_bank(4 + q)
                        for i in range(4):
                            ins = nc.tensor.transpose(bank[4 + q][:, i * P:(i + 1) * P],
                                                      yT[:, 4 * (q % 2) + i, (q // 2) * P:(q // 2 + 1) * P], ident)
                        ins.then_inc(f.count(bank_full[4 + q]), 1)
                    pe.wait_ge(chosen_ready, f.next(chosen_ready))
                    open_bank(0)
                    every = one.to_broadcast([P, P])
                    mm(bank[0][:, 0:8], tri, chosen[:, 0, :], True, True)
                    mm(bank[0][:, 8:16], tri, chosen[:, 1, :], True, False)
                    mm(bank[0][:, 8:16], every, chosen[:, 0, :], False, True)
                    mm(bank[0][:, 16:24], every, chosen[:, 0, :], True, False)
                    mm(bank[0][:, 16:24], every, chosen[:, 1, :], False, True, bank_full[0])

                    seq = [0]

                    def halves(k, n):
                        h = seq[0] % 3
                        seq[0] += 1
                        pe.wait_ge(lo_ready[h], f.next(lo_ready[h]))
                        return [tiles(t[:, h, 0:k * n], k) for t in (ew_hi, ew_lo)]

                    def gather(q):
                        pe.wait_ge(gather_free, f.now(gather_free))
                        for i in range(4):
                            for t in range(2):
                                k = 4 * q + i
                                mm(bank[7][:, i * P:(i + 1) * P], htok[:, t, k * P:(k + 1) * P], select[:, t, :],
                                   t == 0, t == 1, gather_full if (i, t) == (3, 1) else None)
                        f.bump(gather_free)

                    def first(slot, b, done):
                        hi, lo = halves(KD, CW)
                        for t in range(KD):
                            mm(bank[b][:, 0:CW], xe_hi[:, t, :], hi[:, t, :], t == 0, False)
                            mm(bank[b][:, 0:CW], xe_hi[:, t, :], lo[:, t, :], False, False)
                            mm(bank[b][:, 0:CW], xe_lo[:, t, :], hi[:, t, :], False, t == KD - 1, done if t == KD - 1 else None)
                        spent.append(slot)

                    def gate(p):
                        first(3 * p, 2 * p, gate_full[p])

                    def up(p):
                        first(3 * p + 1, 2 * p + 1, up_full[p])

                    def turn(p):
                        pe.wait_ge(turn_ready[p], f.next(turn_ready[p]))
                        for j in range(2):
                            ins = nc.tensor.transpose(bank[6][:, j * P:(j + 1) * P], act[:, p, j, 0:P], ident)
                        ins.then_inc(f.count(turned[p]), 1)

                    def down(p):
                        hi, lo = halves(2, D)
                        pe.wait_ge(act_ready[p], f.next(act_ready[p]))
                        for t in range(2):
                            for n in range(2):
                                cols = slice(n * 512, (n + 1) * 512)
                                mm(bank[4 + n][:, :], eact_hi[:, p, t, :], hi[:, t, cols], False, False, skip_group_check=True)
                                mm(bank[4 + n][:, :], eact_hi[:, p, t, :], lo[:, t, cols], False, False, skip_group_check=True)
                                mm(bank[4 + n][:, :], eact_lo[:, p, t, :], hi[:, t, cols], False, False,
                                   down_done if (t, n) == (1, 1) else None, skip_group_check=True)
                        spent.append(3 * p + 2)
                        mm(bank[4][:, 0:1], zeros[0:1, 0:P], zeros[0:1, 0:1], False, False, skip_group_check=True)

                    def experts():
                        pe.wait_ge(select_ready, f.next(select_ready))
                        taken(7)
                        gather(0)
                        gather(1)
                        taken(0)
                        with f.trips(EXPERTS, EXPERT):
                            seq[0] = 0
                            pe.wait_ge(gather_free, f.now(gather_free))
                            pe.wait_ge(result_free, f.now(result_free))
                            gate(0)
                            up(0)
                            for n in range(2):
                                open_bank(4 + n)
                                mm(bank[4 + n][:, :], zeros[0:1, 0:P], zeros[0:1, :], True, False, skip_group_check=True)
                            with f.trips((FF2 // CW - 1) // 2, FFN3_TRIP):
                                for p in range(2):
                                    gate(1 - p)
                                    turn(p)
                                    up(1 - p)
                                    down(p)
                            gate(1)
                            turn(0)
                            up(1)
                            pe.wait_ge(select_ready, f.next(select_ready))
                            gather(0)
                            down(0)
                            for t in range(2):
                                ins = nc.tensor.transpose(bank[0][:, t * P:(t + 1) * P], weigh[:, t, :], ident)
                            ins.then_inc(f.count(back_full), 1)
                            gather(1)
                            turn(1)
                            down(1)
                            for n in range(2):
                                mm(bank[4 + n][:, :], zeros[0:1, 0:P], zeros[0:1, :], False, True, bank_full[4 + n],
                                   skip_group_check=True)
                            pe.wait_ge(back_free, f.next(back_free))
                            for q in range(4):
                                if q % 2 == 0:
                                    taken(4 + q // 2)
                                for j in range(2):
                                    k = 2 * q + j
                                    mm(bank[q][:, j * TOK:(j + 1) * TOK], ye[:, k * P:(k + 1) * P], back, True, True,
                                       result_full if j else None)
                            f.bump(result_free, 4)

                    experts()
                    pe.wait_ge(crowd_ready, f.next(crowd_ready))
                    with pe.If(pe.value_load(crowded[0:1, 0:1], min_val=0, max_val=1) > 0):
                        experts()
                if l == 0:
                    close_sums()
                pe.wait_ge(x_ready, f.next(x_ready))
            norm_var()

        @block.vector
        def _(dve):
            f = Follow(dve, vector_step, free)
            v = nc.vector
            cos2, sin2 = (spread(const[:, c:c + TOK], 2) for c in (C_COS, C_SIN))

            def pairs(b):
                return tiles(bank[b][:, :], 2)

            def take(b, dst, src=None):
                dve.wait_ge(bank_full[b], f.next(bank_full[b]))
                v.tensor_copy(dst, pairs(b) if src is None else src).then_inc(f.count(bank_free[b]), 1)

            def norm_centre():
                dve.wait_ge(mean_ready, f.next(mean_ready))
                v.tensor_tensor(yT, yT, spread(bank[5][:, 0:TOK], KD), ALU.subtract).then_inc(f.count(centred), 1)

            def scaled_by_std(dst, src):
                dve.wait_ge(std_ready, f.next(std_ready))
                v.reciprocal(std[:, :], std[:, :]).then_inc(f.count(vector_step), 1)
                dve.wait_ge(f.last, f.now(f.last))
                v.tensor_tensor(dst, src, spread(std[:, :], KD), ALU.mult).then_inc(f.count(vector_step), 1)
                dve.wait_ge(f.last, f.now(f.last))

            def norm_finish(gains, biases):
                scaled_by_std(yT, yT)
                for k in range(KD):
                    ins = v.tensor_scalar(xT[:, k, :], yT[:, k, :], gains[:, k:k + 1], biases[:, k:k + 1], ALU.mult, ALU.add)
                ins.then_inc(f.count(x_ready), 1)

            def residual(n, b, done):
                v.scalar_tensor_tensor(yT[:, 2 * n:2 * n + 2, :], xT[:, 2 * n:2 * n + 2, :], ALPHA, pairs(b),
                                       ALU.mult, ALU.add).then_inc(f.count(done), 1)

            def peaks(u, scale, add=None):
                b = u % 2
                dve.wait_ge(bank_full[b], f.next(bank_full[b]))
                s = tiles(scores[:, b, :], 2)
                if add is None:
                    v.tensor_scalar(s, pairs(b), -scale, None, ALU.mult).then_inc(f.count(bank_free[b]), 1)
                else:
                    v.scalar_tensor_tensor(s, pairs(b), -scale, add, ALU.mult, ALU.subtract).then_inc(f.count(bank_free[b]), 1)
                dve.wait_ge(f.last, f.now(f.last))
                v.tensor_reduce(peak[:, b, :], s, AX.X, ALU.min).then_inc(f.count(peak_ready), 1)

            def normalise(u, difference):
                b = u % 2
                dve.wait_ge(exp_ready, f.next(exp_ready))
                v.reciprocal(total[:, b, :], total[:, b, :]).then_inc(f.count(vector_step), 1)
                dve.wait_ge(f.last, f.now(f.last))
                p = tiles(probs[:, b, :], 2)
                if difference:
                    v.tensor_tensor(total[:, b, 1:2], total[:, b, 1:2], lam[:, 4:5], ALU.mult).then_inc(f.count(vector_step), 1)
                    dve.wait_ge(f.last, f.now(f.last))
                    v.tensor_scalar(p[:, 1, :], p[:, 1, :], total[:, b, 1:2], None, ALU.mult).then_inc(f.count(vector_step), 1)
                    dve.wait_ge(f.last, f.now(f.last))
                    v.scalar_tensor_tensor(p[:, 0, :], p[:, 0, :], total[:, b, 0:1], p[:, 1, :], ALU.mult, ALU.add).then_inc(f.count(probs_ready), 1)
                else:
                    r = total[:, b, :].rearrange("p (m o) -> p m o", o=1).broadcast_to([P, 2, TOK])
                    v.tensor_tensor(p, p, r, ALU.mult).then_inc(f.count(probs_ready), 1)

            def split_low(s, h, last=None):
                dve.wait_ge(hi_ready[h], f.next(hi_ready[h]))
                v.tensor_tensor(w_lo[:, h, :], ring(s), w_hi[:, h, :].bitcast(F32), ALU.subtract).then_inc(f.count(lo_ready[h]), 1)

            def x_low(x):
                for q in range(2):
                    ks = slice(4 * q, 4 * q + 4)
                    dve.wait_ge(x_hi_ready, f.next(x_hi_ready))
                    v.tensor_tensor(x_lo[:, ks, :], x[:, ks, :], x_hi[:, ks, :].bitcast(F32), ALU.subtract).then_inc(f.count(x_lo_ready if q else vector_step), 1)

            def dense(form, n, per):
                split_low(1, 1)

                def finish(p):
                    dve.wait_ge(up_full[p], f.next(up_full[p]))
                    dve.wait_ge(silu_ready[p], f.next(silu_ready[p]))
                    v.tensor_tensor(act[:, p, :, :], silu[:, p, :, :], pairs(2 * p + 1), ALU.mult).then_inc(f.count(product_ready[p]), 1)
                    dve.wait_ge(act_hi_ready[p], f.next(act_hi_ready[p]))
                    v.tensor_tensor(act_lo[:, p, :, :], act[:, p, :, :], act_hi[:, p, :, :].bitcast(F32), ALU.subtract).then_inc(f.count(act_ready[p]), 1)

                dense_steps(split_low, form, finish, n, dve, per, f)

            dve.wait_ge(inputs_in, f.next(inputs_in, 64))
            norm_centre()
            norm_finish(eln[:, 0:8], eln[:, 8:16])
            with f.trips(DEPTH, LAYER1) as l:
                dve.wait_ge(par_in, f.next(par_in, 16))
                lv = par[:, A_LAMV:A_LAMV + 256].rearrange("p (a b d) -> p a b d", a=2, b=2)
                v.tensor_tensor(tiles(scores[:, 0, 0:128], 2), lv[:, :, 0, :], lv[:, :, 1, :], ALU.mult).then_inc(f.count(vector_step), 1)
                v.tensor_tensor(lam[:, 5:6], par[:, A_SUB:A_SUB + 1], par[:, A_LAM1:A_LAM1 + 1], ALU.mult).then_inc(f.count(vector_step), 1)
                dve.wait_ge(f.last, f.now(f.last))
                v.tensor_reduce(lam[:, 0:2], tiles(scores[:, 0, 0:128], 2), AX.X, ALU.add).then_inc(f.count(lam_dot), 1)
                dve.wait_ge(lam_exp, f.next(lam_exp))
                v.scalar_tensor_tensor(lam[:, 4:5], lam[:, 3:4], lam[:, 2:3], par[:, A_LAM0:A_LAM0 + 1],
                                       ALU.subtract, ALU.subtract).then_inc(f.count(vector_step), 1)
                for c in range(18):
                    b, i = c % 4, c % 2
                    if c in (6, 7):
                        dve.wait_ge(bank_full[b], f.next(bank_full[b]))
                        for m in range(2):
                            v.tensor_scalar(qhalf[1][m][:, 2 * i:2 * i + 2, :], pairs(b), half[m], None, ALU.mult).then_inc(f.count(bank_free[b] if m else vector_step), 1)
                    elif c in (4, 5, 10, 11):
                        take(b, (va if c < 6 else vb)[:, :, i * CW:(i + 1) * CW])
                    else:
                        take(b, (qa, ka, None, None, kb, None, gb, gc, hc)[c // 2][:, 2 * i:2 * i + 2, :])
                    if c == 7:
                        for j in range(4):
                            src, tmp = (qa, ka)[j // 2][:, 2 * (j % 2):2 * (j % 2) + 2, :], tiles(scores[:, 0, :], 2)
                            dve.wait_ge(bank_full[j], f.next(bank_full[j]))
                            v.tensor_tensor(tmp, pairs(j), sin2, ALU.mult).then_inc(f.count(bank_free[j]), 1)
                            v.tensor_tensor(src, src, cos2, ALU.mult).then_inc(f.count(vector_step), 1)
                            dve.wait_ge(f.last, f.now(f.last))
                            v.tensor_tensor(src, src, tmp, ALU.add).then_inc(f.count(vector_step), 1)
                            dve.wait_ge(f.last, f.now(f.last))
                            if j < 2:
                                for m in range(2):
                                    v.tensor_scalar(qhalf[0][m][:, 2 * j:2 * j + 2, :], src, half[m], None, ALU.mult).then_inc(f.count(vector_step), 1)
                dve.wait_ge(bias_in, f.next(bias_in, 256))
                wide = bias.rearrange("p h j c -> p (h j) c")
                v.tensor_tensor(wide, wide, spread(const[:, C_WIN:C_WIN + 64], 48), ALU.add).then_inc(f.count(vector_step), 1)
                dve.wait_ge(f.last, f.now(f.last))
                v.tensor_tensor(gc[:, :, :], gc[:, :, :], hc[:, :, :], ALU.mult).then_inc(f.count(mixer_in), 1)
                for u in range(18):
                    if u < 8:
                        peaks(u, 0.125)
                    elif u < 16:
                        hp, at = u // 2 - 4, 2 - 2 * (u % 2)
                        peaks(u, 0.125, bias[:, 2 * hp:2 * hp + 2, at:at + 4, :].rearrange("p h j c -> p h (j c)"))
                    if 1 <= u <= 16:
                        normalise(u - 1, u - 1 < 8)
                    if u < 16:
                        b = 2 + u % 2
                        take(b, mod[:, 2 * u:2 * u + 2], bank[b][:, 0:2])
                    if 2 <= u < 6:
                        t = u - 2
                        w = [par[:, A_SCW + 4 * k + t:A_SCW + 4 * k + t + 1] for k in range(3)]
                        dve.wait_ge(f.last, f.now(f.last))
                        v.tensor_scalar(hc[:, t, :], gc[:, t, :], w[1], None, ALU.mult).then_inc(f.count(vector_step), 1)
                        dve.wait_ge(f.last, f.now(f.last))
                        v.scalar_tensor_tensor(hc[:, t, 1:TOK], gc[:, t, 0:TOK - 1], w[0], hc[:, t, 1:TOK], ALU.mult, ALU.add).then_inc(f.count(vector_step), 1)
                        dve.wait_ge(f.last, f.now(f.last))
                        v.scalar_tensor_tensor(hc[:, t, 0:TOK - 1], gc[:, t, 1:TOK], w[2], hc[:, t, 0:TOK - 1], ALU.mult, ALU.add).then_inc(f.count(vector_step), 1)
                        dve.wait_ge(f.last, f.now(f.last))
                        v.tensor_tensor(hc[:, t, :], hc[:, t, :], gb[:, t, :], ALU.mult).then_inc(f.count(vector_step), 1)
                    if u >= 3 and u % 2 == 1:
                        n = (u - 3) // 2
                        b = 2 + n % 2
                        take(b, (qa[:, n, :] if n < 4 else qb[:, n - 4, :]), bank[b][:, 0:TOK])
                        if n < 4:
                            dve.wait_ge(f.last, f.now(f.last))
                            v.tensor_tensor(ka[:, n, :], qa[:, n, :], qa[:, n, :], ALU.mult).then_inc(f.count(sub_squares if n == 3 else vector_step), 1)
                    if u == 14:
                        dve.wait_ge(sub_std, f.next(sub_std))
                        v.reciprocal(ka[:, :, :], ka[:, :, :]).then_inc(f.count(vector_step), 1)
                dve.wait_ge(f.last, f.now(f.last))
                v.scalar_tensor_tensor(qa[:, :, :], qa[:, :, :], lam[:, 5:6], ka[:, :, :], ALU.mult, ALU.mult).then_inc(f.count(heads_ready), 1)
                dve.wait_ge(gates_ready, f.next(gates_ready))
                for n in range(4):
                    for br in range(3):
                        c = 3 * n + br
                        b = c % 4
                        dve.wait_ge(bank_full[b], f.next(bank_full[b]))
                        g = gates[:, 8 * br + 2 * n:8 * br + 2 * n + 2, :]
                        dst = merged[:, 2 * n:2 * n + 2, :] if br == 0 else tiles(scores[:, c % 2, :], 2)
                        dve.wait_ge(f.last, f.now(f.last))
                        v.tensor_tensor(dst, pairs(b), g, ALU.mult).then_inc(f.count(bank_free[b]), 1)
                        if br:
                            dve.wait_ge(f.last, f.now(f.last))
                            m = merged[:, 2 * n:2 * n + 2, :]
                            v.tensor_tensor(m, m, dst, ALU.add).then_inc(f.count(merged_ready if (n, br) == (3, 2) else vector_step), 1)
                for n in range(4):
                    dve.wait_ge(bank_full[n], f.next(bank_full[n]))
                    residual(n, n, bank_free[n])
                for n in range(4):
                    take(n, (qb, kb)[n // 2][:, 2 * (n % 2):2 * (n % 2) + 2, :])
                norm_centre()
                for n in range(2):
                    take(n, va[:, :, n * CW:(n + 1) * CW])
                norm_finish(par[:, A_LNG:A_LNG + 8], par[:, A_LNB:A_LNB + 8])
                for n in range(2):
                    take(2 + n, vb[:, :, n * CW:(n + 1) * CW])
                for n in range(4):
                    take(n, (qa, ka)[n // 2][:, 2 * (n % 2):2 * (n % 2) + 2, :])
                for u in range(6):
                    if u < 4:
                        peaks(u, 1.0 / 16)
                    if 1 <= u <= 4:
                        normalise(u - 1, False)
                    if u < 4:
                        for i in range(2):
                            c = 16 + 2 * u + i
                            take(2 + i, mod[:, 2 * c:2 * c + 2], bank[2 + i][:, 0:2])
                    if u >= 3 and u % 2 == 1:
                        for m in range(2):
                            h = 2 * ((u - 3) // 2) + m
                            take(2 + m, merged[:, 2 * h:2 * h + 2, :])
                v.tensor_copy(mods[:, bass.ds(l, 1), :], mod[:, :].rearrange("p (o c) -> p o c", o=1)).then_inc(f.count(vector_step), 1)
                for n in range(4):
                    dve.wait_ge(bank_full[n], f.next(bank_full[n]))
                    residual(n, n, bank_free[n])
                norm_centre()
                split_low(0, 0)
                norm_finish(par[:, A_LNG + 8:A_LNG + 16], par[:, A_LNB + 8:A_LNB + 16])
                x_low(xT)

                def form(p, i):
                    v.tensor_copy(ffp[:, :], par[:, bass.ds(i * 8 + A_FF, 8)]).then_inc(f.count(vector_step), 1)
                    dve.wait_ge(f.last, f.now(f.last))
                    dve.wait_ge(gate_full[p], f.next(gate_full[p]))
                    g, b = pairs(2 * p), 2 * p
                    for j in range(2):
                        v.tensor_scalar(conva[:, p, j, :], g[:, j, :], ffp[:, 4 * j + 1:4 * j + 2], ffp[:, 4 * j + 3:4 * j + 4],
                                        ALU.mult, ALU.add).then_inc(f.count(vector_step), 1)
                    dve.wait_ge(f.last, f.now(f.last))
                    for j in range(2):
                        v.scalar_tensor_tensor(conva[:, p, j, 1:TOK], g[:, j, 0:TOK - 1], ffp[:, 4 * j:4 * j + 1],
                                               conva[:, p, j, 1:TOK], ALU.mult, ALU.add).then_inc(f.count(vector_step), 1)
                    dve.wait_ge(f.last, f.now(f.last))
                    for j in range(2):
                        v.scalar_tensor_tensor(conva[:, p, j, 0:TOK - 1], g[:, j, 1:TOK], ffp[:, 4 * j + 2:4 * j + 3],
                                               conva[:, p, j, 0:TOK - 1], ALU.mult, ALU.add).then_inc(f.count(conv_ready[p] if j else vector_step), 1)

                dense(form, FF1 // CW, FFN1_TRIP)
                dve.wait_ge(ffn_summed, f.next(ffn_summed))
                for n in range(4):
                    residual(n, 4 + n, y_ready if n == 3 else None)
                norm_centre()
                norm_finish(par[:, A_LNG + 16:A_LNG + 24], par[:, A_LNB + 16:A_LNB + 24])

            def rms_finish(l, which):
                scaled_by_std(yT, xT[:, :, :])
                for k in range(KD):
                    ins = v.tensor_scalar(yT[:, k, :], yT[:, k, :], gain[:, k:k + 1],
                                          mods[:, l, 24 * which + k:24 * which + k + 1], ALU.mult, ALU.add)
                ins.then_inc(f.count(y_ready), 1)

            def rms_gain(l, which, done=None):
                v.scalar_tensor_tensor(gain[:, :], mods[:, l, 24 * which + 8:24 * which + 16], 1.0,
                                       par2[l][:, 8 * which:8 * which + 8], ALU.add, ALU.mult).then_inc(f.count(done), 1)

            def add_gated(l, which, n, b, done):
                for i in range(2):
                    k = 2 * n + i
                    v.scalar_tensor_tensor(xT[:, k, :], pairs(b)[:, i, :], mods[:, l, 24 * which + 16 + k:24 * which + 17 + k],
                                           xT[:, k, :], ALU.mult, ALU.add).then_inc(f.count(done if i else vector_step), 1)

            dve.wait_ge(par2_in, f.next(par2_in, 80))
            for l in range(DEPTH):
                v.tensor_tensor(mods[:, l, :], mods[:, l, :], par2[l][:, B_ADA:B_ADA + 48], ALU.add).then_inc(f.count(vector_step), 1)
            for l in range(DEPTH):
                p2 = par2[l]
                dve.wait_ge(f.last, f.now(f.last))
                rms_gain(l, 0)
                rms_finish(l, 0)
                dsts = [qa[:, 0:2, :], qa[:, 2:4, :], va[:, :, 0:CW], va[:, :, CW:2 * CW], gb[:, 0:2, :], gb[:, 2:4, :],
                        gc[:, 0:2, :], gc[:, 2:4, :], hc[:, 0:2, :], hc[:, 2:4, :], kb[:, 0:2, :]]
                for c, dst in enumerate(dsts):
                    take(c % 4, dst)
                dve.wait_ge(bank_full[3], f.next(bank_full[3]))
                v.tensor_tensor(tiles(dtraw, 2), tiles(bank[3][:, TOK:TOK + 16], 2), spread(p2[:, B_DTB:B_DTB + 8], 2), ALU.add).then_inc(f.count(vector_step), 1)
                dve.wait_ge(f.last, f.now(f.last))
                v.scalar_tensor_tensor(dtabs, dtraw, -1.0, dtraw, ALU.mult, ALU.max).then_inc(f.count(proj_ready), 1)
                v.tensor_copy(alr[0:16, :], bank[3][0:16, 0:TOK]).then_inc(f.count(bank_free[3]), 1)
                dve.wait_ge(f.last, f.now(f.last))
                raw = [hc[:, j, :] for j in range(4)] + [kb[:, j, :] for j in range(2)]
                dst = [qb[:, j, :] for j in range(4)] + [ka[:, j, :] for j in range(2)]
                for tap in (3, 2, 1, 0):
                    s = 3 - tap
                    for j in range(6):
                        w = p2[:, B_CW + 6 * tap + j:B_CW + 6 * tap + j + 1]
                        if s == 0:
                            ins = v.tensor_scalar(dst[j], raw[j], w, p2[:, B_CB + j:B_CB + j + 1], ALU.mult, ALU.add)
                        else:
                            ins = v.scalar_tensor_tensor(dst[j][:, s:TOK], raw[j][:, 0:TOK - s], w, dst[j][:, s:TOK], ALU.mult, ALU.add)
                    ins.then_inc(f.count(conv_in if tap == 0 else vector_step), 1)
                    dve.wait_ge(f.last, f.now(f.last))
                dve.wait_ge(bank_full[0], f.next(bank_full[0]))
                z = ka[:, 2:4, :]
                for j in range(2):
                    v.tensor_scalar(z[:, j, :], pairs(0)[:, j, :], p2[:, B_AB + j:B_AB + j + 1], None, ALU.add).then_inc(f.count(bank_free[0] if j else vector_step), 1)
                dve.wait_ge(f.last, f.now(f.last))
                v.scalar_tensor_tensor(tiles(scores[:, 0, :], 2), z, -1.0, z, ALU.mult, ALU.max).then_inc(f.count(decay_in), 1)
                dve.wait_ge(dt_ln, f.next(dt_ln))
                v.scalar_tensor_tensor(dt, dtraw, 0.0, dtabs, ALU.max, ALU.add).then_inc(f.count(vector_step), 1)
                dve.wait_ge(f.last, f.now(f.last))
                v.scalar_tensor_tensor(dta[:, :, :], tiles(dt, 2), -1.0, spread(aexp, 2), ALU.mult, ALU.mult).then_inc(f.count(dta_ready), 1)
                dve.wait_ge(decay_ln, f.next(decay_ln))
                v.scalar_tensor_tensor(z, z, 0.0, tiles(scores[:, 0, :], 2), ALU.min, ALU.subtract).then_inc(f.count(vector_step), 1)
                dve.wait_ge(f.last, f.now(f.last))
                v.tensor_scalar(z, z, 1.0 / 16, None, ALU.mult).then_inc(f.count(vector_step), 1)
                dve.wait_ge(f.last, f.now(f.last))
                run = probs[:, 0, :].rearrange("p (n c) -> p n c", c=64)
                zc = z.rearrange("p j (n c) -> p (j n) c", c=64)
                for n in range(8):
                    ins = v.tensor_tensor_scan(run[:, n, :], one.to_broadcast([P, 64]), zc[:, n, :], 0.0, ALU.mult, ALU.add)
                ins.then_inc(f.count(vector_step), 1)
                dve.wait_ge(f.last, f.now(f.last))
                v.tensor_tensor(scores[:, 1, :].rearrange("p (n c) -> p n c", c=64), run[:, :, 63:64].broadcast_to([P, 8, 64]), run,
                                ALU.subtract).then_inc(f.count(cum_ready), 1)
                dve.wait_ge(cum_exp, f.next(cum_exp))
                grow2, shrink, tail = tiles(probs[:, 1, :], 2), tiles(scores[:, 0, :], 2), tiles(scores[:, 1, :], 2)
                qs = tiles(probs[:, 0, :], 2)
                v.scalar_tensor_tensor(qs, qa[:, 0:2, :], 0.125, grow2, ALU.mult, ALU.mult).then_inc(f.count(vector_step), 1)
                v.tensor_tensor(ke, qa[:, 2:4, :], shrink, ALU.mult).then_inc(f.count(vector_step), 1)
                dve.wait_ge(f.last, f.now(f.last))
                for m in range(2):
                    v.tensor_scalar(qe[m], qs, half[m], None, ALU.mult).then_inc(f.count(vector_step), 1)
                v.tensor_tensor(ktail, qa[:, 2:4, :], tail, ALU.mult).then_inc(f.count(gla_in), 1)
                v.memset(att, 0.0).then_inc(f.count(vector_step), 1)
                for t in range(2):
                    dve.wait_ge(bank_full[2 + t], f.next(bank_full[2 + t]))
                    v.tensor_tensor(tiles(vb[:, t, :], 8), tiles(bank[2 + t][:, :], 8),
                                    dt[:, 8 * t:8 * t + 8].rearrange("p (h o) -> p h o", o=1).broadcast_to([P, 8, 64]), ALU.mult).then_inc(f.count(bank_free[2 + t]), 1)
                take(1, btok, bank[1][:, 0:P])
                dve.wait_ge(bank_full[1], f.next(bank_full[1]))
                for m in range(2):
                    v.tensor_scalar(ktok[m], pairs(1), half[m], None, ALU.mult).then_inc(f.count(bank_free[1] if m else vector_step), 1)
                allow = const[:, C_DIAG:C_DIAG + P].bitcast(mybir.dt.uint32)
                for a in range(2):
                    dve.wait_ge(bank_full[2 + a], f.next(bank_full[2 + a]))
                    v.copy_predicated(att[:, a, :, :], spread(allow, 4), tiles(bank[2 + a][:, :], 4)).then_inc(f.count(bank_free[2 + a]), 1)
                for j in range(2):
                    dve.wait_ge(bank_full[j], f.next(bank_full[j]))
                    for n in range(3):
                        new = bank[j][:, n * P:(n + 1) * P]
                        if n == 0:
                            ins = v.tensor_copy(states[:, 0, j, :], new)
                        else:
                            at = j * TOK + n * 64 + 63
                            ins = v.scalar_tensor_tensor(states[:, n, j, :], states[:, n - 1, j, :], probs[:, 1, at:at + 1], new, ALU.mult, ALU.add)
                        ins.then_inc(f.count(bank_free[j] if n == 2 else vector_step), 1)
                        dve.wait_ge(f.last, f.now(f.last))
                for j in range(2):
                    take(j, merged[:, 2 * j:2 * j + 2, :])
                dve.wait_ge(f.last, f.now(f.last))
                v.tensor_tensor(osq, merged[:, 0:4, :], merged[:, 0:4, :], ALU.mult).then_inc(f.count(normed_sq), 1)
                for q in range(4):
                    take(q, cumr[:, q * 512:(q + 1) * 512], bank[q][:, :])
                take(0, cumt[:, :], bank[0][:, 0:24])
                dve.wait_ge(f.last, f.now(f.last))
                for c in range(2):
                    for h in range(8):
                        at = (8 * c + h) * P
                        v.scalar_tensor_tensor(seg[:, c, h, :], cumr[:, at:at + P], cumt[:, 8 * c + h:8 * c + h + 1],
                                               const[:, C_BAN:C_BAN + P], ALU.subtract, ALU.add).then_inc(f.count(vector_step), 1)
                v.scalar_tensor_tensor(wtail, cumt[:, 16:24], float(D), cumt[:, 0:8], ALU.mult, ALU.subtract).then_inc(f.count(seg_ready), 1)
                for g in range(2):
                    v.tensor_scalar(cmg[:, g, :], ka[:, 1, :], half[g], None, ALU.mult).then_inc(f.count(ssd_in if g else vector_step), 1)
                dve.wait_ge(normed_std, f.next(normed_std))
                v.reciprocal(osq, osq).then_inc(f.count(vector_step), 1)
                dve.wait_ge(f.last, f.now(f.last))
                v.scalar_tensor_tensor(merged[:, 0:4, :], merged[:, 0:4, :], p2[:, B_GN:B_GN + 1], osq, ALU.mult, ALU.mult).then_inc(f.count(vector_step), 1)
                dve.wait_ge(f.last, f.now(f.last))
                v.tensor_tensor(merged[:, 0:4, :], merged[:, 0:4, :], gb[:, :, :], ALU.mult).then_inc(f.count(vector_step), 1)
                dve.wait_ge(seg_exp, f.next(seg_exp))
                v.tensor_tensor(tiles(xw, 8), tiles(vb[:, 0, :], 8), wtail.rearrange("p (h o) -> p h o", o=1).broadcast_to([P, 8, 64]),
                                ALU.mult).then_inc(f.count(state_in), 1)
                dve.wait_ge(bank_full[1], f.next(bank_full[1]))
                for c in range(2):
                    for g in range(2):
                        s = seg[:, c, 4 * g:4 * g + 4, :]
                        v.tensor_tensor(s, s, spread(bank[1][:, (2 * c + g) * P:(2 * c + g + 1) * P], 4), ALU.mult).then_inc(f.count(bank_free[1] if (c, g) == (1, 1) else vector_step), 1)
                take(2, state, bank[2][:, :])
                for g in range(2):
                    v.tensor_tensor(cme[:, 4 * g:4 * g + 4, :], tiles(ecum, 8)[:, 4 * g:4 * g + 4, :], spread(cmg[:, g, P:TOK], 4),
                                    ALU.mult).then_inc(f.count(pair_ready if g else vector_step), 1)
                for j in range(2):
                    dve.wait_ge(bank_full[j], f.next(bank_full[j]))
                    for i in range(2):
                        t = 2 * j + i
                        v.scalar_tensor_tensor(merged[:, 4 + t, :], qb[:, t, :], p2[:, B_DS + t:B_DS + t + 1], pairs(j)[:, i, :],
                                               ALU.mult, ALU.add).then_inc(f.count(bank_free[j] if i else vector_step), 1)
                dve.wait_ge(f.last, f.now(f.last))
                v.tensor_tensor(merged[:, 4:8, :], merged[:, 4:8, :], gc[:, :, :], ALU.mult).then_inc(f.count(vector_step), 1)
                dve.wait_ge(f.last, f.now(f.last))
                v.tensor_tensor(osq, merged[:, 4:8, :], merged[:, 4:8, :], ALU.mult).then_inc(f.count(normed_sq), 1)
                dve.wait_ge(normed_std, f.next(normed_std))
                v.reciprocal(std[:, :], std[:, :]).then_inc(f.count(vector_step), 1)
                dve.wait_ge(f.last, f.now(f.last))
                for j in range(4):
                    ins = v.scalar_tensor_tensor(merged[:, 4 + j, :], merged[:, 4 + j, :], p2[:, B_SN + j:B_SN + j + 1], std[:, :],
                                                 ALU.mult, ALU.mult)
                ins.then_inc(f.count(merged_ready), 1)
                for n in range(4):
                    dve.wait_ge(bank_full[n], f.next(bank_full[n]))
                    add_gated(l, 0, n, n, bank_free[n])
                rms_gain(l, 1, x_ready)
                if l == 0:
                    split_low(0, 0)
                rms_finish(l, 1)
                if l == 0:
                    x_low(yT)
                    dense(lambda p, i: f.bump(gate_full[p]), FF2 // CW, FFN2_TRIP)
                else:
                    take(0, tiles(logit, 2), tiles(bank[0][:, 0:16], 2))
                    dve.wait_ge(f.last, f.now(f.last))
                    for t in range(2):
                        v.max(best[:, 8 * t:8 * t + 8], logit[:, 8 * t:8 * t + 8]).then_inc(f.count(vector_step), 1)
                    dve.wait_ge(f.last, f.now(f.last))
                    for t in range(2):
                        v.max_index(place[:, 8 * t:8 * t + 8], best[:, 8 * t:8 * t + 8], logit[:, 8 * t:8 * t + 8]).then_inc(f.count(vector_step), 1)
                    b2 = tiles(best, 2)
                    v.tensor_tensor(pair[:, 0:2], b2[:, :, 1], b2[:, :, 0], ALU.subtract).then_inc(f.count(route_in), 1)
                    dve.wait_ge(f.last, f.now(f.last))
                    v.tensor_copy(placef, place[:, :]).then_inc(f.count(vector_step), 1)
                    v.memset(picks[:, EXPERTS:EXPERTS + 1, :], 0.0).then_inc(f.count(vector_step), 1)
                    dve.wait_ge(f.last, f.now(f.last))
                    v.tensor_scalar(placef, placef, 1.0, None, ALU.add).then_inc(f.count(vector_step), 1)
                    dve.wait_ge(f.last, f.now(f.last))
                    number = slots[:, 0:EXPERTS]
                    for t in range(2):
                        v.tensor_scalar(chosen[:, t, :], number, placef[:, 8 * t:8 * t + 1], None, ALU.is_equal).then_inc(f.count(vector_step), 1)
                    dve.wait_ge(f.last, f.now(f.last))
                    for t in range(2):
                        v.scalar_tensor_tensor(chosen[:, t, :], number, placef[:, 8 * t + 1:8 * t + 2], chosen[:, t, :],
                                               ALU.is_equal, ALU.add).then_inc(f.count(chosen_ready if t else vector_step), 1)
                    dve.wait_ge(pair_exp, f.next(pair_exp))
                    v.tensor_scalar(pair[:, 2:4], pair[:, 0:2], 1.0, None, ALU.add).then_inc(f.count(vector_step), 1)
                    dve.wait_ge(f.last, f.now(f.last))
                    v.reciprocal(pair[:, 2:4], pair[:, 2:4]).then_inc(f.count(vector_step), 1)
                    dve.wait_ge(f.last, f.now(f.last))
                    v.tensor_tensor(pair[:, 4:6], pair[:, 0:2], pair[:, 2:4], ALU.mult).then_inc(f.count(vector_step), 1)
                    dve.wait_ge(f.last, f.now(f.last))
                    for t in range(2):
                        v.tensor_scalar(route[:, t, :], number, placef[:, 8 * t:8 * t + 1], pair[:, 2 + t:3 + t], ALU.is_equal, ALU.mult).then_inc(f.count(vector_step), 1)
                        v.tensor_scalar(second[:, t, :], number, placef[:, 8 * t + 1:8 * t + 2], pair[:, 4 + t:5 + t], ALU.is_equal, ALU.mult).then_inc(f.count(vector_step), 1)
                    dve.wait_ge(f.last, f.now(f.last))
                    v.tensor_tensor(picks[:, 0:EXPERTS, 2:4].rearrange("p e t -> p t e"), route[:, :, :], second[:, :, :], ALU.add).then_inc(f.count(vector_step), 1)
                    dve.wait_ge(bank_full[0], f.next(bank_full[0]))
                    v.tensor_tensor(picks[:, 0:EXPERTS, 0:2].rearrange("p e t -> p t e"), tiles(bank[0][:, 0:16], 2), chosen[:, :, :],
                                    ALU.mult).then_inc(f.count(vector_step), 1)
                    v.tensor_reduce(crowd[:, 0:1], bank[0][:, 16:24], AX.X, ALU.max).then_inc(f.count(bank_free[0]), 1)
                    dve.wait_ge(f.last, f.now(f.last))
                    v.tensor_scalar(crowded[:, :], crowd[:, 0:1], float(P), None, ALU.is_gt).then_inc(f.count(crowd_ready), 1)

                    def split(s, h, last=None):
                        dve.wait_ge(hi_ready[h], f.next(hi_ready[h]))
                        v.tensor_tensor(ew_lo[:, h, :], ring(s), ew_hi[:, h, :].bitcast(F32), ALU.subtract).then_inc(f.count(lo_ready[h]), 1)

                    def form(p):
                        f.bump(gate_full[p])
                        dve.wait_ge(up_full[p], f.next(up_full[p]))
                        dve.wait_ge(silu_ready[p], f.next(silu_ready[p]))
                        v.tensor_tensor(act[:, p, :, 0:P], silu[:, p, :, 0:P], tiles(bank[2 * p + 1][:, 0:CW], 2), ALU.mult).then_inc(f.count(turn_ready[p]), 1)

                    def finish(p):
                        dve.wait_ge(act_hi_ready[p], f.next(act_hi_ready[p]))
                        v.tensor_tensor(eact_lo[:, p, :, :], tiles(bank[6][:, 0:CW], 2), eact_hi[:, p, :, :].bitcast(F32),
                                        ALU.subtract).then_inc(f.count(act_ready[p]), 1)

                    def gathered(q):
                        dve.wait_ge(gather_hi, f.next(gather_hi))
                        ks = slice(4 * q, 4 * q + 4)
                        v.tensor_tensor(xe_lo[:, ks, :], tiles(bank[7][:, :], 4), xe_hi[:, ks, :].bitcast(F32),
                                        ALU.subtract).then_inc(f.count(gather_free), 1)

                    def experts():
                        for t in range(2):
                            v.tensor_scalar(select[:, t, :], slots, picks[:, 0, t:t + 1], None, ALU.is_equal).then_inc(f.count(select_ready if t else vector_step), 1)
                        gathered(0)
                        gathered(1)
                        with f.trips(EXPERTS, EXPERT) as e:
                            dve.wait_ge(f.last, f.now(f.last))
                            v.tensor_copy(pick[:, :, :], picks[:, bass.ds(e, 2), :]).then_inc(f.count(vector_step), 1)
                            dve.wait_ge(f.last, f.now(f.last))
                            for t in range(2):
                                v.tensor_scalar(weigh[:, t, :], slots, pick[:, 0, t:t + 1], pick[:, 0, 2 + t:3 + t], ALU.is_equal, ALU.mult).then_inc(f.count(vector_step), 1)
                            for t in range(2):
                                v.tensor_scalar(select[:, t, :], slots, pick[:, 1, t:t + 1], None, ALU.is_equal).then_inc(f.count(select_ready if t else vector_step), 1)
                            expert_steps(split, form, finish, dve, f)
                            split(5, 2)
                            form(1)
                            gathered(0)
                            gathered(1)
                            finish(1)
                            for n in range(4):
                                dve.wait_ge(result_full, f.next(result_full))
                                add_gated(l, 1, n, n, result_free)
                        dve.wait_ge(f.last, f.now(f.last))

                    experts()
                    with dve.If(dve.value_load(crowded[0:1, 0:1], min_val=0, max_val=1) > 0):
                        v.tensor_scalar(picks[:, :, 0:2], picks[:, :, 0:2], -float(P), None, ALU.add).then_inc(f.count(vector_step), 1)
                        dve.wait_ge(f.last, f.now(f.last))
                        experts()
                    v.tensor_copy(gain[:, :], eln[:, 0:8]).then_inc(x_ready, 1)
                if l == 0:
                    dve.wait_ge(ffn_summed, f.next(ffn_summed))
                    for n in range(4):
                        add_gated(l, 1, n, 4 + n, x_ready if n == 3 else None)
            dve.wait_ge(std_ready, f.next(std_ready))
            v.reciprocal(std[:, :], std[:, :]).then_inc(final_step, 1)
            dve.wait_ge(final_step, 1)
            v.tensor_tensor(yT, xT[:, :, :], spread(std[:, :], KD), ALU.mult).then_inc(final_step, 1)
            dve.wait_ge(final_step, 2)
            for k in range(KD):
                ins = v.tensor_scalar(yT[:, k, :], yT[:, k, :], gain[:, k:k + 1], None, ALU.mult)
            ins.then_inc(f.count(y_ready), 1)

        @block.scalar
        def _(eng):
            f = Follow(eng, scalar_step, free)
            a = nc.scalar

            def take(b, dst, src=None):
                eng.wait_ge(bank_full[b], f.next(bank_full[b]))
                a.copy(dst, tiles(bank[b][:, :], 2) if src is None else src).then_inc(f.count(bank_free[b]), 1)

            def split_high(s, h):
                eng.wait_ge(ffn_loaded[s], f.next(ffn_loaded[s], 16))
                a.copy(w_hi[:, h, :], ring(s)).then_inc(f.count(hi_ready[h]), 1)

            def norm(eps, src, before, dense=False):
                a.preload_act_table(ACT.Sqrt)
                eng.wait_ge(before, f.next(before))
                a.activation(squares, src, ACT.Square).then_inc(f.count(squares_ready), 1)
                if dense:
                    split_high(0, 0)
                eng.wait_ge(var_ready, f.next(var_ready))
                a.activation(std[:, :], bank[4][:, 0:TOK], ACT.Sqrt, bias=eps).then_inc(f.count(std_ready), 1)
                a.preload_act_table(ACT.Silu if dense or eps is eps2 else ACT.Exp)

            def dense(x, silu_of, n, per):
                for q in range(2):
                    ks = slice(4 * q, 4 * q + 4)
                    a.copy(x_hi[:, ks, :], x[:, ks, :]).then_inc(f.count(x_hi_ready), 1)
                split_high(1, 1)
                f.bump(gate_full[0])

                done = {0: gate_full[0], 1: up_full[0], 2: down_done, 3: gate_full[1], 4: up_full[1]}

                def split(s, h, last):
                    if last == 5:
                        eng.wait_ge(down_done, f.now(down_done))
                    else:
                        eng.wait_ge(done[last], f.next(done[last]))
                    if s == 5:
                        f.bump(down_done)
                    split_high(s, h)

                def finish(p):
                    silu_of(p)
                    eng.wait_ge(product_ready[p], f.next(product_ready[p]))
                    a.copy(act_hi[:, p, :, :], act[:, p, :, :]).then_inc(f.count(act_hi_ready[p]), 1)

                dense_steps(split, lambda p, i: None, finish, n, eng, per, f)
                f.bump(down_done)

            def exps(u):
                b = u % 2
                eng.wait_ge(peak_ready, f.next(peak_ready))
                for m in range(2):
                    ins = a.activation(probs[:, b, m * TOK:(m + 1) * TOK], scores[:, b, m * TOK:(m + 1) * TOK], ACT.Exp,
                                       bias=peak[:, b, m:m + 1], scale=-1.0, accum_out=total[:, b, m:m + 1])
                ins.then_inc(f.count(exp_ready), 1)

            def probs_out(u, n, whole):
                b, qt = 4 + u % 2, u % 2
                dst = probsT[:, n % 2, :, :, qt * P:(qt + 1) * P]
                if whole:
                    take(b, dst.rearrange("p m t q -> p (m t) q"), tiles(bank[b][:, :], 4))
                else:
                    take(b, dst[:, 0, :, :], tiles(bank[b][:, 0:2 * P], 2))

            eng.wait_ge(inputs_in, f.next(inputs_in, 64))
            a.activation(cond[:, :], eln[:, 16:24], ACT.Silu).then_inc(f.count(cond_ready), 1)
            norm(eps1, yT, centred)
            f.bump(x_ready)
            with f.trips(DEPTH, LAYER1):
                eng.wait_ge(lam_dot, f.next(lam_dot))
                a.activation(lam[:, 2:4], lam[:, 0:2], ACT.Exp).then_inc(f.count(lam_exp), 1)
                for u in range(18):
                    if u < 16:
                        exps(u)
                    if u < 12:
                        take(6 + u % 2, gates[:, 2 * u:2 * u + 2, :])
                    if 1 <= u <= 16:
                        probs_out(u - 1, (u - 1) // 2, u - 1 >= 8)
                    if u == 10:
                        for j in range(2):
                            take(4 + j, ka[:, 2 * j:2 * j + 2, :])
                        eng.wait_ge(f.last, f.now(f.last))
                        a.activation(ka[:, :, :], ka[:, :, :], ACT.Sqrt, bias=eps1, scale=float(D // P)).then_inc(f.count(sub_std), 1)
                eng.wait_ge(f.last, f.now(f.last))
                a.activation(flat, flat, ACT.Sigmoid).then_inc(f.count(gates_ready), 1)
                norm(eps1, yT, centred)
                for u in range(6):
                    if u < 4:
                        exps(u)
                    if 1 <= u <= 4:
                        probs_out(u - 1, (u - 1) // 2, True)
                norm(eps1, yT, centred, True)

                def silu_conv(p):
                    eng.wait_ge(conv_ready[p], f.next(conv_ready[p]))
                    a.activation(silu[:, p, :, :], conva[:, p, :, :], ACT.Silu).then_inc(f.count(silu_ready[p]), 1)

                eng.wait_ge(x_ready, f.now(x_ready) + 2)
                dense(xT, silu_conv, FF1 // CW, FFN1_TRIP)
                norm(eps1, yT, centred)
                f.bump(x_ready, 3)

            def silu_gate(p):
                a.activation(silu[:, p, :, :], tiles(bank[2 * p][:, :], 2), ACT.Silu).then_inc(f.count(silu_ready[p]), 1)

            eng.wait_ge(x_ready, f.now(x_ready))
            for l in range(DEPTH):
                if l == 0:
                    a.activation(squares, xT[:, :, :], ACT.Square).then_inc(f.count(squares_ready), 1)
                    eng.wait_ge(var_ready, f.next(var_ready))
                    a.activation(std[:, :], bank[4][:, 0:TOK], ACT.Sqrt, bias=eps2).then_inc(f.count(std_ready), 1)
                else:
                    norm(eps2, xT[:, :, :], x_ready)
                eng.wait_ge(proj_ready, f.next(proj_ready))
                a.activation(gb[:, :, :], gb[:, :, :], ACT.Silu).then_inc(f.count(scalar_step), 1)
                a.activation(gc[:, :, :], gc[:, :, :], ACT.Silu).then_inc(f.count(scalar_step), 1)
                eng.wait_ge(conv_in, f.next(conv_in))
                a.activation(qb[:, :, :], qb[:, :, :], ACT.Silu).then_inc(f.count(scalar_step), 1)
                a.activation(ka[:, 0:2, :], ka[:, 0:2, :], ACT.Silu).then_inc(f.count(conv_silu), 1)
                a.activation(aexp, par2[l][:, B_ALOG:B_ALOG + 8], ACT.Exp).then_inc(f.count(scalar_step), 1)
                a.activation(dtabs, dtabs, ACT.Exp, scale=-1.0).then_inc(f.count(scalar_step), 1)
                eng.wait_ge(decay_in, f.next(decay_in))
                a.activation(scores[:, 0, :], scores[:, 0, :], ACT.Exp, scale=-1.0).then_inc(f.count(scalar_step), 1)
                eng.wait_ge(f.last, f.now(f.last))
                a.activation(dtabs, dtabs, ACT.Ln, bias=one).then_inc(f.count(dt_ln), 1)
                a.activation(scores[:, 0, :], scores[:, 0, :], ACT.Ln, bias=one).then_inc(f.count(decay_ln), 1)
                eng.wait_ge(cum_ready, f.next(cum_ready))
                a.activation(probs[:, 1, :], probs[:, 0, :], ACT.Exp).then_inc(f.count(scalar_step), 1)
                a.activation(scores[:, 0, :], probs[:, 0, :], ACT.Exp, scale=-1.0).then_inc(f.count(scalar_step), 1)
                a.activation(scores[:, 1, :], scores[:, 1, :], ACT.Exp).then_inc(f.count(cum_exp), 1)
                for j in range(2):
                    take(4 + j, osq[:, 2 * j:2 * j + 2, :])
                eng.wait_ge(f.last, f.now(f.last))
                a.activation(osq, osq, ACT.Sqrt, bias=eps2, scale=float(D // P)).then_inc(f.count(normed_std), 1)
                eng.wait_ge(seg_ready, f.next(seg_ready))
                a.activation(flat[:, CH:2 * CH], flat[:, CH:2 * CH], ACT.Exp).then_inc(f.count(scalar_step), 1)
                a.activation(ecum, cumr[:, 1024:2048], ACT.Exp).then_inc(f.count(scalar_step), 1)
                a.activation(wtail, wtail, ACT.Exp).then_inc(f.count(seg_exp), 1)
                take(4, std[:, :], bank[4][:, 0:TOK])
                eng.wait_ge(f.last, f.now(f.last))
                a.activation(std[:, :], std[:, :], ACT.Sqrt, bias=eps2, scale=2.0).then_inc(f.count(normed_std), 1)
                norm(eps2, xT[:, :, :], x_ready, l == 0)
                if l == 0:
                    eng.wait_ge(y_ready, DEPTH + 2)
                    dense(yT, silu_gate, FF2 // CW, FFN2_TRIP)
                else:
                    eng.wait_ge(route_in, f.next(route_in))
                    a.activation(pair[:, 0:2], pair[:, 0:2], ACT.Exp).then_inc(f.count(pair_exp), 1)
                    for q in range(4):
                        take(4 + q, htok[:, q // 2, 512 * (q % 2):512 * (q % 2) + 512], bank[4 + q][:, :])

                    done = {0: gate_full[0], 1: up_full[0], 2: down_done, 3: gate_full[1], 4: up_full[1]}

                    def split(s, h, last=None):
                        if last == 5:
                            eng.wait_ge(down_done, f.now(down_done))
                        elif last is not None:
                            eng.wait_ge(done[last], f.next(done[last]))
                        if s == 5:
                            f.bump(down_done)
                        eng.wait_ge(ffn_loaded[s], f.next(ffn_loaded[s], 16))
                        a.copy(ew_hi[:, h, :], ring(s)).then_inc(f.count(hi_ready[h]), 1)

                    def form(p):
                        a.activation(silu[:, p, :, 0:P], tiles(bank[2 * p][:, 0:CW], 2), ACT.Silu).then_inc(f.count(silu_ready[p]), 1)

                    def finish(p):
                        eng.wait_ge(turned[p], f.next(turned[p]))
                        a.copy(eact_hi[:, p, :, :], tiles(bank[6][:, 0:CW], 2)).then_inc(f.count(act_hi_ready[p]), 1)

                    def gathered(q):
                        eng.wait_ge(gather_full, f.next(gather_full))
                        a.copy(xe_hi[:, 4 * q:4 * q + 4, :], tiles(bank[7][:, :], 4)).then_inc(f.count(gather_hi), 1)

                    def experts():
                        a.preload_act_table(ACT.Silu)
                        gathered(0)
                        gathered(1)
                        with f.trips(EXPERTS, EXPERT):
                            expert_steps(split, form, finish, eng, f)
                            split(5, 2, 3)
                            form(1)
                            gathered(0)
                            gathered(1)
                            finish(1)
                            f.bump(up_full[1])
                            f.bump(down_done)
                            eng.wait_ge(back_full, f.next(back_full))
                            a.copy(back, bank[0][:, 0:TOK]).then_inc(f.count(back_free), 1)
                            for n in range(2):
                                take(4 + n, ye[:, n * 512:(n + 1) * 512], bank[4 + n][:, :])

                    experts()
                    eng.wait_ge(crowd_ready, f.next(crowd_ready))
                    with eng.If(eng.value_load(crowded[0:1, 0:1], min_val=0, max_val=1) > 0):
                        experts()
            norm(eps2, xT[:, :, :], x_ready)
    if BAD:
        raise AssertionError("counts per trip differ from the tables")


def constants():
    c = np.zeros((P, C_ALL), np.float32)
    c[:, C_ID:C_ID + P] = np.eye(P)
    for m in range(P):
        if m % 64 < 32:
            c[m + 32, C_ROT + m] = -1.0
        else:
            c[m - 32, C_ROT + m] = 1.0
    inv = np.float32(10000.0) ** (-np.arange(32, dtype=np.float32) * np.float32(2.0) / np.float32(64))
    angle = np.arange(TOK, dtype=np.float32)[None, :] * inv.astype(np.float32)[:, None]
    c[:, C_COS:C_COS + TOK] = np.tile(np.cos(angle), (4, 1))
    c[:, C_SIN:C_SIN + TOK] = np.tile(np.sin(angle), (4, 1))
    j, i = np.arange(P)[:, None], np.arange(P)[None, :]
    c[:, C_TRI:C_TRI + P] = j <= i
    c[:, C_BAN:C_BAN + P] = np.where(j <= i, 0.0, NEG)
    c[:, C_DIAG:C_DIAG + P] = (j <= i) & (j // 64 == i // 64)
    q, k = np.arange(64)[:, None], np.arange(64)[None, :]
    start = np.clip(q - 8, 0, 48)
    c[:, C_WIN:C_WIN + 64] = np.tile(np.where((k >= start) & (k < start + 16), 0.0, NEG), (2, 1))
    for m in range(2):
        c[64 * m:64 * m + 64, C_HALF + m] = 1.0
    c[:, C_EPS1], c[:, C_EPS2], c[:, C_ONE] = 1e-5, 1e-6, 1.0
    c[:, C_IOTA:C_IOTA + P] = np.arange(1, P + 1)
    return c


def columns(vector):
    v = np.asarray(vector)
    return np.moveaxis(v.reshape(-1, P), 0, 1)


def rows(vector):
    return np.broadcast_to(np.asarray(vector).reshape(1, -1), (P, np.asarray(vector).size))


BIG = ["w_in", "w_branch", "w_mix_out", "xa_q", "xa_kv", "xa_o", "ffn_w_in", "ffn_w_out", "ada_w_2", "w_in_2", "gla_a_w_2",
       "w_out_2", "ffn_w_gate_2", "ffn_w_up_2", "ffn_w_down_2", "router_w_2", "moe_w_gate_2", "moe_w_up_2", "moe_w_down_2"]


def layout(i):
    arrays = {n: np.ascontiguousarray(i[n]) for n in BIG}
    arrays["xT"] = np.ascontiguousarray(np.asarray(i["x"])[0].T)
    arrays["memT"] = np.ascontiguousarray(np.asarray(i["mem"])[0].T)
    arrays["const"] = constants()
    arrays["eln"] = np.concatenate([columns(i["emb_ln_g"]), columns(i["emb_ln_b"]), columns(i["c_2"])], axis=1)
    arrays["fin"] = np.ascontiguousarray(columns(i["final_norm_w_2"]))
    par1 = np.zeros((DEPTH, P, A_ALL), np.float32)
    par2 = np.zeros((DEPTH, P, B_ALL), np.float32)
    for l in range(DEPTH):
        init = 0.8 - 0.6 * math.exp(-0.3 * l)
        taps = np.concatenate([np.asarray(i["ffn_conv_w"])[l], np.asarray(i["ffn_conv_b"])[l][None]], axis=0)
        par1[l, :, A_LNG:A_LNG + 24] = columns(np.asarray(i["ln_g"])[l])
        par1[l, :, A_LNB:A_LNB + 24] = columns(np.asarray(i["ln_b"])[l])
        par1[l, :, A_SUB:A_SUB + 1] = columns(np.asarray(i["subln_g"])[l])
        par1[l, :, A_SCW:A_SCW + 12] = columns(np.asarray(i["sc_conv_w"])[l])
        par1[l, :, A_FF:A_FF + 88] = np.moveaxis(taps.reshape(4, FF1 // P, P), (0, 1, 2), (2, 1, 0)).reshape(P, 88)
        par1[l, :, A_LAM0] = init
        par1[l, :, A_LAM1] = 1.0 - init
        for k, n in enumerate(("lam_q1", "lam_k1", "lam_q2", "lam_k2")):
            par1[l, :, A_LAMV + 64 * k:A_LAMV + 64 * k + 64] = rows(np.asarray(i[n])[l])
        for at, value in ((B_N1, columns(np.asarray(i["norm1_w_2"])[l])), (B_N2, columns(np.asarray(i["norm2_w_2"])[l])),
                          (B_ADA, columns(np.asarray(i["ada_b_2"])[l])), (B_AB, columns(np.asarray(i["gla_a_b_2"])[l])),
                          (B_GN, columns(np.asarray(i["gla_norm_w_2"])[l])), (B_CW, columns(np.asarray(i["conv_w_2"])[l])),
                          (B_CB, columns(np.asarray(i["conv_b_2"])[l])), (B_DTB, rows(np.asarray(i["dt_bias_2"])[l])),
                          (B_ALOG, rows(np.asarray(i["a_log_2"])[l])),
                          (B_DS, columns(np.repeat(np.asarray(i["d_skip_2"])[l], 64))),
                          (B_SN, columns(np.asarray(i["ssd_norm_w_2"])[l]))):
            par2[l, :, at:at + value.shape[1]] = value
    arrays["par1"], arrays["par2"] = par1, par2
    rpb = np.zeros((DEPTH, 8, 7, 127), np.float32)
    rpb[..., 48:79] = np.asarray(i["rpb"])[:, :, 4:11, :]
    arrays["rpb"] = rpb
    return {n: np.ascontiguousarray(a) for n, a in arrays.items()}


def kernel(**inputs):
    import concourse.bacc as bacc
    from concourse.bass_utils import run_bass_kernel_spmd as run

    nc = bacc.Bacc("TRN2", target_bir_lowering=False, num_devices=1)
    arrays = layout(inputs)
    io = {n: nc.dram_tensor(f"in_{n}", a.shape, F32, kind="ExternalInput").ap() for n, a in arrays.items()}
    io["out"] = nc.dram_tensor("outT", (D, TOK), F32, kind="ExternalOutput").ap()
    io["windows"] = nc.dram_tensor("windows", (DEPTH, 64, 8, 7, 127), F32, kind="Internal").ap()
    program(nc, io)
    r = run(nc, [{f"in_{n}": a for n, a in arrays.items()}], core_ids=[0])
    return np.ascontiguousarray(r.results[0]["outT"].T)[None]
```

```python
import math
from contextlib import ExitStack, contextmanager

import numpy as np

import concourse.bass as bass
from concourse import mybir

F32 = mybir.dt.float32
F32R = mybir.dt.float32r
ALU = mybir.AluOpType
ACT = mybir.ActivationFunctionType
AX = mybir.AxisListType

P = 128
TOK = 256
D = 1024
KD = D // P
DEPTH = 2
ALPHA = (2.0 * DEPTH) ** 0.25
SLOTS = 9
CH = 2048
CW = CH // KD
FF1, FF2 = 2816, 3584
EXPERTS = 8
NEG = -1.0e30


class Follow:

    def __init__(self, eng, own, given=()):
        self.eng, self.own, self.last = eng, own, own
        self.base, self.here, self.followed = {}, {s.name: 1 for s in given}, set()

    def now(self, sem):
        return self.base.get(sem.name, 0) + self.here.get(sem.name, 0)

    def bump(self, sem, by=1):
        self.followed.add(sem.name)
        self.here[sem.name] = self.here.get(sem.name, 0) + by

    def next(self, sem, by=1):
        self.bump(sem, by)
        return self.now(sem)

    def count(self, sem):
        self.last = sem if sem is not None else self.own
        self.bump(self.last)
        return self.last

    @contextmanager
    def trips(self, n, per):
        with self.eng.Fori(0, n) as i:
            base, here = self.base, self.here
            names = set(per) | set(base) | set(here)
            start = {s: base.get(s, 0) + here.get(s, 0) for s in names}
            self.base = {s: start[s] + i * per[s] if per.get(s) else start[s] for s in names}
            self.here = {}
            yield i
            wrong = {s: self.here.get(s, 0) for s in set(self.here) | set(per)
                     if s in self.followed and per.get(s, 0) != self.here.get(s, 0)}
            if wrong:
                BAD.append((per, wrong))
        self.base, self.here = base, {s: here.get(s, 0) + n * per.get(s, 0) for s in set(per) | set(here)}


C_ID, C_ROT, C_COS, C_SIN, C_TRI, C_BAN, C_DIAG, C_WIN, C_HALF, C_EPS1, C_EPS2, C_ONE, C_IOTA = (
    0, 128, 256, 512, 768, 896, 1024, 1152, 1216, 1218, 1219, 1220, 1221)
C_ALL = C_IOTA + P
A_LNG, A_LNB, A_SUB, A_SCW, A_FF, A_LAM0, A_LAM1, A_LAMV = 0, 24, 48, 49, 61, 149, 150, 151
A_ALL = A_LAMV + 256
B_N1, B_N2, B_ADA, B_AB, B_GN, B_CW, B_CB, B_DTB, B_ALOG, B_DS, B_SN = 0, 8, 16, 64, 66, 67, 91, 97, 105, 113, 117
B_ALL = B_SN + 4

LAYER1 = {
    "act_hi_ready0": 6, "act_hi_ready1": 5, "act_ready0": 6, "act_ready1": 5, "ada_loaded1": 64, "ada_loaded2": 64,
    "ada_loaded4": 64, "ada_loaded5": 64, "ada_loaded7": 64, "ada_loaded8": 64, "bank_free0": 24, "bank_free1": 24,
    "bank_free2": 31, "bank_free3": 31, "bank_free4": 11, "bank_free5": 11, "bank_free6": 6, "bank_free7": 6,
    "bank_full0": 24, "bank_full1": 24, "bank_full2": 31, "bank_full3": 31, "bank_full4": 11, "bank_full5": 11,
    "bank_full6": 6, "bank_full7": 6, "bias_in": 256, "centred": 12, "conv_ready0": 6, "conv_ready1": 5, "down_done": 11,
    "exp_ready": 20, "ffn_loaded0": 96, "ffn_loaded1": 96, "ffn_loaded2": 96, "ffn_loaded3": 80, "ffn_loaded4": 80,
    "ffn_loaded5": 80, "ffn_summed": 1, "gate_full0": 6, "gate_full1": 5, "gates_ready": 1, "heads_ready": 1,
    "hi_ready0": 17, "hi_ready1": 16, "lam_dot": 1, "lam_exp": 1, "mean_ready": 3, "merged_ready": 1, "mixer_in": 1,
    "mod_ready": 24, "mod_scaled": 24, "par_in": 16, "peak_ready": 20, "probs_ready": 20, "product_ready0": 6,
    "product_ready1": 5, "silu_ready0": 6, "silu_ready1": 5, "squares_ready": 12, "std_ready": 3, "sub_squares": 1,
    "sub_std": 1, "up_full0": 6, "up_full1": 5, "var_ready": 3, "vector_step": 190, "w_loaded0": 160, "w_loaded1": 96,
    "w_loaded2": 96, "w_loaded3": 160, "w_loaded4": 96, "w_loaded5": 80, "w_loaded6": 144, "w_loaded7": 80,
    "w_loaded8": 80, "w_used0": 16, "w_used1": 16, "w_used2": 16, "w_used3": 15, "w_used4": 15, "w_used5": 14,
    "w_used6": 9, "w_used7": 9, "w_used8": 9, "x_hi_ready": 4, "x_lo_ready": 4, "x_pieces": 9, "x_ready": 3, "y_ready": 1,}
FFN1_TRIP = {
    "act_hi_ready0": 1, "act_hi_ready1": 1, "act_ready0": 1, "act_ready1": 1, "conv_ready0": 1, "conv_ready1": 1,
    "down_done": 2, "ffn_loaded0": 16, "ffn_loaded1": 16, "ffn_loaded2": 16, "ffn_loaded3": 16, "ffn_loaded4": 16,
    "ffn_loaded5": 16, "gate_full0": 1, "gate_full1": 1, "hi_ready0": 3, "hi_ready1": 3, "product_ready0": 1,
    "product_ready1": 1, "silu_ready0": 1, "silu_ready1": 1, "up_full0": 1, "up_full1": 1, "vector_step": 12, "w_used0": 1,
    "w_used1": 1, "w_used2": 1, "w_used3": 1, "w_used4": 1, "w_used5": 1,}
FFN2_TRIP = {
    "act_hi_ready0": 1, "act_hi_ready1": 1, "act_ready0": 1, "act_ready1": 1, "down_done": 2, "ffn_loaded0": 16,
    "ffn_loaded1": 16, "ffn_loaded2": 16, "ffn_loaded3": 16, "ffn_loaded4": 16, "ffn_loaded5": 16, "gate_full0": 1,
    "gate_full1": 1, "hi_ready0": 3, "hi_ready1": 3, "product_ready0": 1, "product_ready1": 1, "silu_ready0": 1,
    "silu_ready1": 1, "up_full0": 1, "up_full1": 1, "w_used0": 1, "w_used1": 1, "w_used2": 1, "w_used3": 1, "w_used4": 1,
    "w_used5": 1,}
FFN3_TRIP = {
    "act_hi_ready0": 1, "act_hi_ready1": 1, "act_ready0": 1, "act_ready1": 1, "down_done": 2, "ffn_loaded0": 16,
    "ffn_loaded1": 16, "ffn_loaded2": 16, "ffn_loaded3": 16, "ffn_loaded4": 16, "ffn_loaded5": 16, "gate_full0": 1,
    "gate_full1": 1, "hi_ready0": 2, "hi_ready1": 2, "hi_ready2": 2, "silu_ready0": 1, "silu_ready1": 1, "turn_ready0": 1,
    "turn_ready1": 1, "turned0": 1, "turned1": 1, "up_full0": 1, "up_full1": 1, "w_used0": 1, "w_used1": 1, "w_used2": 1,
    "w_used3": 1, "w_used4": 1, "w_used5": 1,}
EXPERT = {
    "act_hi_ready0": 7, "act_hi_ready1": 7, "act_ready0": 7, "act_ready1": 7, "back_free": 1, "back_full": 1,
    "bank_free4": 1, "bank_free5": 1, "bank_full4": 1, "bank_full5": 1, "down_done": 14, "ffn_loaded0": 112,
    "ffn_loaded1": 112, "ffn_loaded2": 112, "ffn_loaded3": 112, "ffn_loaded4": 112, "ffn_loaded5": 112, "gate_full0": 7,
    "gate_full1": 7, "gather_free": 2, "gather_full": 2, "gather_hi": 2, "hi_ready0": 14, "hi_ready1": 14, "hi_ready2": 14,
    "result_free": 4, "result_full": 4, "select_ready": 1, "silu_ready0": 7, "silu_ready1": 7, "turn_ready0": 7,
    "turn_ready1": 7, "turned0": 7, "turned1": 7, "up_full0": 7, "up_full1": 7, "vector_step": 8, "w_used0": 7,
    "w_used1": 7, "w_used2": 7, "w_used3": 7, "w_used4": 7, "w_used5": 7,}
BAD = []


def program(nc, io):
    w_in, w_branch, w_mix, xa_q, xa_kv, xa_o, ffn_in, ffn_out = (
        io[n] for n in ("w_in", "w_branch", "w_mix_out", "xa_q", "xa_kv", "xa_o", "ffn_w_in", "ffn_w_out"))

    with ExitStack() as ctx:
        def sb(name, *shape, dt=F32):
            return ctx.enter_context(nc.sbuf_tensor(name, [P, *shape], dt))

        def sem(name):
            return ctx.enter_context(nc.semaphore(name))

        def tiles(ap, k):
            return ap.rearrange("p (k t) -> p k t", k=k)

        def spread(ap, k):
            return ap.rearrange("p (o t) -> p o t", o=1).broadcast_to([P, k, ap.shape[1]])

        ring_head = sb("ring_head", 6, CH)
        xT = sb("xT", KD, TOK)
        work = sb("work", 2 * CH)
        yT = tiles(work[:, 0:CH], KD)
        merged = tiles(work[:, CH:2 * CH], KD)
        bias = work[:, 0:3072].rearrange("p (h j c) -> p h j c", h=8, j=6)
        memT = sb("memT", KD, TOK)
        kb = sb("kb", 4, TOK)
        gates = sb("gates", 24, TOK)
        flat = gates[:, :, :].rearrange("p n t -> p (n t)")
        squares = tiles(flat[:, 0:CH], KD)
        conva, silu, act = (flat[:, i * 1024:(i + 1) * 1024].rearrange("p (b j t) -> p b j t", b=2, j=2) for i in range(3))
        scores = sb("scores", 2, 512)
        probs = sb("probs", 2, 512)
        const = sb("const", C_ALL)
        ones = sb("ones", P)
        zeros = sb("zeros", 512, dt=mybir.dt.bfloat16)
        par = sb("par", A_ALL)
        par2 = [par[:, l * B_ALL:(l + 1) * B_ALL] for l in range(DEPTH)]
        std = sb("std", TOK)
        peak = sb("peak", 2, 2)
        total = sb("total", 2, 2)
        lam = sb("lam", 8)
        ffp = sb("ffp", 8)
        eln = sb("eln", 24)
        cond = sb("cond", KD)
        mod = sb("mod", 48)
        mods = sb("mods", DEPTH, 48)
        gain = sb("gain", KD)
        small = sb("small", 64)
        dta, route, second = (sb(n, 2, 8) for n in ("dta", "route", "second"))
        cumt = sb("cumt", 24)
        flag = sb("flag", SLOTS + 10)
        place = sb("place", 16, dt=mybir.dt.uint32)
        chosen = sb("chosen", 2, 8)
        picks = sb("picks", EXPERTS + 1, 4)
        pick = sb("pick", 2, 4)
        crowd = sb("crowd", 8)
        crowded = sb("crowded", 1, dt=mybir.dt.int32)
        def in_scope(scope, name, *shape, dt=F32):
            return scope.enter_context(nc.sbuf_tensor(name, [P, *shape], dt))

        with ExitStack() as loads:
            ring_tail = in_scope(loads, "ring_tail", SLOTS - 6, CH)
            with ExitStack() as mixer:
                qa, ka, qb, gb, gc, hc = (in_scope(mixer, n, 4, TOK) for n in ("qa", "ka", "qb", "gb", "gc", "hc"))
                va, vb = (in_scope(mixer, n, 2, 512) for n in ("va", "vb"))
                qhalf = [[in_scope(mixer, f"qhalf{a}{m}", 4, TOK) for m in range(2)] for a in range(2)]
                probsT = in_scope(mixer, "probsT", 2, 2, 2, TOK)
            with ExitStack() as ffns:
                w_hi, w_lo = (in_scope(ffns, n, 2, CH, dt=F32R) for n in ("w_hi", "w_lo"))
                x_hi, x_lo = (in_scope(ffns, n, KD, TOK, dt=F32R) for n in ("x_hi", "x_lo"))
                act_hi, act_lo = (in_scope(ffns, n, 2, 2, TOK, dt=F32R) for n in ("act_hi", "act_lo"))
        ew_hi, ew_lo = (sb(n, 3, CH, dt=F32R) for n in ("ew_hi", "ew_lo"))
        xe_hi, xe_lo = (sb(n, KD, P, dt=F32R) for n in ("xe_hi", "xe_lo"))
        eact_hi, eact_lo = (sb(n, 2, 2, P, dt=F32R) for n in ("eact_hi", "eact_lo"))

        def ring(s):
            return ring_head[:, s, :] if s < 6 else ring_tail[:, s - 6, :]

        ident = const[:, C_ID:C_ID + P]
        rot = const[:, C_ROT:C_ROT + P]
        tri = const[:, C_TRI:C_TRI + P]
        half = [const[:, C_HALF + m:C_HALF + m + 1] for m in range(2)]
        eps1, eps2, one = (const[:, c:c + 1] for c in (C_EPS1, C_EPS2, C_ONE))
        bank = [ctx.enter_context(nc.psum_tensor(f"bank{b}", [P, 512], F32)) for b in range(8)]


        alr = scores[:, 1, 0:TOK]
        half_kv = probsT[:, :, :, :, :].rearrange("p a b c t -> p (a b c t)")
        qe = [tiles(half_kv[:, 512 * m:512 * m + 512], 2) for m in range(2)]
        ke, ktail = (tiles(half_kv[:, c:c + 512], 2) for c in (1024, 1536))
        ktok = [hc[:, 2 * m:2 * m + 2, :] for m in range(2)]
        att = flat[:, 4096:5120].rearrange("p (a h t) -> p a h t", a=2, h=4)
        states = work[:, 0:768].rearrange("p (n j v) -> p n j v", n=3, j=2)
        cmg, btok, state = tiles(work[:, 768:1280], 2), work[:, 1280:1408], work[:, 1408:1920]
        osq = memT[:, 4:8, :]
        cme = memT[:, 0:4, :].rearrange("p k t -> p (k t)").rearrange("p (h t) -> p h t", h=8)
        cumr, ecum = flat[:, 0:CH], flat[:, 5120:6144]
        seg = flat[:, CH:2 * CH].rearrange("p (c h t) -> p c h t", c=2, h=8)
        xw = kb[:, 0:2, :].rearrange("p k t -> p (k t)")
        dtraw, dtabs, dt, aexp, wtail = (small[:, c:c + n] for c, n in ((0, 16), (16, 16), (32, 16), (48, 8), (56, 8)))
        logit, best, placef, pair = small[:, 0:16], small[:, 16:32], small[:, 32:48], small[:, 48:56]

        htok = work[:, CH:2 * CH].rearrange("p (t d) -> p t d", t=2)
        ye = memT[:, 4:8, :].rearrange("p k t -> p (k t)")
        select, weigh = (tiles(kb[:, i, :], 2) for i in range(2))
        back = kb[:, 2, :]
        slots = const[:, C_IOTA:C_IOTA + P]

        w_loaded = [sem(f"w_loaded{s}") for s in range(SLOTS)]
        w_used = [sem(f"w_used{s}") for s in range(SLOTS)]
        bank_full = [sem(f"bank_full{b}") for b in range(8)]
        bank_free = [sem(f"bank_free{b}") for b in range(8)]
        tensor_step, vector_step, scalar_step, pool_step = (sem(n + "_step") for n in ("tensor", "vector", "scalar", "pool"))
        inputs_in, mem_in, par_in, bias_in, par2_in = (sem(n) for n in ("inputs_in", "mem_in", "par_in", "bias_in", "par2_in"))
        windows_out = sem("windows_out")
        x_ready, y_ready, mean_ready, centred = sem("x_ready"), sem("y_ready"), sem("mean_ready"), sem("centred")
        x_pieces, y_pieces = sem("x_pieces"), sem("y_pieces")
        squares_ready, var_ready, std_ready = sem("squares_ready"), sem("var_ready"), sem("std_ready")
        mixer_in, peak_ready, exp_ready, probs_ready = (
            sem("mixer_in"), sem("peak_ready"), sem("exp_ready"), sem("probs_ready"))
        heads_ready, merged_ready, lam_dot, lam_exp = sem("heads_ready"), sem("merged_ready"), sem("lam_dot"), sem("lam_exp")
        sub_squares, sub_std, gates_ready = sem("sub_squares"), sem("sub_std"), sem("gates_ready")
        cond_ready = sem("cond_ready")
        gate_full, up_full, conv_ready, silu_ready, act_ready = (
            [sem(f"{n}{i}") for i in range(2)] for n in ("gate_full", "up_full", "conv_ready", "silu_ready", "act_ready"))
        ada_loaded = [sem(f"ada_loaded{s}") for s in range(SLOTS)]
        mod_scaled, mod_ready = sem("mod_scaled"), sem("mod_ready")
        ffn_loaded = [sem(f"ffn_loaded{s}") for s in range(6)]
        hi_ready = [sem(f"hi_ready{h}") for h in range(3)]
        down_done, x_hi_ready, x_lo_ready = sem("down_done"), sem("x_hi_ready"), sem("x_lo_ready")
        product_ready, act_hi_ready, turn_ready, turned = (
            [sem(f"{n}{i}") for i in range(2)] for n in ("product_ready", "act_hi_ready", "turn_ready", "turned"))
        gather_full, gather_hi, gather_free = sem("gather_full"), sem("gather_hi"), sem("gather_free")
        ffn_summed, out_done = sem("ffn_summed"), sem("out_done")
        alr_ready, decay_in, decay_exp, decay_ln, cum_ready, cum_exp, gla_in = (sem(n) for n in (
            "alr_ready", "decay_in", "decay_exp", "decay_ln", "cum_ready", "cum_exp", "gla_in"))
        normed_sq, normed_std = sem("normed_sq"), sem("normed_std")
        conv_in, conv_silu, dt_ln, dta_ready, seg_ready, seg_exp, ssd_in, state_in = (sem(n) for n in (
            "conv_in", "conv_silu", "dt_ln", "dta_ready", "seg_ready", "seg_exp", "ssd_in", "state_in"))
        back_full, back_free, result_full, result_free = (sem(n) for n in ("back_full", "back_free", "result_full", "result_free"))
        proj_ready, pair_exp, pair_ready, route_in, chosen_ready, crowd_ready, select_ready, final_step = (sem(n) for n in (
            "proj_ready", "pair_exp", "pair_ready", "route_in", "chosen_ready", "crowd_ready", "select_ready", "final_step"))

        free = w_used + bank_free + [result_free, down_done]

        block = ctx.enter_context(nc.Block())

        def ada_slot(c):
            return (18 + c // 2 * 3 + 1 + c % 2) % SLOTS

        def kpn(w):
            return w.rearrange("(k p) n -> p k n", p=P)

        cuts = [[(1536, 16), (2832, 8)]] + [[(c, CW)] for c in (0, 256, 2064, 2320, 2576, 512, 768, 1024, 1280, 1552, 1808)]

        def ffn_steps(up, down, n, engine, per, f):
            up(0, 0)
            with f.trips((n - 1) // 2, per) as i:
                up(1, 2 * i + 1)
                down(0, 2 * i)
                up(0, 2 * i + 2)
                down(1, 2 * i + 1)
            if n % 2 == 0:
                up(1, n - 1)
                down(0, n - 2)
            down((n - 1) % 2, n - 1)

        def dense_steps(split, form, finish, n, engine, per, f):
            with f.trips((n - 1) // 2, per) as i:
                form(0, 2 * i)
                split(3, 0, 1)
                finish(0)
                split(4, 1, 5)
                split(2, 0, 3)
                form(1, 2 * i + 1)
                split(0, 1, 4)
                finish(1)
                split(1, 0, 2)
                split(5, 1, 0)
            form(0, n - 2 + n % 2)
            if n % 2 == 0:
                split(3, 0, 1)
                finish(0)
                split(4, 1, 5)
                split(2, 0, 3)
                form(1, n - 1)
                finish(1)
                split(5, 1, 4)
            else:
                finish(0)
                split(2, 0, 1)

        def expert_steps(split, form, finish, engine, f, between=lambda: None):
            split(0, 0)
            split(1, 1)
            between()
            with f.trips((FF2 // CW - 1) // 2, FFN3_TRIP):
                split(3, 2, 0)
                form(0)
                split(4, 0, 1)
                split(2, 1, 5)
                finish(0)
                split(0, 2, 3)
                form(1)
                split(1, 0, 4)
                split(5, 1, 2)
                finish(1)
            split(3, 2, 0)
            form(0)
            split(4, 0, 1)
            split(2, 1, 5)
            finish(0)

        @block.sync
        def _(sp):
            f = Follow(sp, tensor_step, free)
            turn = [0]
            for dst, src in ((yT, kpn(io["xT"])), (eln[:, :], io["eln"]), (const[:, :], io["const"])):
                sp.dma_start(dst, src).then_inc(inputs_in, 16)

            def load(pieces, slot=None, loaded=w_loaded):
                s = turn[0] % SLOTS if slot is None else slot
                turn[0] += 1
                sp.wait_ge(w_used[s], f.now(w_used[s]))
                f.bump(w_used[s])
                pieces = pieces if isinstance(pieces, list) else [pieces]
                k, n = pieces[0].shape[1], sum(piece.shape[2] for piece in pieces)
                dst = tiles(ring(s)[:, 0:k * n], k)
                at = 0
                for piece in pieces:
                    sp.dma_start(dst[:, :, at:at + piece.shape[2]], piece).then_inc(loaded[s], 16)
                    at += piece.shape[2]

            def ffn(gate, up_w, down_w, n, per):
                def up(p, i):
                    load(up_w(i), 3 * p + 1, ffn_loaded)
                    load(gate(i), 3 * p, ffn_loaded)

                def down(p, i):
                    load(down_w(i), 3 * p + 2, ffn_loaded)

                ffn_steps(up, down, n, sp, per, f)

            with f.trips(DEPTH, LAYER1) as l:
                turn[0] = 0
                for c in range(18):
                    load(kpn(w_in[l])[:, :, c * CW:(c + 1) * CW])
                for u in range(12):
                    load(kpn(w_in[l])[:, :, (18 + u) * CW:(19 + u) * CW])
                    for c in range(2 * u, 2 * u + 2):
                        load(kpn(io["ada_w_2"][l])[:, :, c * CW:(c + 1) * CW], None, ada_loaded)
                for n in range(4):
                    for b in range(3):
                        load(kpn(w_branch[l, b])[:, :, n * CW:(n + 1) * CW])
                for n in range(4):
                    load(kpn(w_mix[l])[:, :, n * CW:(n + 1) * CW])
                for n in range(8):
                    load(kpn(xa_kv[l])[:, :, n * CW:(n + 1) * CW])
                for n in range(4):
                    load(kpn(xa_q[l])[:, :, n * CW:(n + 1) * CW])
                for n in range(4):
                    load(kpn(xa_o[l])[:, :, n * CW:(n + 1) * CW])
                ffn(lambda i: kpn(ffn_in[l])[:, :, bass.ds(i * CW + FF1, CW)],
                    lambda i: kpn(ffn_in[l])[:, :, bass.ds(i * CW, CW)],
                    lambda i: kpn(ffn_out[l, bass.ds(i * CW, CW), :]), FF1 // CW, FFN1_TRIP)
            for l in range(DEPTH):
                turn[0] = 0
                for cut in cuts:
                    load([kpn(io["w_in_2"][l])[:, :, c:c + n] for c, n in cut])
                for n in range(4):
                    load(kpn(io["w_out_2"][l])[:, :, n * CW:(n + 1) * CW])
                names = [("ffn_w_gate_2", "ffn_w_up_2", "ffn_w_down_2"), ("moe_w_gate_2", "moe_w_up_2", "moe_w_down_2")][l]
                wg, wu, wd = (io[n] for n in names)
                if l == 0:
                    ffn(lambda i: kpn(wg[0])[:, :, bass.ds(i * CW, CW)], lambda i: kpn(wu[0])[:, :, bass.ds(i * CW, CW)],
                        lambda i: kpn(wd[0, bass.ds(i * CW, CW), :]), FF2 // CW, FFN2_TRIP)
                else:
                    load(kpn(io["router_w_2"][0]))
                    def experts():
                        with f.trips(EXPERTS, EXPERT) as e:
                            ffn(lambda i: kpn(wg[0, e])[:, :, bass.ds(i * CW, CW)],
                                lambda i: kpn(wu[0, e])[:, :, bass.ds(i * CW, CW)],
                                lambda i: kpn(wd[0, e, bass.ds(i * CW, CW), :]), FF2 // CW, FFN3_TRIP)

                    experts()
                    sp.wait_ge(crowd_ready, f.next(crowd_ready))
                    with sp.If(sp.value_load(crowded[0:1, 0:1], min_val=0, max_val=1) > 0):
                        experts()

        @block.gpsimd
        def _(pool):
            f = Follow(pool, pool_step)
            for i, s in enumerate(free):
                pool.memset(flag[0:1, i:i + 1], 0.0).then_inc(s, 1)
            pool.memset(ones[:, :], 1.0 / D)
            pool.memset(zeros[:, :], 0.0).then_inc(f.count(pool_step), 1)
            pool.dma_start(memT[:, :, :], kpn(io["memT"])).then_inc(mem_in, 16)
            for l in range(DEPTH):
                src = io["rpb"][l].rearrange("h j i -> (h j i)")
                pool.dma_start(io["windows"][l].rearrange("c h j i -> c (h j i)"),
                               bass.AP(src.tensor, src.offset, [[0, 64], [1, 8 * 7 * 127]])).then_inc(windows_out, 16)
            pool.wait_ge(windows_out, 16 * DEPTH)
            with f.trips(DEPTH, LAYER1) as l:
                pool.wait_ge(x_ready, f.now(x_ready) + 1)
                f.bump(x_ready, 3)
                pool.dma_start(par[:, :], io["par1"][l]).then_inc(par_in, 16)
                for side in range(2):
                    for h in range(8):
                        at = io["windows"][l, :, h, 1 - side:7 - side, 63:127]
                        src = bass.AP(at.tensor, at.offset, [[8 * 7 * 127 - 1, 64], [127, 6], [1, 64]])
                        pool.dma_start(bias[64 * side:64 * side + 64, h], src).then_inc(bias_in, 16)
            pool.wait_ge(x_ready, f.now(x_ready) + 1)
            f.bump(x_ready)
            for l in range(DEPTH):
                pool.dma_start(par2[l], io["par2"][l]).then_inc(par2_in, 16)
                pool.dma_start(kb[0:16, 2 + l, :], io["gla_a_w_2"][l]).then_inc(par2_in, 16)
            f.bump(x_ready, 2 * DEPTH)
            pool.dma_start(eln[:, 0:8], io["fin"]).then_inc(par2_in, 16)
            pool.wait_ge(y_ready, 2 + 2 * DEPTH + 1)
            pool.dma_start(kpn(io["out"]), yT).then_inc(out_done, 16)
            pool.wait_ge(out_done, 16)

        @block.tensor
        def _(pe):
            f = Follow(pe, tensor_step, free)
            turn, spent = [0], []

            def mm(out, lhsT, rhs, start, stop, done=None, **kw):
                ins = nc.tensor.matmul(out, lhsT, rhs, start=start, stop=stop, **kw)
                if done is not None:
                    ins.then_inc(f.count(done), 1)
                elif spent:
                    ins.then_inc(f.count(w_used[spent.pop()]), 1)

            def chunk(k=KD, n=CW, slot=None, pieces=1):
                s = turn[0] % SLOTS if slot is None else slot
                turn[0] += 1
                pe.wait_ge(w_loaded[s], f.next(w_loaded[s], 16 * pieces))
                return tiles(ring(s)[:, 0:k * n], k), s

            def open_bank(b):
                pe.wait_ge(bank_free[b], f.now(bank_free[b]))
                f.bump(bank_free[b])

            def piece(t, pieces, ready):
                if t == 6:
                    pe.wait_ge(ready, f.next(ready))
                elif t % 2 == 0:
                    pe.wait_ge(pieces, f.next(pieces))

            def by_features(b, x, w, k, done, normed=False):
                for j in range(2):
                    for t in range(k):
                        if normed and j == 0:
                            piece(t, x_pieces, x_ready)
                        mm(bank[b][:, j * TOK:(j + 1) * TOK], w[:, t, j * P:(j + 1) * P], x[:, t, :],
                           t == 0, t == k - 1, done if (j, t) == (1, k - 1) else None)

            def features(b, x, k=KD, normed=False):
                w, s = chunk(k)
                open_bank(b)
                by_features(b, x, w, k, bank_full[b], normed)
                spent.append(s)

            def tokens(b, x):
                w, s = chunk()
                open_bank(b)
                for j in range(2):
                    for t in range(KD):
                        mm(bank[b][:, j * CW:(j + 1) * CW], x[:, t, j * P:(j + 1) * P], w[:, t, :],
                           t == 0, t == KD - 1, bank_full[b] if (j, t) == (1, KD - 1) else None)
                spent.append(s)

            def modulation(b, c):
                turn[0] += 1
                w = tiles(ring(ada_slot(c)), KD)
                pe.wait_ge(mod_ready, f.next(mod_ready))
                open_bank(b)
                for j in range(2):
                    for t in range(2):
                        mm(bank[b][:, j:j + 1], w[:, t, j * P:(j + 1) * P], one, t == 0, t == 1,
                           bank_full[b] if (j, t) == (1, 1) else None)
                spent.append(ada_slot(c))

            def taken(b):
                pe.wait_ge(bank_free[b], f.now(bank_free[b]))

            def norm_mean():
                for t in range(KD):
                    mm(bank[5][:, 0:TOK], ones[:, :], yT[:, t, :], t == 0, t == KD - 1,
                       mean_ready if t == KD - 1 else None)

            def norm_var():
                for t in range(KD):
                    if t % 2 == 0:
                        pe.wait_ge(squares_ready, f.next(squares_ready))
                    mm(bank[4][:, 0:TOK], ones[:, :], squares[:, t, :], t == 0, t == KD - 1,
                       var_ready if t == KD - 1 else None)

            def turn_probs(u, n):
                pe.wait_ge(probs_ready, f.next(probs_ready))
                b = 4 + u % 2
                open_bank(b)
                for i in range(n):
                    ins = nc.tensor.transpose(bank[b][:, i * P:(i + 1) * P], probs[:, u % 2, i * P:(i + 1) * P], ident)
                ins.then_inc(f.count(bank_full[b]), 1)

            def probs_turned(u):
                pe.wait_ge(bank_free[4 + u % 2], f.now(bank_free[4 + u % 2]))

            def ffn(n, per):
                seq = [0]
                pe.wait_ge(x_lo_ready, f.next(x_lo_ready))
                open_sums()

                def halves(s, k, n):
                    h = seq[0] % 2
                    seq[0] += 1
                    pe.wait_ge(w_used[s], f.next(w_used[s]))
                    return [tiles(t[:, h, 0:k * n], k) for t in (w_hi, w_lo)]

                def up(p, i):
                    for o, full in ((0, gate_full[p]), (1, up_full[p])):
                        hi, lo = halves(3 * p + o, KD, CW)
                        for j in range(2):
                            for t in range(KD):
                                if isinstance(i, int) and (i, o, j) == (0, 0, 0) and t in (2, 4, 6):
                                    pe.wait_ge(x_lo_ready, f.next(x_lo_ready))
                                cols, out = slice(j * P, (j + 1) * P), bank[2 * p + o][:, j * TOK:(j + 1) * TOK]
                                mm(out, hi[:, t, cols], x_hi[:, t, :], t == 0, False)
                                mm(out, hi[:, t, cols], x_lo[:, t, :], False, False)
                                mm(out, lo[:, t, cols], x_hi[:, t, :], False, t == KD - 1, full if (j, t) == (1, KD - 1) else None)

                def down(p, i):
                    hi, lo = halves(3 * p + 2, 2, D)
                    pe.wait_ge(act_ready[p], f.next(act_ready[p]))
                    for t in range(2):
                        for n in range(KD):
                            cols, out = slice(n * P, (n + 1) * P), bank[4 + n // 2][:, (n % 2) * TOK:(n % 2 + 1) * TOK]
                            mm(out, hi[:, t, cols], act_hi[:, p, t, :], False, False, skip_group_check=True)
                            mm(out, hi[:, t, cols], act_lo[:, p, t, :], False, False, skip_group_check=True)
                            mm(out, lo[:, t, cols], act_hi[:, p, t, :], False, False,
                               down_done if (t, n) == (1, KD - 1) else None, skip_group_check=True)

                ffn_steps(up, down, n, pe, per, f)

            def open_sums():
                for b in range(4, 8):
                    mm(bank[b][:, :], zeros[0:1, 0:P], zeros[0:1, :], True, False, skip_group_check=True)

            def close_sums():
                for b in range(4, 8):
                    mm(bank[b][:, :], zeros[0:1, 0:P], zeros[0:1, :], False, True, ffn_summed if b == 7 else None,
                       skip_group_check=True)

            pe.wait_ge(inputs_in, f.next(inputs_in, 48))
            pe.wait_ge(pool_step, f.next(pool_step))
            norm_mean()
            norm_var()
            pe.wait_ge(cond_ready, f.next(cond_ready))
            with f.trips(DEPTH, LAYER1) as l:
                turn[0] = 0
                for c in range(18):
                    if c in (4, 5, 10, 11):
                        tokens(c % 4, xT)
                    else:
                        features(c % 4, xT, normed=c == 0)
                    if c == 7:
                        for j in range(4):
                            open_bank(j)
                            mm(bank[j][:, :], rot, (qa, ka)[j // 2][:, 2 * (j % 2):2 * (j % 2) + 2, :], True, True, bank_full[j])
                pe.wait_ge(mixer_in, f.next(mixer_in))
                for u in range(18):
                    if u < 16:
                        b = u % 2
                        open_bank(b)
                        a, t, qt = u // 8, u // 2 % 4, u % 2
                        for m in range(2):
                            mm(bank[b][:, m * TOK:(m + 1) * TOK], qhalf[a][m][:, t, qt * P:(qt + 1) * P], (ka, kb)[a][:, t, :],
                               True, True, bank_full[b] if m else None)
                    if u < 12:
                        features(6 + u % 2, xT)
                        for i in range(2):
                            modulation(2 + i, 2 * u + i)
                    if 1 <= u <= 16:
                        turn_probs(u - 1, 2 if u - 1 < 8 else 4)
                    if u == 10:
                        pe.wait_ge(sub_squares, f.next(sub_squares))
                        for h in range(4):
                            b = 4 + h // 2
                            if h % 2 == 0:
                                open_bank(b)
                            mm(bank[b][:, (h % 2) * TOK:(h % 2 + 1) * TOK], ones[:, :], ka[:, h, :], True, True,
                               bank_full[b] if h % 2 else None)
                    if u >= 3 and u % 2 == 1:
                        n = (u - 3) // 2
                        probs_turned(u - 2)
                        b = 2 + n % 2
                        open_bank(b)
                        for m in range(1 if n < 4 else 2):
                            for t in range(2):
                                if n < 4:
                                    v, out = va[:, t, n * P:(n + 1) * P], bank[b][:, 0:TOK]
                                else:
                                    h = 2 * (n - 4) + m
                                    v, out = vb[:, t, 64 * h:64 * h + 64], bank[b][64 * m:64 * m + 64, 0:TOK]
                                mm(out, v, probsT[:, n % 2, m, t, :], t == 0, t == 1,
                                   bank_full[b] if t and (n < 4 or m) else None)
                pe.wait_ge(heads_ready, f.next(heads_ready))
                for n in range(4):
                    for br, src in enumerate((qa, qb, hc)):
                        features((3 * n + br) % 4, src, 4)
                pe.wait_ge(merged_ready, f.next(merged_ready))
                for n in range(4):
                    features(n, merged)
                pe.wait_ge(mem_in, 16)
                for n in range(4):
                    features(n, memT)
                taken(3)
                norm_mean()
                for n in range(2):
                    tokens(n, memT)
                norm_var()
                for n in range(2):
                    tokens(2 + n, memT)
                for n in range(4):
                    features(n, xT, normed=n == 0)
                taken(3)
                for u in range(6):
                    if u < 4:
                        b = u % 2
                        open_bank(b)
                        for m in range(2):
                            h, qt = 2 * (u // 2) + m, u % 2
                            for t in range(2):
                                mm(bank[b][:, m * TOK:(m + 1) * TOK],
                                   (qa, ka)[h // 2][:, 2 * (h % 2) + t, qt * P:(qt + 1) * P],
                                   (qb, kb)[h // 2][:, 2 * (h % 2) + t, :], t == 0, t == 1, bank_full[b] if m and t else None)
                    if 1 <= u <= 4:
                        turn_probs(u - 1, 4)
                    if u >= 3 and u % 2 == 1:
                        n = (u - 3) // 2
                        probs_turned(u - 2)
                        for m in range(2):
                            h, b = 2 * n + m, 2 + m
                            open_bank(b)
                            for j in range(2):
                                for t in range(2):
                                    mm(bank[b][:, j * TOK:(j + 1) * TOK],
                                       (va, vb)[n][:, t, m * TOK + j * P:m * TOK + (j + 1) * P],
                                       probsT[:, n % 2, m, t, :], t == 0, t == 1, bank_full[b] if j and t else None)
                taken(3)
                for n in range(4):
                    features(n, merged)
                taken(3)
                norm_mean()
                norm_var()
                f.bump(x_ready)
                f.bump(x_pieces, 3)
                ffn(FF1 // CW, FFN1_TRIP)
                close_sums()
                pe.wait_ge(y_ready, f.next(y_ready))
                norm_mean()
                norm_var()

            f.bump(x_ready)
            f.bump(x_pieces, 3)
            for l in range(DEPTH):
                turn[0] = 0
                norm_var()
                w, s = chunk(KD, 24, pieces=2)
                open_bank(3)
                for t in range(KD):
                    piece(t, y_pieces, y_ready)
                    mm(bank[3][0:16, 0:TOK], w[:, t, 0:16], yT[:, t, :], t == 0, t == KD - 1)
                for j in range(2):
                    for t in range(KD):
                        mm(bank[3][:, TOK + 8 * j:TOK + 8 * j + 8], yT[:, t, j * P:(j + 1) * P], w[:, t, 16:24],
                           t == 0, t == KD - 1, bank_full[3] if (j, t) == (1, KD - 1) else None)
                spent.append(s)
                for b in (0, 1, 2, 3, 0):
                    features(b, yT)
                open_bank(1)
                for j in range(2):
                    mm(bank[1][:, j * TOK:(j + 1) * TOK], kb[0:16, 2 + l, j * P:(j + 1) * P], alr[0:16, :], True, True,
                       bank_full[1] if j else None)
                for b in (2, 3):
                    tokens(b, yT)
                for b in range(4):
                    features(b, yT)
                pe.wait_ge(conv_silu, f.next(conv_silu))
                for t in range(2):
                    open_bank(2 + t)
                    for j in range(4):
                        ins = nc.tensor.transpose(bank[2 + t][:, j * P:(j + 1) * P], qb[:, j, t * P:(t + 1) * P], ident)
                    ins.then_inc(f.count(bank_full[2 + t]), 1)
                open_bank(1)
                nc.tensor.transpose(bank[1][:, 0:P], ka[:, 0, 0:P], ident).then_inc(f.count(bank_full[1]), 1)
                pe.wait_ge(gla_in, f.next(gla_in))
                open_bank(1)
                for t in range(2):
                    for j in range(2):
                        ins = nc.tensor.transpose(bank[1][:, (2 * t + j) * P:(2 * t + j + 1) * P], ktail[:, j, t * P:(t + 1) * P], ident)
                ins.then_inc(f.count(bank_full[1]), 1)
                for a in range(2):
                    open_bank(2 + a)
                    for h in range(4):
                        mm(bank[2 + a][:, h * P:(h + 1) * P], ke[:, h // 2, a * P:(a + 1) * P],
                           qe[h % 2][:, h // 2, a * P:(a + 1) * P], True, True, bank_full[2 + a] if h == 3 else None)
                taken(1)
                for j in range(2):
                    open_bank(j)
                    for n in range(3):
                        for m in range(2):
                            h = 2 * j + m
                            mm(bank[j][64 * m:64 * m + 64, n * P:(n + 1) * P], ktok[n % 2][:, n // 2, h * 64:h * 64 + 64],
                               va[:, n // 2, h * P:(h + 1) * P], True, True, bank_full[j] if (n, m) == (2, 1) else None)
                for j in range(2):
                    open_bank(j)
                    for m in range(2):
                        h = 2 * j + m
                        for a in range(2):
                            at = m * TOK + a * P
                            mm(bank[j][:, at:at + P], va[:, a, h * P:(h + 1) * P], att[:, a, h, :], True, False,
                               skip_group_check=True)
                            for n in range(max(1, 2 * a), 2 * a + 2):
                                at = m * TOK + n * 64
                                mm(bank[j][:, at:at + 64], states[:, n - 1, j, :], qe[m][:, j, n * 64:n * 64 + 64],
                                   False, n == 2 * a + 1, bank_full[j] if (m, n) == (1, 3) else None, skip_group_check=True)
                pe.wait_ge(normed_sq, f.next(normed_sq))
                for j in range(2):
                    open_bank(4 + j)
                    for m in range(2):
                        mm(bank[4 + j][:, m * TOK:(m + 1) * TOK], ones[:, :], osq[:, 2 * j + m, :], True, True,
                           bank_full[4 + j] if m else None)
                pe.wait_ge(dta_ready, f.next(dta_ready))
                for q in range(4):
                    open_bank(q)
                    for i in range(4):
                        c, h = q // 2, 4 * (q % 2) + i
                        mm(bank[q][:, i * P:(i + 1) * P], dta[:, c, h:h + 1].to_broadcast([P, P]), tri, True, True,
                           bank_full[q] if i == 3 else None)
                open_bank(0)
                for c in range(2):
                    mm(bank[0][:, 8 * c:8 * c + 8], tri, dta[:, c, :], True, True)
                mm(bank[0][:, 16:24], ones[:, :], dta[:, 0, :], True, True, bank_full[0])
                pe.wait_ge(ssd_in, f.next(ssd_in))
                open_bank(1)
                for c in range(2):
                    for g in range(2):
                        mm(bank[1][:, (2 * c + g) * P:(2 * c + g + 1) * P], ka[:, 0, c * P:(c + 1) * P], cmg[:, g, c * P:(c + 1) * P],
                           True, True, bank_full[1] if (c, g) == (1, 1) else None)
                pe.wait_ge(state_in, f.next(state_in))
                open_bank(2)
                mm(bank[2][:, :], btok, xw, True, True, bank_full[2])
                pe.wait_ge(pair_ready, f.next(pair_ready))
                for j in range(2):
                    open_bank(j)
                    for i in range(2):
                        for m in range(2):
                            h = 4 * j + 2 * i + m
                            for c in range(2):
                                out = bank[j][64 * m:64 * m + 64, i * TOK + c * P:i * TOK + (c + 1) * P]
                                mm(out, vb[:, c, h * 64:h * 64 + 64], seg[:, c, h, :], True, c == 0, skip_group_check=True)
                            mm(out, state[:, h * 64:h * 64 + 64], cme[:, h, :], False, True,
                               bank_full[j] if (i, m) == (1, 1) else None, skip_group_check=True)
                pe.wait_ge(normed_sq, f.next(normed_sq))
                open_bank(4)
                for j in range(4):
                    mm(bank[4][:, 0:TOK], ones[:, :], hc[:, j, :], j == 0, j == 3, bank_full[4] if j == 3 else None)
                pe.wait_ge(merged_ready, f.next(merged_ready))
                for n in range(4):
                    features(n, merged)
                pe.wait_ge(x_ready, f.next(x_ready))
                norm_var()
                if l == 0:
                    f.bump(y_ready)
                    f.bump(y_pieces, 3)
                    ffn(FF2 // CW, FFN2_TRIP)
                else:
                    w, s = chunk(KD, 8)
                    open_bank(0)
                    for j in range(2):
                        for t in range(KD):
                            if j == 0:
                                piece(t, y_pieces, y_ready)
                            mm(bank[0][:, 8 * j:8 * j + 8], yT[:, t, j * P:(j + 1) * P], w[:, t, :], t == 0, t == KD - 1,
                               bank_full[0] if (j, t) == (1, KD - 1) else None)
                    spent.append(s)
                    for q in range(4):
                        open_bank(4 + q)
                        for i in range(4):
                            ins = nc.tensor.transpose(bank[4 + q][:, i * P:(i + 1) * P],
                                                      yT[:, 4 * (q % 2) + i, (q // 2) * P:(q // 2 + 1) * P], ident)
                        ins.then_inc(f.count(bank_full[4 + q]), 1)
                    pe.wait_ge(chosen_ready, f.next(chosen_ready))
                    open_bank(0)
                    every = one.to_broadcast([P, P])
                    mm(bank[0][:, 0:8], tri, chosen[:, 0, :], True, True)
                    mm(bank[0][:, 8:16], tri, chosen[:, 1, :], True, False)
                    mm(bank[0][:, 8:16], every, chosen[:, 0, :], False, True)
                    mm(bank[0][:, 16:24], every, chosen[:, 0, :], True, False)
                    mm(bank[0][:, 16:24], every, chosen[:, 1, :], False, True, bank_full[0])

                    seq = [0]

                    def halves(s, k, n):
                        h = seq[0] % 3
                        seq[0] += 1
                        pe.wait_ge(w_used[s], f.next(w_used[s]))
                        return [tiles(t[:, h, 0:k * n], k) for t in (ew_hi, ew_lo)]

                    def gather(q):
                        pe.wait_ge(gather_free, f.now(gather_free))
                        for i in range(4):
                            for t in range(2):
                                k = 4 * q + i
                                mm(bank[7][:, i * P:(i + 1) * P], htok[:, t, k * P:(k + 1) * P], select[:, t, :],
                                   t == 0, t == 1, gather_full if (i, t) == (3, 1) else None)
                        f.bump(gather_free)

                    def first(slot, b, done):
                        hi, lo = halves(slot, KD, CW)
                        for t in range(KD):
                            mm(bank[b][:, 0:CW], xe_hi[:, t, :], hi[:, t, :], t == 0, False)
                            mm(bank[b][:, 0:CW], xe_hi[:, t, :], lo[:, t, :], False, False)
                            mm(bank[b][:, 0:CW], xe_lo[:, t, :], hi[:, t, :], False, t == KD - 1, done if t == KD - 1 else None)

                    def gate(p):
                        first(3 * p, 2 * p, gate_full[p])

                    def up(p):
                        first(3 * p + 1, 2 * p + 1, up_full[p])

                    def turn(p):
                        pe.wait_ge(turn_ready[p], f.next(turn_ready[p]))
                        for j in range(2):
                            ins = nc.tensor.transpose(bank[6][:, j * P:(j + 1) * P], act[:, p, j, 0:P], ident)
                        ins.then_inc(f.count(turned[p]), 1)

                    def down(p):
                        hi, lo = halves(3 * p + 2, 2, D)
                        pe.wait_ge(act_ready[p], f.next(act_ready[p]))
                        for t in range(2):
                            for n in range(2):
                                cols = slice(n * 512, (n + 1) * 512)
                                mm(bank[4 + n][:, :], eact_hi[:, p, t, :], hi[:, t, cols], False, False, skip_group_check=True)
                                mm(bank[4 + n][:, :], eact_hi[:, p, t, :], lo[:, t, cols], False, False, skip_group_check=True)
                                mm(bank[4 + n][:, :], eact_lo[:, p, t, :], hi[:, t, cols], False, False,
                                   down_done if (t, n) == (1, 1) else None, skip_group_check=True)

                    def experts():
                        pe.wait_ge(select_ready, f.next(select_ready))
                        taken(7)
                        gather(0)
                        gather(1)
                        taken(0)
                        with f.trips(EXPERTS, EXPERT):
                            seq[0] = 0
                            pe.wait_ge(gather_free, f.now(gather_free))
                            pe.wait_ge(result_free, f.now(result_free))
                            gate(0)
                            up(0)
                            for n in range(2):
                                open_bank(4 + n)
                                mm(bank[4 + n][:, :], zeros[0:1, 0:P], zeros[0:1, :], True, False, skip_group_check=True)
                            with f.trips((FF2 // CW - 1) // 2, FFN3_TRIP):
                                for p in range(2):
                                    gate(1 - p)
                                    turn(p)
                                    up(1 - p)
                                    down(p)
                            gate(1)
                            turn(0)
                            up(1)
                            pe.wait_ge(select_ready, f.next(select_ready))
                            gather(0)
                            down(0)
                            for t in range(2):
                                ins = nc.tensor.transpose(bank[0][:, t * P:(t + 1) * P], weigh[:, t, :], ident)
                            ins.then_inc(f.count(back_full), 1)
                            turn(1)
                            gather(1)
                            down(1)
                            for n in range(2):
                                mm(bank[4 + n][:, :], zeros[0:1, 0:P], zeros[0:1, :], False, True, bank_full[4 + n],
                                   skip_group_check=True)
                            pe.wait_ge(back_free, f.next(back_free))
                            for q in range(4):
                                if q % 2 == 0:
                                    taken(4 + q // 2)
                                for j in range(2):
                                    k = 2 * q + j
                                    mm(bank[q][:, j * TOK:(j + 1) * TOK], ye[:, k * P:(k + 1) * P], back, True, True,
                                       result_full if j else None)
                            f.bump(result_free, 4)

                    experts()
                    pe.wait_ge(crowd_ready, f.next(crowd_ready))
                    with pe.If(pe.value_load(crowded[0:1, 0:1], min_val=0, max_val=1) > 0):
                        experts()
                if l == 0:
                    close_sums()
                pe.wait_ge(x_ready, f.next(x_ready))
            norm_var()

        @block.vector
        def _(dve):
            f = Follow(dve, vector_step, free)
            v = nc.vector
            cos2, sin2 = (spread(const[:, c:c + TOK], 2) for c in (C_COS, C_SIN))

            def pairs(b):
                return tiles(bank[b][:, :], 2)

            def take(b, dst, src=None):
                dve.wait_ge(bank_full[b], f.next(bank_full[b]))
                v.tensor_copy(dst, pairs(b) if src is None else src).then_inc(f.count(bank_free[b]), 1)

            def norm_centre():
                dve.wait_ge(mean_ready, f.next(mean_ready))
                for q in range(4):
                    y = yT[:, 2 * q:2 * q + 2, :]
                    v.tensor_tensor(y, y, spread(bank[5][:, 0:TOK], 2), ALU.subtract).then_inc(f.count(centred), 1)

            def normed(dst, src, gains, biases, pieces, done, dense=False):
                dve.wait_ge(std_ready, f.next(std_ready))
                v.reciprocal(std[:, :], std[:, :]).then_inc(f.count(vector_step), 1)
                dve.wait_ge(f.last, f.now(f.last))
                for q in range(4):
                    v.tensor_tensor(yT[:, 2 * q:2 * q + 2, :], src[:, 2 * q:2 * q + 2, :], spread(std[:, :], 2), ALU.mult).then_inc(f.count(vector_step), 1)
                    dve.wait_ge(f.last, f.now(f.last))
                    for k in range(2 * q, 2 * q + 2):
                        ins = v.tensor_scalar(dst[:, k, :], yT[:, k, :], gains[:, k:k + 1], biases[:, k:k + 1], ALU.mult, ALU.add)
                    ins.then_inc(f.count(done if q == 3 else pieces), 1)
                    if dense and q:
                        x_low(dst, q - 1)
                if dense:
                    x_low(dst, 3)

            def norm_finish(gains, biases, dense=False):
                normed(xT, yT, gains, biases, x_pieces, x_ready, dense)

            def residual(n, b, done):
                v.scalar_tensor_tensor(yT[:, 2 * n:2 * n + 2, :], xT[:, 2 * n:2 * n + 2, :], ALPHA, pairs(b),
                                       ALU.mult, ALU.add).then_inc(f.count(done), 1)

            def peaks(u, scale, add=None):
                b = u % 2
                dve.wait_ge(bank_full[b], f.next(bank_full[b]))
                s = tiles(scores[:, b, :], 2)
                if add is None:
                    v.tensor_scalar(s, pairs(b), -scale, None, ALU.mult).then_inc(f.count(bank_free[b]), 1)
                else:
                    v.scalar_tensor_tensor(s, pairs(b), -scale, add, ALU.mult, ALU.subtract).then_inc(f.count(bank_free[b]), 1)
                dve.wait_ge(f.last, f.now(f.last))
                v.tensor_reduce(peak[:, b, :], s, AX.X, ALU.min).then_inc(f.count(peak_ready), 1)

            def normalise(u, difference):
                b = u % 2
                dve.wait_ge(exp_ready, f.next(exp_ready))
                v.reciprocal(total[:, b, :], total[:, b, :]).then_inc(f.count(vector_step), 1)
                dve.wait_ge(f.last, f.now(f.last))
                p = tiles(probs[:, b, :], 2)
                if difference:
                    v.tensor_tensor(total[:, b, 1:2], total[:, b, 1:2], lam[:, 4:5], ALU.mult).then_inc(f.count(vector_step), 1)
                    dve.wait_ge(f.last, f.now(f.last))
                    v.tensor_scalar(p[:, 1, :], p[:, 1, :], total[:, b, 1:2], None, ALU.mult).then_inc(f.count(vector_step), 1)
                    dve.wait_ge(f.last, f.now(f.last))
                    v.scalar_tensor_tensor(p[:, 0, :], p[:, 0, :], total[:, b, 0:1], p[:, 1, :], ALU.mult, ALU.add).then_inc(f.count(probs_ready), 1)
                else:
                    r = total[:, b, :].rearrange("p (m o) -> p m o", o=1).broadcast_to([P, 2, TOK])
                    v.tensor_tensor(p, p, r, ALU.mult).then_inc(f.count(probs_ready), 1)

            def split_low(s, h, last=None):
                dve.wait_ge(hi_ready[h], f.next(hi_ready[h]))
                v.tensor_tensor(w_lo[:, h, :], ring(s), w_hi[:, h, :].bitcast(F32), ALU.subtract).then_inc(w_used[s], 1)

            def x_low(x, q):
                ks = slice(2 * q, 2 * q + 2)
                dve.wait_ge(x_hi_ready, f.next(x_hi_ready))
                v.tensor_tensor(x_lo[:, ks, :], x[:, ks, :], x_hi[:, ks, :].bitcast(F32), ALU.subtract).then_inc(f.count(x_lo_ready), 1)

            def dense(form, n, per):
                split_low(1, 1)

                def finish(p):
                    dve.wait_ge(up_full[p], f.next(up_full[p]))
                    dve.wait_ge(silu_ready[p], f.next(silu_ready[p]))
                    v.tensor_tensor(act[:, p, :, :], silu[:, p, :, :], pairs(2 * p + 1), ALU.mult).then_inc(f.count(product_ready[p]), 1)
                    dve.wait_ge(act_hi_ready[p], f.next(act_hi_ready[p]))
                    v.tensor_tensor(act_lo[:, p, :, :], act[:, p, :, :], act_hi[:, p, :, :].bitcast(F32), ALU.subtract).then_inc(f.count(act_ready[p]), 1)

                dense_steps(split_low, form, finish, n, dve, per, f)

            dve.wait_ge(inputs_in, f.next(inputs_in, 48))
            norm_centre()
            norm_finish(eln[:, 0:8], eln[:, 8:16])
            with f.trips(DEPTH, LAYER1) as l:
                dve.wait_ge(par_in, f.next(par_in, 16))
                lv = par[:, A_LAMV:A_LAMV + 256].rearrange("p (a b d) -> p a b d", a=2, b=2)
                v.tensor_tensor(tiles(scores[:, 0, 0:128], 2), lv[:, :, 0, :], lv[:, :, 1, :], ALU.mult).then_inc(f.count(vector_step), 1)
                v.tensor_tensor(lam[:, 5:6], par[:, A_SUB:A_SUB + 1], par[:, A_LAM1:A_LAM1 + 1], ALU.mult).then_inc(f.count(vector_step), 1)
                dve.wait_ge(f.last, f.now(f.last))
                v.tensor_reduce(lam[:, 0:2], tiles(scores[:, 0, 0:128], 2), AX.X, ALU.add).then_inc(f.count(lam_dot), 1)
                dve.wait_ge(lam_exp, f.next(lam_exp))
                v.scalar_tensor_tensor(lam[:, 4:5], lam[:, 3:4], lam[:, 2:3], par[:, A_LAM0:A_LAM0 + 1],
                                       ALU.subtract, ALU.subtract).then_inc(f.count(vector_step), 1)
                for c in range(18):
                    b, i = c % 4, c % 2
                    if c in (6, 7):
                        dve.wait_ge(bank_full[b], f.next(bank_full[b]))
                        for m in range(2):
                            v.tensor_scalar(qhalf[1][m][:, 2 * i:2 * i + 2, :], pairs(b), half[m], None, ALU.mult).then_inc(f.count(bank_free[b] if m else vector_step), 1)
                    elif c in (4, 5, 10, 11):
                        take(b, (va if c < 6 else vb)[:, :, i * CW:(i + 1) * CW])
                    else:
                        take(b, (qa, ka, None, None, kb, None, gb, gc, hc)[c // 2][:, 2 * i:2 * i + 2, :])
                    if c == 7:
                        for j in range(4):
                            src, tmp = (qa, ka)[j // 2][:, 2 * (j % 2):2 * (j % 2) + 2, :], tiles(scores[:, 0, :], 2)
                            dve.wait_ge(bank_full[j], f.next(bank_full[j]))
                            v.tensor_tensor(tmp, pairs(j), sin2, ALU.mult).then_inc(f.count(bank_free[j]), 1)
                            v.tensor_tensor(src, src, cos2, ALU.mult).then_inc(f.count(vector_step), 1)
                            dve.wait_ge(f.last, f.now(f.last))
                            v.tensor_tensor(src, src, tmp, ALU.add).then_inc(f.count(vector_step), 1)
                            dve.wait_ge(f.last, f.now(f.last))
                            if j < 2:
                                for m in range(2):
                                    v.tensor_scalar(qhalf[0][m][:, 2 * j:2 * j + 2, :], src, half[m], None, ALU.mult).then_inc(f.count(vector_step), 1)
                dve.wait_ge(bias_in, f.next(bias_in, 256))
                wide = bias.rearrange("p h j c -> p (h j) c")
                v.tensor_tensor(wide, wide, spread(const[:, C_WIN:C_WIN + 64], 48), ALU.add).then_inc(f.count(vector_step), 1)
                dve.wait_ge(f.last, f.now(f.last))
                v.tensor_tensor(gc[:, :, :], gc[:, :, :], hc[:, :, :], ALU.mult).then_inc(f.count(mixer_in), 1)
                for u in range(18):
                    if u < 8:
                        peaks(u, 0.125)
                    elif u < 16:
                        hp, at = u // 2 - 4, 2 - 2 * (u % 2)
                        peaks(u, 0.125, bias[:, 2 * hp:2 * hp + 2, at:at + 4, :].rearrange("p h j c -> p h (j c)"))
                    if 1 <= u <= 16:
                        normalise(u - 1, u - 1 < 8)
                    if u < 12:
                        for c in range(2 * u, 2 * u + 2):
                            w = tiles(ring(ada_slot(c)), KD)
                            dve.wait_ge(mod_scaled, f.next(mod_scaled))
                            v.tensor_tensor(w[:, 0:4, :], w[:, 0:4, :], w[:, 4:8, :], ALU.add).then_inc(f.count(vector_step), 1)
                            dve.wait_ge(f.last, f.now(f.last))
                            v.tensor_tensor(w[:, 0:2, :], w[:, 0:2, :], w[:, 2:4, :], ALU.add).then_inc(f.count(mod_ready), 1)
                        for i in range(2):
                            c = 2 * u + i
                            take(2 + i, mod[:, 2 * c:2 * c + 2], bank[2 + i][:, 0:2])
                    if 2 <= u < 6:
                        t = u - 2
                        w = [par[:, A_SCW + 4 * k + t:A_SCW + 4 * k + t + 1] for k in range(3)]
                        dve.wait_ge(f.last, f.now(f.last))
                        v.tensor_scalar(hc[:, t, :], gc[:, t, :], w[1], None, ALU.mult).then_inc(f.count(vector_step), 1)
                        dve.wait_ge(f.last, f.now(f.last))
                        v.scalar_tensor_tensor(hc[:, t, 1:TOK], gc[:, t, 0:TOK - 1], w[0], hc[:, t, 1:TOK], ALU.mult, ALU.add).then_inc(f.count(vector_step), 1)
                        dve.wait_ge(f.last, f.now(f.last))
                        v.scalar_tensor_tensor(hc[:, t, 0:TOK - 1], gc[:, t, 1:TOK], w[2], hc[:, t, 0:TOK - 1], ALU.mult, ALU.add).then_inc(f.count(vector_step), 1)
                        dve.wait_ge(f.last, f.now(f.last))
                        v.tensor_tensor(hc[:, t, :], hc[:, t, :], gb[:, t, :], ALU.mult).then_inc(f.count(vector_step), 1)
                    if u >= 3 and u % 2 == 1:
                        n = (u - 3) // 2
                        b = 2 + n % 2
                        take(b, (qa[:, n, :] if n < 4 else qb[:, n - 4, :]), bank[b][:, 0:TOK])
                        if n < 4:
                            dve.wait_ge(f.last, f.now(f.last))
                            v.tensor_tensor(ka[:, n, :], qa[:, n, :], qa[:, n, :], ALU.mult).then_inc(f.count(sub_squares if n == 3 else vector_step), 1)
                    if u == 14:
                        dve.wait_ge(sub_std, f.next(sub_std))
                        v.reciprocal(ka[:, :, :], ka[:, :, :]).then_inc(f.count(vector_step), 1)
                dve.wait_ge(f.last, f.now(f.last))
                v.scalar_tensor_tensor(qa[:, :, :], qa[:, :, :], lam[:, 5:6], ka[:, :, :], ALU.mult, ALU.mult).then_inc(f.count(heads_ready), 1)
                dve.wait_ge(gates_ready, f.next(gates_ready))
                for n in range(4):
                    for br in range(3):
                        c = 3 * n + br
                        b = c % 4
                        dve.wait_ge(bank_full[b], f.next(bank_full[b]))
                        g = gates[:, 8 * br + 2 * n:8 * br + 2 * n + 2, :]
                        dst = merged[:, 2 * n:2 * n + 2, :] if br == 0 else tiles(scores[:, c % 2, :], 2)
                        dve.wait_ge(f.last, f.now(f.last))
                        v.tensor_tensor(dst, pairs(b), g, ALU.mult).then_inc(f.count(bank_free[b]), 1)
                        if br:
                            dve.wait_ge(f.last, f.now(f.last))
                            m = merged[:, 2 * n:2 * n + 2, :]
                            v.tensor_tensor(m, m, dst, ALU.add).then_inc(f.count(merged_ready if (n, br) == (3, 2) else vector_step), 1)
                for n in range(4):
                    dve.wait_ge(bank_full[n], f.next(bank_full[n]))
                    residual(n, n, bank_free[n])
                for n in range(4):
                    take(n, (qb, kb)[n // 2][:, 2 * (n % 2):2 * (n % 2) + 2, :])
                norm_centre()
                for n in range(2):
                    take(n, va[:, :, n * CW:(n + 1) * CW])
                norm_finish(par[:, A_LNG:A_LNG + 8], par[:, A_LNB:A_LNB + 8])
                for n in range(2):
                    take(2 + n, vb[:, :, n * CW:(n + 1) * CW])
                for n in range(4):
                    take(n, (qa, ka)[n // 2][:, 2 * (n % 2):2 * (n % 2) + 2, :])
                for u in range(6):
                    if u < 4:
                        peaks(u, 1.0 / 16)
                    if 1 <= u <= 4:
                        normalise(u - 1, False)
                    if u >= 3 and u % 2 == 1:
                        for m in range(2):
                            h = 2 * ((u - 3) // 2) + m
                            take(2 + m, merged[:, 2 * h:2 * h + 2, :])
                v.tensor_copy(mods[:, bass.ds(l, 1), :], mod[:, :].rearrange("p (o c) -> p o c", o=1)).then_inc(f.count(vector_step), 1)
                for n in range(4):
                    dve.wait_ge(bank_full[n], f.next(bank_full[n]))
                    residual(n, n, bank_free[n])
                norm_centre()
                split_low(0, 0)
                norm_finish(par[:, A_LNG + 8:A_LNG + 16], par[:, A_LNB + 8:A_LNB + 16], True)

                def form(p, i):
                    v.tensor_copy(ffp[:, :], par[:, bass.ds(i * 8 + A_FF, 8)]).then_inc(f.count(vector_step), 1)
                    dve.wait_ge(f.last, f.now(f.last))
                    dve.wait_ge(gate_full[p], f.next(gate_full[p]))
                    g, b = pairs(2 * p), 2 * p
                    for j in range(2):
                        v.tensor_scalar(conva[:, p, j, :], g[:, j, :], ffp[:, 4 * j + 1:4 * j + 2], ffp[:, 4 * j + 3:4 * j + 4],
                                        ALU.mult, ALU.add).then_inc(f.count(vector_step), 1)
                    dve.wait_ge(f.last, f.now(f.last))
                    for j in range(2):
                        v.scalar_tensor_tensor(conva[:, p, j, 1:TOK], g[:, j, 0:TOK - 1], ffp[:, 4 * j:4 * j + 1],
                                               conva[:, p, j, 1:TOK], ALU.mult, ALU.add).then_inc(f.count(vector_step), 1)
                    dve.wait_ge(f.last, f.now(f.last))
                    for j in range(2):
                        v.scalar_tensor_tensor(conva[:, p, j, 0:TOK - 1], g[:, j, 1:TOK], ffp[:, 4 * j + 2:4 * j + 3],
                                               conva[:, p, j, 0:TOK - 1], ALU.mult, ALU.add).then_inc(f.count(conv_ready[p] if j else vector_step), 1)

                dense(form, FF1 // CW, FFN1_TRIP)
                dve.wait_ge(ffn_summed, f.next(ffn_summed))
                for n in range(4):
                    residual(n, 4 + n, y_ready if n == 3 else None)
                norm_centre()
                norm_finish(par[:, A_LNG + 16:A_LNG + 24], par[:, A_LNB + 16:A_LNB + 24])

            def rms_finish(l, which, dense=False):
                normed(yT, xT, gain, mods[:, l, 24 * which:24 * which + 8], y_pieces, y_ready, dense)

            def rms_gain(l, which, done=None):
                v.scalar_tensor_tensor(gain[:, :], mods[:, l, 24 * which + 8:24 * which + 16], 1.0,
                                       par2[l][:, 8 * which:8 * which + 8], ALU.add, ALU.mult).then_inc(f.count(done), 1)

            def add_gated(l, which, n, b, done):
                for i in range(2):
                    k = 2 * n + i
                    v.scalar_tensor_tensor(xT[:, k, :], pairs(b)[:, i, :], mods[:, l, 24 * which + 16 + k:24 * which + 17 + k],
                                           xT[:, k, :], ALU.mult, ALU.add).then_inc(f.count(done if i else vector_step), 1)

            dve.wait_ge(par2_in, f.next(par2_in, 80))
            for l in range(DEPTH):
                v.tensor_tensor(mods[:, l, :], mods[:, l, :], par2[l][:, B_ADA:B_ADA + 48], ALU.add).then_inc(f.count(vector_step), 1)
            for l in range(DEPTH):
                p2 = par2[l]
                dve.wait_ge(f.last, f.now(f.last))
                rms_gain(l, 0)
                rms_finish(l, 0)
                dve.wait_ge(bank_full[3], f.next(bank_full[3]))
                v.tensor_tensor(tiles(dtraw, 2), tiles(bank[3][:, TOK:TOK + 16], 2), spread(p2[:, B_DTB:B_DTB + 8], 2), ALU.add).then_inc(f.count(vector_step), 1)
                dve.wait_ge(f.last, f.now(f.last))
                v.scalar_tensor_tensor(dtabs, dtraw, -1.0, dtraw, ALU.mult, ALU.max).then_inc(f.count(vector_step), 1)
                v.tensor_copy(alr[0:16, :], bank[3][0:16, 0:TOK]).then_inc(f.count(bank_free[3]), 1)
                for c, dst in enumerate([qa[:, 0:2, :], qa[:, 2:4, :], hc[:, 0:2, :], hc[:, 2:4, :], kb[:, 0:2, :]]):
                    take(c % 4, dst)
                dve.wait_ge(f.last, f.now(f.last))
                raw = [hc[:, j, :] for j in range(4)] + [kb[:, j, :] for j in range(2)]
                dst = [qb[:, j, :] for j in range(4)] + [ka[:, j, :] for j in range(2)]
                for tap in (3, 2, 1, 0):
                    s = 3 - tap
                    for j in range(6):
                        w = p2[:, B_CW + 6 * tap + j:B_CW + 6 * tap + j + 1]
                        if s == 0:
                            ins = v.tensor_scalar(dst[j], raw[j], w, p2[:, B_CB + j:B_CB + j + 1], ALU.mult, ALU.add)
                        else:
                            ins = v.scalar_tensor_tensor(dst[j][:, s:TOK], raw[j][:, 0:TOK - s], w, dst[j][:, s:TOK], ALU.mult, ALU.add)
                    ins.then_inc(f.count(conv_in if tap == 0 else vector_step), 1)
                    dve.wait_ge(f.last, f.now(f.last))
                dve.wait_ge(bank_full[1], f.next(bank_full[1]))
                z = ka[:, 2:4, :]
                for j in range(2):
                    v.tensor_scalar(z[:, j, :], pairs(1)[:, j, :], p2[:, B_AB + j:B_AB + j + 1], None, ALU.add).then_inc(f.count(bank_free[1] if j else vector_step), 1)
                dve.wait_ge(f.last, f.now(f.last))
                v.scalar_tensor_tensor(tiles(scores[:, 0, :], 2), z, -1.0, z, ALU.mult, ALU.max).then_inc(f.count(decay_in), 1)
                dve.wait_ge(dt_ln, f.next(dt_ln))
                v.scalar_tensor_tensor(dt, dtraw, 0.0, dtabs, ALU.max, ALU.add).then_inc(f.count(vector_step), 1)
                dve.wait_ge(f.last, f.now(f.last))
                v.scalar_tensor_tensor(dta[:, :, :], tiles(dt, 2), -1.0, spread(aexp, 2), ALU.mult, ALU.mult).then_inc(f.count(dta_ready), 1)
                dve.wait_ge(decay_ln, f.next(decay_ln))
                v.scalar_tensor_tensor(z, z, 0.0, tiles(scores[:, 0, :], 2), ALU.min, ALU.subtract).then_inc(f.count(vector_step), 1)
                dve.wait_ge(f.last, f.now(f.last))
                v.tensor_scalar(z, z, 1.0 / 16, None, ALU.mult).then_inc(f.count(vector_step), 1)
                dve.wait_ge(f.last, f.now(f.last))
                run = probs[:, 0, :].rearrange("p (n c) -> p n c", c=64)
                zc = z.rearrange("p j (n c) -> p (j n) c", c=64)
                for n in range(8):
                    ins = v.tensor_tensor_scan(run[:, n, :], one.to_broadcast([P, 64]), zc[:, n, :], 0.0, ALU.mult, ALU.add)
                ins.then_inc(f.count(vector_step), 1)
                dve.wait_ge(f.last, f.now(f.last))
                v.tensor_tensor(scores[:, 1, :].rearrange("p (n c) -> p n c", c=64), run[:, :, 63:64].broadcast_to([P, 8, 64]), run,
                                ALU.subtract).then_inc(f.count(cum_ready), 1)
                dve.wait_ge(cum_exp, f.next(cum_exp))
                grow2, shrink, tail = tiles(probs[:, 1, :], 2), tiles(scores[:, 0, :], 2), tiles(scores[:, 1, :], 2)
                qs = tiles(probs[:, 0, :], 2)
                v.scalar_tensor_tensor(qs, qa[:, 0:2, :], 0.125, grow2, ALU.mult, ALU.mult).then_inc(f.count(vector_step), 1)
                v.tensor_tensor(ke, qa[:, 2:4, :], shrink, ALU.mult).then_inc(f.count(vector_step), 1)
                dve.wait_ge(f.last, f.now(f.last))
                for m in range(2):
                    v.tensor_scalar(qe[m], qs, half[m], None, ALU.mult).then_inc(f.count(vector_step), 1)
                v.tensor_tensor(ktail, qa[:, 2:4, :], tail, ALU.mult).then_inc(f.count(gla_in), 1)
                for t in range(2):
                    take(2 + t, va[:, :, t * CW:(t + 1) * CW])
                for c, dst in enumerate([gb[:, 0:2, :], gb[:, 2:4, :], gc[:, 0:2, :], gc[:, 2:4, :]]):
                    take(c, dst)
                v.memset(att, 0.0).then_inc(f.count(proj_ready), 1)
                for t in range(2):
                    dve.wait_ge(bank_full[2 + t], f.next(bank_full[2 + t]))
                    v.tensor_tensor(tiles(vb[:, t, :], 8), tiles(bank[2 + t][:, :], 8),
                                    dt[:, 8 * t:8 * t + 8].rearrange("p (h o) -> p h o", o=1).broadcast_to([P, 8, 64]), ALU.mult).then_inc(f.count(bank_free[2 + t]), 1)
                take(1, btok, bank[1][:, 0:P])
                dve.wait_ge(bank_full[1], f.next(bank_full[1]))
                for m in range(2):
                    v.tensor_scalar(ktok[m], pairs(1), half[m], None, ALU.mult).then_inc(f.count(bank_free[1] if m else vector_step), 1)
                allow = const[:, C_DIAG:C_DIAG + P].bitcast(mybir.dt.uint32)
                for a in range(2):
                    dve.wait_ge(bank_full[2 + a], f.next(bank_full[2 + a]))
                    v.copy_predicated(att[:, a, :, :], spread(allow, 4), tiles(bank[2 + a][:, :], 4)).then_inc(f.count(bank_free[2 + a]), 1)
                for j in range(2):
                    dve.wait_ge(bank_full[j], f.next(bank_full[j]))
                    for n in range(3):
                        new = bank[j][:, n * P:(n + 1) * P]
                        if n == 0:
                            ins = v.tensor_copy(states[:, 0, j, :], new)
                        else:
                            at = j * TOK + n * 64 + 63
                            ins = v.scalar_tensor_tensor(states[:, n, j, :], states[:, n - 1, j, :], probs[:, 1, at:at + 1], new, ALU.mult, ALU.add)
                        ins.then_inc(f.count(bank_free[j] if n == 2 else vector_step), 1)
                        dve.wait_ge(f.last, f.now(f.last))
                for j in range(2):
                    take(j, merged[:, 2 * j:2 * j + 2, :])
                dve.wait_ge(f.last, f.now(f.last))
                v.tensor_tensor(osq, merged[:, 0:4, :], merged[:, 0:4, :], ALU.mult).then_inc(f.count(normed_sq), 1)
                for q in range(4):
                    take(q, cumr[:, q * 512:(q + 1) * 512], bank[q][:, :])
                take(0, cumt[:, :], bank[0][:, 0:24])
                dve.wait_ge(f.last, f.now(f.last))
                for c in range(2):
                    for h in range(8):
                        at = (8 * c + h) * P
                        v.scalar_tensor_tensor(seg[:, c, h, :], cumr[:, at:at + P], cumt[:, 8 * c + h:8 * c + h + 1],
                                               const[:, C_BAN:C_BAN + P], ALU.subtract, ALU.add).then_inc(f.count(vector_step), 1)
                v.scalar_tensor_tensor(wtail, cumt[:, 16:24], float(D), cumt[:, 0:8], ALU.mult, ALU.subtract).then_inc(f.count(seg_ready), 1)
                for g in range(2):
                    v.tensor_scalar(cmg[:, g, :], ka[:, 1, :], half[g], None, ALU.mult).then_inc(f.count(ssd_in if g else vector_step), 1)
                dve.wait_ge(seg_exp, f.next(seg_exp))
                v.tensor_tensor(tiles(xw, 8), tiles(vb[:, 0, :], 8), wtail.rearrange("p (h o) -> p h o", o=1).broadcast_to([P, 8, 64]),
                                ALU.mult).then_inc(f.count(state_in), 1)
                dve.wait_ge(bank_full[1], f.next(bank_full[1]))
                for c in range(2):
                    for g in range(2):
                        s = seg[:, c, 4 * g:4 * g + 4, :]
                        v.tensor_tensor(s, s, spread(bank[1][:, (2 * c + g) * P:(2 * c + g + 1) * P], 4), ALU.mult).then_inc(f.count(bank_free[1] if (c, g) == (1, 1) else vector_step), 1)
                take(2, state, bank[2][:, :])
                for g in range(2):
                    v.tensor_tensor(cme[:, 4 * g:4 * g + 4, :], tiles(ecum, 8)[:, 4 * g:4 * g + 4, :], spread(cmg[:, g, P:TOK], 4),
                                    ALU.mult).then_inc(f.count(pair_ready if g else vector_step), 1)
                dve.wait_ge(normed_std, f.next(normed_std))
                v.reciprocal(osq[:, 0:2, :], osq[:, 0:2, :]).then_inc(f.count(vector_step), 1)
                for j in range(2):
                    dve.wait_ge(bank_full[j], f.next(bank_full[j]))
                    for i in range(2):
                        t = 2 * j + i
                        v.scalar_tensor_tensor(merged[:, 4 + t, :], qb[:, t, :], p2[:, B_DS + t:B_DS + t + 1], pairs(j)[:, i, :],
                                               ALU.mult, ALU.add).then_inc(f.count(bank_free[j] if i else vector_step), 1)
                dve.wait_ge(f.last, f.now(f.last))
                v.tensor_tensor(merged[:, 4:8, :], merged[:, 4:8, :], gc[:, :, :], ALU.mult).then_inc(f.count(vector_step), 1)
                dve.wait_ge(f.last, f.now(f.last))
                v.tensor_tensor(hc[:, :, :], merged[:, 4:8, :], merged[:, 4:8, :], ALU.mult).then_inc(f.count(normed_sq), 1)
                v.reciprocal(osq[:, 2:4, :], osq[:, 2:4, :]).then_inc(f.count(vector_step), 1)
                dve.wait_ge(f.last, f.now(f.last))
                v.scalar_tensor_tensor(merged[:, 0:4, :], merged[:, 0:4, :], p2[:, B_GN:B_GN + 1], osq, ALU.mult, ALU.mult).then_inc(f.count(vector_step), 1)
                dve.wait_ge(f.last, f.now(f.last))
                v.tensor_tensor(merged[:, 0:4, :], merged[:, 0:4, :], gb[:, :, :], ALU.mult).then_inc(f.count(vector_step), 1)
                dve.wait_ge(normed_std, f.next(normed_std))
                v.reciprocal(std[:, :], std[:, :]).then_inc(f.count(vector_step), 1)
                dve.wait_ge(f.last, f.now(f.last))
                for j in range(4):
                    ins = v.scalar_tensor_tensor(merged[:, 4 + j, :], merged[:, 4 + j, :], p2[:, B_SN + j:B_SN + j + 1], std[:, :],
                                                 ALU.mult, ALU.mult)
                ins.then_inc(f.count(merged_ready), 1)
                for n in range(4):
                    dve.wait_ge(bank_full[n], f.next(bank_full[n]))
                    add_gated(l, 0, n, n, bank_free[n])
                rms_gain(l, 1, x_ready)
                if l == 0:
                    split_low(0, 0)
                rms_finish(l, 1, l == 0)
                if l == 0:
                    dense(lambda p, i: f.bump(gate_full[p]), FF2 // CW, FFN2_TRIP)
                else:
                    take(0, tiles(logit, 2), tiles(bank[0][:, 0:16], 2))
                    dve.wait_ge(f.last, f.now(f.last))
                    for t in range(2):
                        v.max(best[:, 8 * t:8 * t + 8], logit[:, 8 * t:8 * t + 8]).then_inc(f.count(vector_step), 1)
                    dve.wait_ge(f.last, f.now(f.last))
                    for t in range(2):
                        v.max_index(place[:, 8 * t:8 * t + 8], best[:, 8 * t:8 * t + 8], logit[:, 8 * t:8 * t + 8]).then_inc(f.count(vector_step), 1)
                    b2 = tiles(best, 2)
                    v.tensor_tensor(pair[:, 0:2], b2[:, :, 1], b2[:, :, 0], ALU.subtract).then_inc(f.count(route_in), 1)
                    dve.wait_ge(f.last, f.now(f.last))
                    v.tensor_copy(placef, place[:, :]).then_inc(f.count(vector_step), 1)
                    v.memset(picks[:, EXPERTS:EXPERTS + 1, :], 0.0).then_inc(f.count(vector_step), 1)
                    dve.wait_ge(f.last, f.now(f.last))
                    v.tensor_scalar(placef, placef, 1.0, None, ALU.add).then_inc(f.count(vector_step), 1)
                    dve.wait_ge(f.last, f.now(f.last))
                    number = slots[:, 0:EXPERTS]
                    for t in range(2):
                        v.tensor_scalar(chosen[:, t, :], number, placef[:, 8 * t:8 * t + 1], None, ALU.is_equal).then_inc(f.count(vector_step), 1)
                    dve.wait_ge(f.last, f.now(f.last))
                    for t in range(2):
                        v.scalar_tensor_tensor(chosen[:, t, :], number, placef[:, 8 * t + 1:8 * t + 2], chosen[:, t, :],
                                               ALU.is_equal, ALU.add).then_inc(f.count(chosen_ready if t else vector_step), 1)
                    dve.wait_ge(pair_exp, f.next(pair_exp))
                    v.tensor_scalar(pair[:, 2:4], pair[:, 0:2], 1.0, None, ALU.add).then_inc(f.count(vector_step), 1)
                    dve.wait_ge(f.last, f.now(f.last))
                    v.reciprocal(pair[:, 2:4], pair[:, 2:4]).then_inc(f.count(vector_step), 1)
                    dve.wait_ge(f.last, f.now(f.last))
                    v.tensor_tensor(pair[:, 4:6], pair[:, 0:2], pair[:, 2:4], ALU.mult).then_inc(f.count(vector_step), 1)
                    dve.wait_ge(f.last, f.now(f.last))
                    for t in range(2):
                        v.tensor_scalar(route[:, t, :], number, placef[:, 8 * t:8 * t + 1], pair[:, 2 + t:3 + t], ALU.is_equal, ALU.mult).then_inc(f.count(vector_step), 1)
                        v.tensor_scalar(second[:, t, :], number, placef[:, 8 * t + 1:8 * t + 2], pair[:, 4 + t:5 + t], ALU.is_equal, ALU.mult).then_inc(f.count(vector_step), 1)
                    dve.wait_ge(f.last, f.now(f.last))
                    v.tensor_tensor(picks[:, 0:EXPERTS, 2:4].rearrange("p e t -> p t e"), route[:, :, :], second[:, :, :], ALU.add).then_inc(f.count(vector_step), 1)
                    dve.wait_ge(bank_full[0], f.next(bank_full[0]))
                    v.tensor_tensor(picks[:, 0:EXPERTS, 0:2].rearrange("p e t -> p t e"), tiles(bank[0][:, 0:16], 2), chosen[:, :, :],
                                    ALU.mult).then_inc(f.count(vector_step), 1)
                    v.tensor_reduce(crowd[:, 0:1], bank[0][:, 16:24], AX.X, ALU.max).then_inc(f.count(bank_free[0]), 1)
                    dve.wait_ge(f.last, f.now(f.last))
                    v.tensor_scalar(crowded[:, :], crowd[:, 0:1], float(P), None, ALU.is_gt).then_inc(f.count(crowd_ready), 1)

                    def split(s, h, last=None):
                        dve.wait_ge(hi_ready[h], f.next(hi_ready[h]))
                        v.tensor_tensor(ew_lo[:, h, :], ring(s), ew_hi[:, h, :].bitcast(F32), ALU.subtract).then_inc(w_used[s], 1)

                    def form(p):
                        f.bump(gate_full[p])
                        dve.wait_ge(up_full[p], f.next(up_full[p]))
                        dve.wait_ge(silu_ready[p], f.next(silu_ready[p]))
                        v.tensor_tensor(act[:, p, :, 0:P], silu[:, p, :, 0:P], tiles(bank[2 * p + 1][:, 0:CW], 2), ALU.mult).then_inc(f.count(turn_ready[p]), 1)

                    def finish(p):
                        dve.wait_ge(act_hi_ready[p], f.next(act_hi_ready[p]))
                        v.tensor_tensor(eact_lo[:, p, :, :], tiles(bank[6][:, 0:CW], 2), eact_hi[:, p, :, :].bitcast(F32),
                                        ALU.subtract).then_inc(f.count(act_ready[p]), 1)

                    def gathered(q):
                        dve.wait_ge(gather_hi, f.next(gather_hi))
                        ks = slice(4 * q, 4 * q + 4)
                        v.tensor_tensor(xe_lo[:, ks, :], tiles(bank[7][:, :], 4), xe_hi[:, ks, :].bitcast(F32),
                                        ALU.subtract).then_inc(f.count(gather_free), 1)

                    def experts():
                        for t in range(2):
                            v.tensor_scalar(select[:, t, :], slots, picks[:, 0, t:t + 1], None, ALU.is_equal).then_inc(f.count(select_ready if t else vector_step), 1)
                        gathered(0)
                        gathered(1)
                        with f.trips(EXPERTS, EXPERT) as e:
                            def selections():
                                dve.wait_ge(f.last, f.now(f.last))
                                v.tensor_copy(pick[:, :, :], picks[:, bass.ds(e, 2), :]).then_inc(f.count(vector_step), 1)
                                dve.wait_ge(f.last, f.now(f.last))
                                for t in range(2):
                                    v.tensor_scalar(weigh[:, t, :], slots, pick[:, 0, t:t + 1], pick[:, 0, 2 + t:3 + t], ALU.is_equal, ALU.mult).then_inc(f.count(vector_step), 1)
                                for t in range(2):
                                    v.tensor_scalar(select[:, t, :], slots, pick[:, 1, t:t + 1], None, ALU.is_equal).then_inc(f.count(select_ready if t else vector_step), 1)

                            expert_steps(split, form, finish, dve, f, selections)
                            split(5, 2)
                            form(1)
                            gathered(0)
                            finish(1)
                            gathered(1)
                            for n in range(4):
                                dve.wait_ge(result_full, f.next(result_full))
                                add_gated(l, 1, n, n, result_free)
                        dve.wait_ge(f.last, f.now(f.last))

                    experts()
                    with dve.If(dve.value_load(crowded[0:1, 0:1], min_val=0, max_val=1) > 0):
                        v.tensor_scalar(picks[:, :, 0:2], picks[:, :, 0:2], -float(P), None, ALU.add).then_inc(f.count(vector_step), 1)
                        dve.wait_ge(f.last, f.now(f.last))
                        experts()
                    v.tensor_copy(gain[:, :], eln[:, 0:8]).then_inc(x_ready, 1)
                if l == 0:
                    dve.wait_ge(ffn_summed, f.next(ffn_summed))
                    for n in range(4):
                        add_gated(l, 1, n, 4 + n, x_ready if n == 3 else None)
            dve.wait_ge(std_ready, f.next(std_ready))
            v.reciprocal(std[:, :], std[:, :]).then_inc(final_step, 1)
            dve.wait_ge(final_step, 1)
            v.tensor_tensor(yT, xT[:, :, :], spread(std[:, :], KD), ALU.mult).then_inc(final_step, 1)
            dve.wait_ge(final_step, 2)
            for k in range(KD):
                ins = v.tensor_scalar(yT[:, k, :], yT[:, k, :], gain[:, k:k + 1], None, ALU.mult)
            ins.then_inc(f.count(y_ready), 1)

        @block.scalar
        def _(eng):
            f = Follow(eng, scalar_step, free)
            a = nc.scalar

            def take(b, dst, src=None):
                eng.wait_ge(bank_full[b], f.next(bank_full[b]))
                a.copy(dst, tiles(bank[b][:, :], 2) if src is None else src).then_inc(f.count(bank_free[b]), 1)

            def split_high(s, h):
                eng.wait_ge(ffn_loaded[s], f.next(ffn_loaded[s], 16))
                a.copy(w_hi[:, h, :], ring(s)).then_inc(f.count(hi_ready[h]), 1)

            def norm(eps, src, before, dense=False):
                a.preload_act_table(ACT.Sqrt)
                for q in range(4):
                    if q == 0 or before is centred:
                        eng.wait_ge(before, f.next(before))
                    a.activation(squares[:, 2 * q:2 * q + 2, :], src[:, 2 * q:2 * q + 2, :], ACT.Square).then_inc(f.count(squares_ready), 1)
                if dense:
                    split_high(0, 0)
                eng.wait_ge(var_ready, f.next(var_ready))
                a.activation(std[:, :], bank[4][:, 0:TOK], ACT.Sqrt, bias=eps).then_inc(f.count(std_ready), 1)
                a.preload_act_table(ACT.Silu if dense or eps is eps2 else ACT.Exp)

            def dense(x, pieces, ready, at, silu_of, n, per):
                for q in range(4):
                    ks = slice(2 * q, 2 * q + 2)
                    if q < 3:
                        eng.wait_ge(pieces, f.next(pieces))
                    else:
                        eng.wait_ge(ready, at)
                    a.copy(x_hi[:, ks, :], x[:, ks, :]).then_inc(f.count(x_hi_ready), 1)
                split_high(1, 1)
                f.bump(gate_full[0])

                done = {0: gate_full[0], 1: up_full[0], 2: down_done, 3: gate_full[1], 4: up_full[1]}

                def split(s, h, last):
                    if last == 5:
                        eng.wait_ge(down_done, f.now(down_done))
                    else:
                        eng.wait_ge(done[last], f.next(done[last]))
                    if s == 5:
                        f.bump(down_done)
                    split_high(s, h)

                def finish(p):
                    silu_of(p)
                    eng.wait_ge(product_ready[p], f.next(product_ready[p]))
                    a.copy(act_hi[:, p, :, :], act[:, p, :, :]).then_inc(f.count(act_hi_ready[p]), 1)

                dense_steps(split, lambda p, i: None, finish, n, eng, per, f)
                f.bump(down_done)

            def exps(u):
                b = u % 2
                eng.wait_ge(peak_ready, f.next(peak_ready))
                for m in range(2):
                    ins = a.activation(probs[:, b, m * TOK:(m + 1) * TOK], scores[:, b, m * TOK:(m + 1) * TOK], ACT.Exp,
                                       bias=peak[:, b, m:m + 1], scale=-1.0, accum_out=total[:, b, m:m + 1])
                ins.then_inc(f.count(exp_ready), 1)

            def probs_out(u, n, whole):
                b, qt = 4 + u % 2, u % 2
                dst = probsT[:, n % 2, :, :, qt * P:(qt + 1) * P]
                if whole:
                    take(b, dst.rearrange("p m t q -> p (m t) q"), tiles(bank[b][:, :], 4))
                else:
                    take(b, dst[:, 0, :, :], tiles(bank[b][:, 0:2 * P], 2))

            def modulate(c):
                s = ada_slot(c)
                w = tiles(ring(s), KD)
                eng.wait_ge(ada_loaded[s], f.next(ada_loaded[s], 16))
                for k in range(KD):
                    ins = a.activation(w[:, k, :], w[:, k, :], ACT.Copy, scale=cond[:, k:k + 1])
                ins.then_inc(f.count(mod_scaled), 1)

            eng.wait_ge(inputs_in, f.next(inputs_in, 48))
            a.activation(cond[:, :], eln[:, 16:24], ACT.Silu).then_inc(f.count(cond_ready), 1)
            norm(eps1, yT, centred)
            f.bump(x_ready)
            f.bump(x_pieces, 3)
            with f.trips(DEPTH, LAYER1):
                eng.wait_ge(lam_dot, f.next(lam_dot))
                a.activation(lam[:, 2:4], lam[:, 0:2], ACT.Exp).then_inc(f.count(lam_exp), 1)
                modulate(0)
                modulate(1)
                for u in range(18):
                    if u < 16:
                        exps(u)
                    if u < 11:
                        modulate(2 * u + 2)
                    if u < 12:
                        take(6 + u % 2, gates[:, 2 * u:2 * u + 2, :])
                    if u < 11:
                        modulate(2 * u + 3)
                    if 1 <= u <= 16:
                        probs_out(u - 1, (u - 1) // 2, u - 1 >= 8)
                    if u == 10:
                        for j in range(2):
                            take(4 + j, ka[:, 2 * j:2 * j + 2, :])
                        eng.wait_ge(f.last, f.now(f.last))
                        a.activation(ka[:, :, :], ka[:, :, :], ACT.Sqrt, bias=eps1, scale=float(D // P)).then_inc(f.count(sub_std), 1)
                eng.wait_ge(f.last, f.now(f.last))
                a.activation(flat, flat, ACT.Sigmoid).then_inc(f.count(gates_ready), 1)
                norm(eps1, yT, centred)
                for u in range(6):
                    if u < 4:
                        exps(u)
                    if 1 <= u <= 4:
                        probs_out(u - 1, (u - 1) // 2, True)
                norm(eps1, yT, centred, True)

                def silu_conv(p):
                    eng.wait_ge(conv_ready[p], f.next(conv_ready[p]))
                    a.activation(silu[:, p, :, :], conva[:, p, :, :], ACT.Silu).then_inc(f.count(silu_ready[p]), 1)

                f.bump(x_pieces, 3)
                dense(xT, x_pieces, x_ready, f.now(x_ready) + 2, silu_conv, FF1 // CW, FFN1_TRIP)
                norm(eps1, yT, centred)
                f.bump(x_ready, 3)
                f.bump(x_pieces, 3)

            def silu_gate(p):
                a.activation(silu[:, p, :, :], tiles(bank[2 * p][:, :], 2), ACT.Silu).then_inc(f.count(silu_ready[p]), 1)

            eng.wait_ge(x_ready, f.now(x_ready))
            for l in range(DEPTH):
                if l == 0:
                    f.bump(x_ready, -1)
                norm(eps2, xT, x_ready)
                eng.wait_ge(conv_in, f.next(conv_in))
                a.activation(qb[:, :, :], qb[:, :, :], ACT.Silu).then_inc(f.count(scalar_step), 1)
                a.activation(ka[:, 0:2, :], ka[:, 0:2, :], ACT.Silu).then_inc(f.count(conv_silu), 1)
                a.activation(aexp, par2[l][:, B_ALOG:B_ALOG + 8], ACT.Exp).then_inc(f.count(scalar_step), 1)
                a.activation(dtabs, dtabs, ACT.Exp, scale=-1.0).then_inc(f.count(scalar_step), 1)
                eng.wait_ge(decay_in, f.next(decay_in))
                a.activation(scores[:, 0, :], scores[:, 0, :], ACT.Exp, scale=-1.0).then_inc(f.count(scalar_step), 1)
                eng.wait_ge(f.last, f.now(f.last))
                a.activation(dtabs, dtabs, ACT.Ln, bias=one).then_inc(f.count(dt_ln), 1)
                a.activation(scores[:, 0, :], scores[:, 0, :], ACT.Ln, bias=one).then_inc(f.count(decay_ln), 1)
                eng.wait_ge(cum_ready, f.next(cum_ready))
                a.activation(probs[:, 1, :], probs[:, 0, :], ACT.Exp).then_inc(f.count(scalar_step), 1)
                a.activation(scores[:, 0, :], probs[:, 0, :], ACT.Exp, scale=-1.0).then_inc(f.count(scalar_step), 1)
                a.activation(scores[:, 1, :], scores[:, 1, :], ACT.Exp).then_inc(f.count(cum_exp), 1)
                a.preload_act_table(ACT.Silu)
                eng.wait_ge(proj_ready, f.next(proj_ready))
                a.activation(gb[:, :, :], gb[:, :, :], ACT.Silu).then_inc(f.count(scalar_step), 1)
                a.activation(gc[:, :, :], gc[:, :, :], ACT.Silu).then_inc(f.count(scalar_step), 1)
                a.preload_act_table(ACT.Sqrt)
                for j in range(2):
                    take(4 + j, osq[:, 2 * j:2 * j + 2, :])
                eng.wait_ge(f.last, f.now(f.last))
                a.activation(osq, osq, ACT.Sqrt, bias=eps2, scale=float(D // P)).then_inc(f.count(normed_std), 1)
                eng.wait_ge(seg_ready, f.next(seg_ready))
                a.activation(flat[:, CH:2 * CH], flat[:, CH:2 * CH], ACT.Exp).then_inc(f.count(scalar_step), 1)
                a.activation(ecum, cumr[:, 1024:2048], ACT.Exp).then_inc(f.count(scalar_step), 1)
                a.activation(wtail, wtail, ACT.Exp).then_inc(f.count(seg_exp), 1)
                a.preload_act_table(ACT.Sqrt)
                take(4, std[:, :], bank[4][:, 0:TOK])
                eng.wait_ge(f.last, f.now(f.last))
                a.activation(std[:, :], std[:, :], ACT.Sqrt, bias=eps2, scale=2.0).then_inc(f.count(normed_std), 1)
                norm(eps2, xT, x_ready, l == 0)
                if l == 0:
                    f.bump(y_pieces, 3)
                    dense(yT, y_pieces, y_ready, DEPTH + 2, silu_gate, FF2 // CW, FFN2_TRIP)
                else:
                    eng.wait_ge(route_in, f.next(route_in))
                    a.activation(pair[:, 0:2], pair[:, 0:2], ACT.Exp).then_inc(f.count(pair_exp), 1)
                    for q in range(4):
                        take(4 + q, htok[:, q // 2, 512 * (q % 2):512 * (q % 2) + 512], bank[4 + q][:, :])

                    done = {0: gate_full[0], 1: up_full[0], 2: down_done, 3: gate_full[1], 4: up_full[1]}

                    def split(s, h, last=None):
                        if last == 5:
                            eng.wait_ge(down_done, f.now(down_done))
                        elif last is not None:
                            eng.wait_ge(done[last], f.next(done[last]))
                        if s == 5:
                            f.bump(down_done)
                        eng.wait_ge(ffn_loaded[s], f.next(ffn_loaded[s], 16))
                        a.copy(ew_hi[:, h, :], ring(s)).then_inc(f.count(hi_ready[h]), 1)

                    def form(p):
                        a.activation(silu[:, p, :, 0:P], tiles(bank[2 * p][:, 0:CW], 2), ACT.Silu).then_inc(f.count(silu_ready[p]), 1)

                    def finish(p):
                        eng.wait_ge(turned[p], f.next(turned[p]))
                        a.copy(eact_hi[:, p, :, :], tiles(bank[6][:, 0:CW], 2)).then_inc(f.count(act_hi_ready[p]), 1)

                    def gathered(q):
                        eng.wait_ge(gather_full, f.next(gather_full))
                        a.copy(xe_hi[:, 4 * q:4 * q + 4, :], tiles(bank[7][:, :], 4)).then_inc(f.count(gather_hi), 1)

                    def experts():
                        a.preload_act_table(ACT.Silu)
                        gathered(0)
                        gathered(1)
                        with f.trips(EXPERTS, EXPERT):
                            expert_steps(split, form, finish, eng, f)
                            split(5, 2, 3)
                            form(1)
                            gathered(0)
                            finish(1)
                            gathered(1)
                            f.bump(up_full[1])
                            f.bump(down_done)
                            eng.wait_ge(back_full, f.next(back_full))
                            a.copy(back, bank[0][:, 0:TOK]).then_inc(f.count(back_free), 1)
                            for n in range(2):
                                take(4 + n, ye[:, n * 512:(n + 1) * 512], bank[4 + n][:, :])

                    experts()
                    eng.wait_ge(crowd_ready, f.next(crowd_ready))
                    with eng.If(eng.value_load(crowded[0:1, 0:1], min_val=0, max_val=1) > 0):
                        experts()
            norm(eps2, xT, x_ready)
    if BAD:
        raise AssertionError("counts per trip differ from the tables")


def constants():
    c = np.zeros((P, C_ALL), np.float32)
    c[:, C_ID:C_ID + P] = np.eye(P)
    for m in range(P):
        if m % 64 < 32:
            c[m + 32, C_ROT + m] = -1.0
        else:
            c[m - 32, C_ROT + m] = 1.0
    inv = np.float32(10000.0) ** (-np.arange(32, dtype=np.float32) * np.float32(2.0) / np.float32(64))
    angle = np.arange(TOK, dtype=np.float32)[None, :] * inv.astype(np.float32)[:, None]
    c[:, C_COS:C_COS + TOK] = np.tile(np.cos(angle), (4, 1))
    c[:, C_SIN:C_SIN + TOK] = np.tile(np.sin(angle), (4, 1))
    j, i = np.arange(P)[:, None], np.arange(P)[None, :]
    c[:, C_TRI:C_TRI + P] = j <= i
    c[:, C_BAN:C_BAN + P] = np.where(j <= i, 0.0, NEG)
    c[:, C_DIAG:C_DIAG + P] = (j <= i) & (j // 64 == i // 64)
    q, k = np.arange(64)[:, None], np.arange(64)[None, :]
    start = np.clip(q - 8, 0, 48)
    c[:, C_WIN:C_WIN + 64] = np.tile(np.where((k >= start) & (k < start + 16), 0.0, NEG), (2, 1))
    for m in range(2):
        c[64 * m:64 * m + 64, C_HALF + m] = 1.0
    c[:, C_EPS1], c[:, C_EPS2], c[:, C_ONE] = 1e-5, 1e-6, 1.0
    c[:, C_IOTA:C_IOTA + P] = np.arange(1, P + 1)
    return c


def columns(vector):
    v = np.asarray(vector)
    return np.moveaxis(v.reshape(-1, P), 0, 1)


def rows(vector):
    return np.broadcast_to(np.asarray(vector).reshape(1, -1), (P, np.asarray(vector).size))


BIG = ["w_in", "w_branch", "w_mix_out", "xa_q", "xa_kv", "xa_o", "ffn_w_in", "ffn_w_out", "ada_w_2", "w_in_2", "gla_a_w_2",
       "w_out_2", "ffn_w_gate_2", "ffn_w_up_2", "ffn_w_down_2", "router_w_2", "moe_w_gate_2", "moe_w_up_2", "moe_w_down_2"]


def layout(i):
    arrays = {n: np.ascontiguousarray(i[n]) for n in BIG}
    arrays["xT"] = np.ascontiguousarray(np.asarray(i["x"])[0].T)
    arrays["memT"] = np.ascontiguousarray(np.asarray(i["mem"])[0].T)
    arrays["const"] = constants()
    arrays["eln"] = np.concatenate([columns(i["emb_ln_g"]), columns(i["emb_ln_b"]), columns(i["c_2"])], axis=1)
    arrays["fin"] = np.ascontiguousarray(columns(i["final_norm_w_2"]))
    par1 = np.zeros((DEPTH, P, A_ALL), np.float32)
    par2 = np.zeros((DEPTH, P, B_ALL), np.float32)
    for l in range(DEPTH):
        init = 0.8 - 0.6 * math.exp(-0.3 * l)
        taps = np.concatenate([np.asarray(i["ffn_conv_w"])[l], np.asarray(i["ffn_conv_b"])[l][None]], axis=0)
        par1[l, :, A_LNG:A_LNG + 24] = columns(np.asarray(i["ln_g"])[l])
        par1[l, :, A_LNB:A_LNB + 24] = columns(np.asarray(i["ln_b"])[l])
        par1[l, :, A_SUB:A_SUB + 1] = columns(np.asarray(i["subln_g"])[l])
        par1[l, :, A_SCW:A_SCW + 12] = columns(np.asarray(i["sc_conv_w"])[l])
        par1[l, :, A_FF:A_FF + 88] = np.moveaxis(taps.reshape(4, FF1 // P, P), (0, 1, 2), (2, 1, 0)).reshape(P, 88)
        par1[l, :, A_LAM0] = init
        par1[l, :, A_LAM1] = 1.0 - init
        for k, n in enumerate(("lam_q1", "lam_k1", "lam_q2", "lam_k2")):
            par1[l, :, A_LAMV + 64 * k:A_LAMV + 64 * k + 64] = rows(np.asarray(i[n])[l])
        for at, value in ((B_N1, columns(np.asarray(i["norm1_w_2"])[l])), (B_N2, columns(np.asarray(i["norm2_w_2"])[l])),
                          (B_ADA, columns(np.asarray(i["ada_b_2"])[l])), (B_AB, columns(np.asarray(i["gla_a_b_2"])[l])),
                          (B_GN, columns(np.asarray(i["gla_norm_w_2"])[l])), (B_CW, columns(np.asarray(i["conv_w_2"])[l])),
                          (B_CB, columns(np.asarray(i["conv_b_2"])[l])), (B_DTB, rows(np.asarray(i["dt_bias_2"])[l])),
                          (B_ALOG, rows(np.asarray(i["a_log_2"])[l])),
                          (B_DS, columns(np.repeat(np.asarray(i["d_skip_2"])[l], 64))),
                          (B_SN, columns(np.asarray(i["ssd_norm_w_2"])[l]))):
            par2[l, :, at:at + value.shape[1]] = value
    arrays["par1"], arrays["par2"] = par1, par2
    rpb = np.zeros((DEPTH, 8, 7, 127), np.float32)
    rpb[..., 48:79] = np.asarray(i["rpb"])[:, :, 4:11, :]
    arrays["rpb"] = rpb
    return {n: np.ascontiguousarray(a) for n, a in arrays.items()}


def kernel(**inputs):
    import concourse.bacc as bacc
    from concourse.bass_utils import run_bass_kernel_spmd as run

    nc = bacc.Bacc("TRN2", target_bir_lowering=False, num_devices=1)
    arrays = layout(inputs)
    io = {n: nc.dram_tensor(f"in_{n}", a.shape, F32, kind="ExternalInput").ap() for n, a in arrays.items()}
    io["out"] = nc.dram_tensor("outT", (D, TOK), F32, kind="ExternalOutput").ap()
    io["windows"] = nc.dram_tensor("windows", (DEPTH, 64, 8, 7, 127), F32, kind="Internal").ap()
    program(nc, io)
    r = run(nc, [{f"in_{n}": a for n, a in arrays.items()}], core_ids=[0])
    return np.ascontiguousarray(r.results[0]["outT"].T)[None]
```
